# Optimizing a Trainium2 kernel written in Bass

```python
import math
import jax
import jax.numpy as jnp
from jax import lax
import numpy as np

D_MODEL = 1024
BATCH = 1
SEQ = 512
DEPTH = 1
DEC_BATCH = 8
DEC_SEQ = 4
PAST_LEN = 256
PAGE_SIZE = 128

HEAD_DIM = 64
H_A = 4
DSA_PAIRS = ((128, 1), (512, 4), (2048, 16))
H_B_GROUP = 2
H_B = H_B_GROUP * len(DSA_PAIRS)
H_C = 6
W_A = H_A * HEAD_DIM
W_B = H_B * HEAD_DIM
W_C = H_C * HEAD_DIM
N_BRANCH = 3
MLSTM_CHUNK = 64
FORGET_BIAS = 3.0
MOBA_BLOCK = 256
MOBA_TOPK = 3
MOBA_QCHUNK = 64
REL_BUCKETS = 32
REL_MAX_DIST = 2048
D_FF = ((8 * D_MODEL + 3 * 256 - 1) // (3 * 256)) * 256
SPLIT_SIZES = (W_A, W_A, W_A, W_A, H_A, H_A, W_B, W_B, W_B, W_C, W_C, W_C, N_BRANCH * D_MODEL)
N_IN = sum(SPLIT_SIZES)
SPLIT_IDX = [int(i) for i in np.cumsum(SPLIT_SIZES)[:-1]]
EPS = 1e-6

kernel_name = 'hybrid_mlstm_dilated_moba_decoder_step'

def rmsnorm(x, g):
    xf = x.astype(jnp.float32)
    y = xf * lax.rsqrt(jnp.mean(xf * xf, axis=-1, keepdims=True) + EPS)
    return (y * g.astype(jnp.float32)).astype(x.dtype)

def softmax_lse(s):
    mx = jnp.max(s, axis=-1, keepdims=True)
    p = jnp.exp(s - mx)
    den = jnp.sum(p, axis=-1, keepdims=True)
    return p / den, (mx + jnp.log(den))[..., 0]

def rel_bucket(dist):
    dist = jnp.maximum(dist, 0)
    max_exact = REL_BUCKETS // 2
    ratio = jnp.log(jnp.maximum(dist, 1).astype(jnp.float32) / max_exact) / math.log(REL_MAX_DIST / max_exact)
    large = jnp.minimum(max_exact + (ratio * (REL_BUCKETS - max_exact)).astype(jnp.int32), REL_BUCKETS - 1)
    return jnp.where(dist < max_exact, dist, large)

def project(x, g_mix, w_in, b_if):
    B, T, _ = x.shape
    h = rmsnorm(x, g_mix)
    z = jnp.einsum('btd,dn->btn', h, w_in)
    qa, ka, va, oa, ia, fa, qb, kb, vb, qc, kc, vc, gates = jnp.split(z, SPLIT_IDX, axis=-1)
    hd = lambda a: a.reshape(B, T, -1, HEAD_DIM)
    mix_a = (hd(qa), hd(ka) * HEAD_DIM ** -0.5, hd(va), ia + b_if[:H_A], fa + b_if[H_A:])
    return mix_a, oa, (hd(qb), hd(kb), hd(vb)), (hd(qc), hd(kc), hd(vc)), gates

def mlstm(q, k, v, i_pre, f_pre, C0, n0, m0):
    B, T, H, Dh = q.shape
    L = math.gcd(MLSTM_CHUNK, T)
    nc = T // L

    def chunks(a):
        a = a.astype(jnp.float32).reshape((B, nc, L, H) + a.shape[3:])
        return jnp.transpose(a, (1, 0, 3, 2) + tuple(range(4, a.ndim)))

    causal = jnp.tril(jnp.ones((L, L), dtype=bool))

    def step(carry, xs):
        C, n, m = carry
        qc, kc, vc, ic, fc = xs
        b = jnp.cumsum(jax.nn.log_sigmoid(fc), axis=-1)
        dmat = jnp.where(causal, b[..., :, None] - b[..., None, :] + ic[..., None, :], -jnp.inf)
        inter = b + m[..., None]
        m_t = jnp.maximum(inter, jnp.max(dmat, axis=-1))
        w = jnp.exp(dmat - m_t[..., None])
        iw = jnp.exp(inter - m_t)
        s = jnp.einsum('bhtk,bhsk->bhts', qc, kc) * w
        num = iw[..., None] * jnp.einsum('bhtk,bhkv->bhtv', qc, C) + jnp.einsum('bhts,bhsv->bhtv', s, vc)
        den = iw * jnp.einsum('bhtk,bhk->bht', qc, n) + jnp.sum(s, axis=-1)
        h = num / jnp.maximum(jnp.abs(den), jnp.exp(-m_t))[..., None]
        m_new = m_t[..., -1]
        decay = jnp.exp(b[..., -1] + m - m_new)
        ws = jnp.exp(b[..., -1:] - b + ic - m_new[..., None])
        C_new = decay[..., None, None] * C + jnp.einsum('bhs,bhsk,bhsv->bhkv', ws, kc, vc)
        n_new = decay[..., None] * n + jnp.einsum('bhs,bhsk->bhk', ws, kc)
        return (C_new, n_new, m_new), h

    init = (C0.astype(jnp.float32), n0.astype(jnp.float32), m0.astype(jnp.float32))
    (C, n, m), h = lax.scan(step, init, (chunks(q), chunks(k), chunks(v), chunks(i_pre), chunks(f_pre)))
    h = jnp.transpose(h, (1, 0, 3, 2, 4)).reshape(B, T, H, Dh)
    return h, C, n, m

def dsa_group_prompt(q, k, v, bias_tab, win, dil):
    B, T, H, Dh = q.shape
    ns = win // dil
    span = ns * dil
    Tpad = -(-T // span) * span
    nb = Tpad // span

    def blocks(a):
        a = jnp.pad(a.astype(jnp.float32), ((0, 0), (0, Tpad - T), (0, 0), (0, 0)))
        return a.reshape(B, nb, ns, dil, H, Dh)

    def with_prev(a):
        prev = jnp.pad(a, ((0, 0), (1, 0)) + ((0, 0),) * 4)[:, :-1]
        return jnp.concatenate([prev, a], axis=2)

    qb = blocks(q)
    kk, vv = with_prev(blocks(k)), with_prev(blocks(v))
    s = jnp.einsum('bnqrhd,bnkrhd->bnrhqk', qb, kk) * Dh ** -0.5
    qi = jnp.arange(ns)[:, None]
    ki = jnp.arange(2 * ns)[None, :]
    steps = qi + ns - ki
    bias = jnp.transpose(bias_tab[rel_bucket(jnp.clip(steps, 0, ns) * dil)], (2, 0, 1))
    valid = (steps >= 0) & (steps <= ns) & ((jnp.arange(nb)[:, None, None] > 0) | (ki >= ns))
    s = jnp.where(valid[None, :, None, None], s + bias, -jnp.inf)
    p, lse = softmax_lse(s)
    o = jnp.einsum('bnrhqk,bnkrhd->bnqrhd', p, vv).reshape(B, Tpad, H, Dh)[:, :T]
    lse = jnp.transpose(lse, (0, 1, 4, 2, 3)).reshape(B, Tpad, H)[:, :T]
    return o, lse

def dsa_group_sample(q, k, v, buf, bias_tab, win, dil):
    B, T, H, Dh = q.shape
    Lw = buf.shape[1]
    ns = win // dil
    kv = jnp.concatenate([buf, jnp.stack([k, v], axis=2).astype(buf.dtype)], axis=1)
    steps = jnp.arange(ns + 1)
    idx = Lw + jnp.arange(T)[:, None] - dil * steps[None, :]
    g = kv[:, jnp.maximum(idx, 0)].astype(jnp.float32)
    s = jnp.einsum('bthd,btjhd->bthj', q.astype(jnp.float32), g[:, :, :, 0]) * Dh ** -0.5
    bias = bias_tab[rel_bucket(steps * dil)].T
    s = jnp.where((idx >= 0)[None, :, None, :], s + bias, -jnp.inf)
    p, lse = softmax_lse(s)
    o = jnp.einsum('bthj,btjhd->bthd', p, g[:, :, :, 1])
    return o, lse, kv[:, -Lw:]

def dsa_combine(outs, lses):
    alpha = jax.nn.softmax(jnp.stack(lses, axis=0), axis=0)
    return jnp.concatenate([o * alpha[g][..., None] for g, o in enumerate(outs)], axis=2)

def moba_blocks(k, v):
    B, T, H, Dh = k.shape
    nb = -(-T // MOBA_BLOCK)
    pad = ((0, 0), (0, nb * MOBA_BLOCK - T), (0, 0), (0, 0))
    kb = jnp.pad(k.astype(jnp.float32), pad).reshape(B, nb, MOBA_BLOCK, H, Dh)
    vb = jnp.pad(v.astype(jnp.float32), pad).reshape(B, nb, MOBA_BLOCK, H, Dh)
    kmean = jnp.mean(kb, axis=2)
    return kb, vb, kmean

def moba_queries(q, pos, kb, vb, kmean, bias_tab, ksel):
    B, Q, H, Dh = q.shape
    nb = kb.shape[1]
    scale = Dh ** -0.5
    bq = pos // MOBA_BLOCK
    gate = jnp.einsum('bqhd,bnhd->bqhn', q, kmean)
    fully_past = jnp.arange(nb)[None, :] < bq[:, None]
    gate = jnp.where(fully_past[None, :, None, :], gate, -jnp.inf)
    gval, idx = lax.top_k(gate, ksel)
    sel_ok = gval > -jnp.inf
    bi = jnp.arange(B)[:, None, None, None]
    hi = jnp.arange(H)[None, None, :, None]
    ks = kb[bi, idx, :, hi]
    vs = vb[bi, idx, :, hi]
    ko = kb[:, bq]
    vo = vb[:, bq]
    offs = jnp.arange(MOBA_BLOCK)
    d_sel = pos[None, :, None, None, None] - (idx[..., None] * MOBA_BLOCK + offs)
    s_sel = jnp.einsum('bqhd,bqhskd->bqhsk', q, ks) * scale + bias_tab[rel_bucket(d_sel), hi[..., None]]
    s_sel = jnp.where(sel_ok[..., None], s_sel, -jnp.inf).reshape(B, Q, H, ksel * MOBA_BLOCK)
    d_own = pos[:, None] - (bq[:, None] * MOBA_BLOCK + offs[None, :])
    s_own = jnp.einsum('bqhd,bqkhd->bqhk', q, ko) * scale + jnp.transpose(bias_tab[rel_bucket(d_own)], (0, 2, 1))
    s_own = jnp.where((d_own >= 0)[:, None, :], s_own, -jnp.inf)
    p, _ = softmax_lse(jnp.concatenate([s_sel, s_own], axis=-1))
    n_sel = ksel * MOBA_BLOCK
    return (jnp.einsum('bqhsk,bqhskd->bqhd', p[..., :n_sel].reshape(B, Q, H, ksel, MOBA_BLOCK), vs)
            + jnp.einsum('bqhk,bqkhd->bqhd', p[..., n_sel:], vo))

def moba_prompt(q, k, v, bias_tab):
    B, T, H, Dh = q.shape
    kb, vb, kmean = moba_blocks(k, v)
    ksel = min(MOBA_TOPK, kb.shape[1])
    qc = math.gcd(MOBA_QCHUNK, T)
    nq = T // qc
    q_chunks = jnp.moveaxis(q.astype(jnp.float32).reshape(B, nq, qc, H, Dh), 1, 0)
    p_chunks = jnp.arange(T, dtype=jnp.int32).reshape(nq, qc)
    o = lax.map(lambda a: moba_queries(a[0], a[1], kb, vb, kmean, bias_tab, ksel), (q_chunks, p_chunks))
    return jnp.moveaxis(o, 0, 1).reshape(B, T, H, Dh)

def moba_sample(q, k, v, past_k, past_v, bias_tab):
    P, T = past_k.shape[1], q.shape[1]
    kb, vb, kmean = moba_blocks(jnp.concatenate([past_k, k.astype(past_k.dtype)], axis=1),
                                jnp.concatenate([past_v, v.astype(past_v.dtype)], axis=1))
    ksel = min(MOBA_TOPK, kb.shape[1])
    pos = P + jnp.arange(T, dtype=jnp.int32)
    return moba_queries(q.astype(jnp.float32), pos, kb, vb, kmean, bias_tab, ksel)

def gather_pages(pool, page_table):
    g = pool[page_table]
    return g.reshape(g.shape[0], g.shape[1] * g.shape[2], g.shape[3], g.shape[4])

def merge_and_ffn(x, ya, yb, yc, oa, gates, gain, wa, wb, wc, wo, g_ffn, w_gu, w_dn):
    B, T, _ = x.shape
    ya = ya.astype(jnp.float32)
    ya = ya * lax.rsqrt(jnp.mean(ya * ya, axis=-1, keepdims=True) + EPS)
    ya = (ya.reshape(B, T, W_A) * gain.astype(jnp.float32) * jax.nn.sigmoid(oa.astype(jnp.float32))).astype(x.dtype)
    ga, gb, gc = jnp.split(jax.nn.sigmoid(gates), N_BRANCH, axis=-1)
    merged = (ga * (ya @ wa)
              + gb * (yb.reshape(B, T, W_B).astype(x.dtype) @ wb)
              + gc * (yc.reshape(B, T, W_C).astype(x.dtype) @ wc))
    x = x + merged @ wo
    h = rmsnorm(x, g_ffn)
    a, u = jnp.split(h @ w_gu, 2, axis=-1)
    return x + (jax.nn.silu(a) * u) @ w_dn

def prompt_layer(x, lw, bias_b, bias_c):
    g_mix, w_in_l, b_if_l, gain, wa, wb, wc, wo, g_ffn, w_gu, w_dn = lw
    B, T, _ = x.shape
    (qa, ka, va, ia, fa), oa, (qb, kb, vb), (qc, kc, vc), gates = project(x, g_mix, w_in_l, b_if_l)
    ya, C, n, m = mlstm(qa, ka, va, ia, fa,
                        jnp.zeros((B, H_A, HEAD_DIM, HEAD_DIM), jnp.float32),
                        jnp.zeros((B, H_A, HEAD_DIM), jnp.float32),
                        jnp.zeros((B, H_A), jnp.float32))
    kv_b = jnp.stack([kb, vb], axis=2)
    outs, lses, bufs = [], [], []
    for g, (win, dil) in enumerate(DSA_PAIRS):
        hs = slice(g * H_B_GROUP, (g + 1) * H_B_GROUP)
        o, lse = dsa_group_prompt(qb[:, :, hs], kb[:, :, hs], vb[:, :, hs], bias_b[:, hs], win, dil)
        outs.append(o)
        lses.append(lse)
        bufs.append(kv_b[:, T - min(win, T):, :, hs])
    yb = dsa_combine(outs, lses)
    yc = moba_prompt(qc, kc, vc, bias_c)
    x = merge_and_ffn(x, ya, yb, yc, oa, gates, gain, wa, wb, wc, wo, g_ffn, w_gu, w_dn)
    return x, (C, n, m), bufs, kc, vc

def sample_layer(x, lw, st_C, st_n, st_m, bufs_in, pool_k, pool_v, page_table, bias_b, bias_c):
    g_mix, w_in_l, b_if_l, gain, wa, wb, wc, wo, g_ffn, w_gu, w_dn = lw
    (qa, ka, va, ia, fa), oa, (qb, kb, vb), (qc, kc, vc), gates = project(x, g_mix, w_in_l, b_if_l)
    ya, C, n, m = mlstm(qa, ka, va, ia, fa, st_C, st_n, st_m)
    outs, lses, bufs = [], [], []
    for g, (win, dil) in enumerate(DSA_PAIRS):
        hs = slice(g * H_B_GROUP, (g + 1) * H_B_GROUP)
        o, lse, nbuf = dsa_group_sample(qb[:, :, hs], kb[:, :, hs], vb[:, :, hs], bufs_in[g], bias_b[:, hs], win, dil)
        outs.append(o)
        lses.append(lse)
        bufs.append(nbuf)
    yb = dsa_combine(outs, lses)
    yc = moba_sample(qc, kc, vc, gather_pages(pool_k, page_table), gather_pages(pool_v, page_table), bias_c)
    x = merge_and_ffn(x, ya, yb, yc, oa, gates, gain, wa, wb, wc, wo, g_ffn, w_gu, w_dn)
    return x, (C, n, m), bufs, kc, vc

def setup_inputs(seed: int = 0) -> dict:
    key = jax.random.key(seed)
    ks = jax.random.split(key, 32)
    n_pages = PAST_LEN // PAGE_SIZE
    n_used = DEC_BATCH * n_pages
    n_phys = n_used + n_used // 4

    def nrm(k, shape, scale=1.0):
        return scale * jax.random.normal(k, shape, jnp.float32)

    buf_shape = lambda win: (DEPTH, DEC_BATCH, min(win, PAST_LEN), 2, H_B_GROUP, HEAD_DIM)
    page_table = jax.random.permutation(ks[10], n_phys)[:n_used].reshape(DEC_BATCH, n_pages).astype(jnp.int32)
    b_if = jnp.concatenate([nrm(ks[14], (DEPTH, H_A), 0.1),
                            FORGET_BIAS + nrm(ks[15], (DEPTH, H_A), 0.1)], axis=-1)
    return {
        'x_prompt': nrm(ks[0], (BATCH, SEQ, D_MODEL)),
        'x_sample': nrm(ks[1], (DEC_BATCH, DEC_SEQ, D_MODEL)),
        'state_mlstm_C': nrm(ks[2], (DEPTH, DEC_BATCH, H_A, HEAD_DIM, HEAD_DIM), 0.1),
        'state_mlstm_n': nrm(ks[3], (DEPTH, DEC_BATCH, H_A, HEAD_DIM), 0.1),
        'state_mlstm_m': nrm(ks[4], (DEPTH, DEC_BATCH, H_A), 0.5),
        'cache_dsa_kv1': nrm(ks[5], buf_shape(DSA_PAIRS[0][0])),
        'cache_dsa_kv2': nrm(ks[6], buf_shape(DSA_PAIRS[1][0])),
        'cache_dsa_kv3': nrm(ks[7], buf_shape(DSA_PAIRS[2][0])),
        'cache_moba_k': nrm(ks[8], (DEPTH, n_phys, PAGE_SIZE, H_C, HEAD_DIM)),
        'cache_moba_v': nrm(ks[9], (DEPTH, n_phys, PAGE_SIZE, H_C, HEAD_DIM)),
        'page_table': page_table,
        'norm_mix': 1.0 + nrm(ks[11], (DEPTH, D_MODEL), 0.02),
        'w_in': nrm(ks[12], (DEPTH, D_MODEL, N_IN), D_MODEL ** -0.5),
        'b_if': b_if,
        'mlstm_gain': 1.0 + nrm(ks[13], (DEPTH, W_A), 0.02),
        'rel_bias': nrm(ks[16], (REL_BUCKETS, H_B + H_C), 0.1),
        'w_br_a': nrm(ks[17], (DEPTH, W_A, D_MODEL), W_A ** -0.5),
        'w_br_b': nrm(ks[18], (DEPTH, W_B, D_MODEL), W_B ** -0.5),
        'w_br_c': nrm(ks[19], (DEPTH, W_C, D_MODEL), W_C ** -0.5),
        'w_out': nrm(ks[20], (DEPTH, D_MODEL, D_MODEL), D_MODEL ** -0.5),
        'norm_ffn': 1.0 + nrm(ks[21], (DEPTH, D_MODEL), 0.02),
        'w_gate_up': nrm(ks[22], (DEPTH, D_MODEL, 2 * D_FF), D_MODEL ** -0.5),
        'w_down': nrm(ks[23], (DEPTH, D_FF, D_MODEL), D_FF ** -0.5),
        'norm_final': 1.0 + nrm(ks[24], (D_MODEL,), 0.02),
    }

def reference(x_prompt, x_sample, state_mlstm_C, state_mlstm_n, state_mlstm_m,
              cache_dsa_kv1, cache_dsa_kv2, cache_dsa_kv3, cache_moba_k, cache_moba_v, page_table,
              norm_mix, w_in, b_if, mlstm_gain, rel_bias, w_br_a, w_br_b, w_br_c, w_out,
              norm_ffn, w_gate_up, w_down, norm_final):
    bias_b = rel_bias[:, :H_B].astype(jnp.float32)
    bias_c = rel_bias[:, H_B:].astype(jnp.float32)
    dsa_caches = (cache_dsa_kv1, cache_dsa_kv2, cache_dsa_kv3)
    xp, xs = x_prompt, x_sample
    pC, pn, pm, sC, sn, sm = [], [], [], [], [], []
    pkv = [[] for _ in DSA_PAIRS]
    skv = [[] for _ in DSA_PAIRS]
    pk, pv, sk, sv = [], [], [], []
    for l in range(DEPTH):
        lw = (norm_mix[l], w_in[l], b_if[l], mlstm_gain[l], w_br_a[l], w_br_b[l], w_br_c[l], w_out[l],
              norm_ffn[l], w_gate_up[l], w_down[l])
        xp, st_p, bufs_p, kc_p, vc_p = prompt_layer(xp, lw, bias_b, bias_c)
        xs, st_s, bufs_s, kc_s, vc_s = sample_layer(
            xs, lw, state_mlstm_C[l], state_mlstm_n[l], state_mlstm_m[l],
            tuple(c[l] for c in dsa_caches), cache_moba_k[l], cache_moba_v[l], page_table, bias_b, bias_c)
        pC.append(st_p[0]); pn.append(st_p[1]); pm.append(st_p[2])
        sC.append(st_s[0]); sn.append(st_s[1]); sm.append(st_s[2])
        for g in range(len(DSA_PAIRS)):
            pkv[g].append(bufs_p[g])
            skv[g].append(bufs_s[g])
        pk.append(kc_p); pv.append(vc_p); sk.append(kc_s); sv.append(vc_s)
    y_prompt = rmsnorm(xp, norm_final)
    y_sample = rmsnorm(xs, norm_final)
    prompt_C, prompt_n, prompt_m = jnp.stack(pC), jnp.stack(pn), jnp.stack(pm)
    sample_C, sample_n, sample_m = jnp.stack(sC), jnp.stack(sn), jnp.stack(sm)
    prompt_kv1, prompt_kv2, prompt_kv3 = jnp.stack(pkv[0]), jnp.stack(pkv[1]), jnp.stack(pkv[2])
    sample_kv1, sample_kv2, sample_kv3 = jnp.stack(skv[0]), jnp.stack(skv[1]), jnp.stack(skv[2])
    prompt_k, prompt_v = jnp.stack(pk), jnp.stack(pv)
    sample_k, sample_v = jnp.stack(sk), jnp.stack(sv)
    return (y_prompt, y_sample, prompt_C, prompt_n, prompt_m, sample_C, sample_n, sample_m,
            prompt_kv1, prompt_kv2, prompt_kv3, sample_kv1, sample_kv2, sample_kv3,
            prompt_k, prompt_v, sample_k, sample_v)


_drawn_inputs = setup_inputs


def setup_inputs(seed=0):
    import zlib

    import numpy as np

    out = dict(_drawn_inputs(seed))
    spreads = {}
    factors = {'mlstm_gain': 8.0, 'rel_bias': 6.475, 'norm_ffn': 3.836, 'norm_final': 2.852}
    for name, (base, spread) in spreads.items():
        noise = np.random.default_rng([zlib.crc32(name.encode()), seed]).standard_normal(out[name].shape)
        drawn = base * np.exp(spread * noise) if base else spread * noise
        out[name] = jnp.asarray(drawn.astype(out[name].dtype))
    for name, factor in factors.items():
        out[name] = (out[name] * factor).astype(out[name].dtype)
    return out
```

```python
from contextlib import ExitStack

import numpy as np

import concourse.bass as bass
from concourse import mybir

ALU = mybir.AluOpType
ACT = mybir.ActivationFunctionType
AXX = mybir.AxisListType.X
F32 = mybir.dt.float32
F32R = mybir.dt.float32r

P = 128
D = 1024
KD = D // P
TP, NB, TB = 512, 8, 4
TS = NB * TB
T = TP + TS
H2 = T // 2
NT = TP // P
HD = 64
HA = 4
D_FF = 2816
KF = D_FF // P
N_QKV = 1032
N_GATE = 3336
REV = 640
NEG = -1e30
EPS = 1e-6
SCALE = HD ** -0.5
HEADS = 12


def kind_of(head):
    return 1 + head // 2 if head < 6 else 0


def rel_bucket(dist):
    dist = np.maximum(dist, 0)
    ratio = np.log(np.maximum(dist, 1).astype(np.float64) / 16) / np.log(2048 / 16)
    large = np.minimum(16 + (ratio * 16).astype(np.int64), 31)
    return np.where(dist < 16, dist, large)


def bias_selectors():
    dist = TP - 1 - np.arange(REV)
    out = np.zeros((33, 4, REV), np.float32)
    for kind in range(4):
        ok = dist >= 0
        if kind:
            win, dil = ((128, 1), (512, 4), (2048, 16))[kind - 1]
            ok = ok & (dist <= win) & (dist % dil == 0)
        out[rel_bucket(dist), kind, np.arange(REV)] = ok
        out[32, kind] = np.where(ok, 0.0, NEG)
    return out


C_ID, C_CM, C_NEW, C_SM, C_BM = 0, 128, 256, 288, 320
C_W = 328
R_SEL, R_RS, R_RM = 0, 512, 512 + T
R_W = 512 + 2 * T


def wide_constants():
    out = np.zeros((P, C_W), np.float32)
    r = np.arange(P)
    out[:, C_ID:C_ID + P] = np.eye(P)
    out[:, C_CM:C_CM + P] = np.where(r[None, :] >= r[:, None], 0.0, NEG)
    s = np.arange(TS)
    out[:, C_NEW:C_NEW + TS] = np.where((r[:, None] % TS) // TB == s[None, :] // TB, 0.0, NEG)
    same = (s[:, None] // TB == s[None, :] // TB) & (s[None, :] >= s[:, None])
    out[:TS, C_SM:C_SM + TS] = np.where(same, 0.0, NEG)
    out[:TS, C_BM:C_BM + NB] = s[:, None] // TB == np.arange(NB)[None, :]
    return out


def row_constants():
    out = np.zeros((HA, R_W), np.float32)
    for h in range(HA):
        out[h, R_SEL + P * h:R_SEL + P * (h + 1)] = -1.0
    starts = np.concatenate([[0], TP + TB * np.arange(NB)])
    out[:, R_RS:R_RS + T] = 1.0
    out[:, R_RS + starts] = 0.0
    out[:, R_RM + starts] = NEG
    return out


class Steps:

    def __init__(self, eng, sem, start=0):
        self.eng, self.sem, self.n = eng, sem, start

    def do(self, ins):
        ins.then_inc(self.sem, 1)
        self.n += 1
        return self.n

    def sync(self):
        self.eng.wait_ge(self.sem, self.n)

    def then(self, ins):
        self.do(ins)
        self.sync()


def build(nc, I, O, X):
    with ExitStack() as ctx:
        low = nc.sbuf_base
        low += -low % 64
        top = nc.sbuf_top
        ctx.enter_context(nc.sbuf_tensor("whole", [P, (top - low) // 4 - 16], F32))
        sems = {}

        def sem(name):
            if name not in sems:
                sems[name] = ctx.enter_context(nc.semaphore(name))
            return sems[name]

        class Map:

            def __init__(self, at):
                self.at = at

            def __call__(self, name, shape, dt=F32):
                n = 4 * int(np.prod(shape[1:]))
                assert self.at + n <= top - 64, (name, self.at, n, top)
                t = nc.alloc_sbuf_tensor_at(name, shape, dt, offset=self.at)
                self.at += n + (-n % 64)
                return t

        keep = Map(low)
        con = keep("con", [P, C_W])
        ident = con[:, C_ID:C_ID + P]
        rowc = keep("rowc", [HA, R_W])
        vecs = keep("vecs", [P, 26])
        ones = keep("ones", [P, P])
        eps = keep("eps", [P, 1])
        one = keep("one", [P, 1])
        rstd = keep("rstd", [P, T])
        ssq = keep("ssq", [P, T])
        xT = keep("xT", [P, KD, T])
        h_hi = keep("h_hi", [P, KD, T], F32R)
        h_lo = keep("h_lo", [P, KD, T], F32R)
        raw_at = keep.at
        raw = keep("raw", [P, 3, 2048])
        whi_at = keep.at
        w_hi = keep("w_hi", [P, 2, 1024], F32R)
        w_lo = keep("w_lo", [P, 2, 1024], F32R)
        sq_at = keep.at
        sq = keep("sq", [P, 2, T])
        region = keep.at

        acc = ctx.enter_context(nc.psum_tensor("acc", [P, 4, 1024], F32))

        def halves(slot):
            return acc[:, slot].rearrange("p (b n) -> p b n", b=2)[:, :, 0:H2]

        def two(ap):
            return ap.rearrange("p (b n) -> p b n", b=2)

        w_in, w_gu, w_dn, w_out = I["w_in"][0], I["w_gate_up"][0], I["w_down"][0], I["w_out"][0]

        def rows(w, k0, k1, c0, n):
            return w[k0 * P:k1 * P, c0:c0 + n].rearrange("(k p) n -> p k n", p=P)

        loads = []
        blocks = []

        def add_load(parts, kts, ncol):
            loads.append((parts, ncol))
            for j in range(ncol // P):
                blocks.append((len(loads) - 1, kts, ncol, j * P))

        loads.append(([(0, 0, rows(w_in, 0, KD, 1024, 32)), (0, 32, rows(w_in, 0, KD, 1028, 96))], P))
        blocks.append((0, KD, P, 0))
        for c in list(range(0, 1024, 256)) + list(range(N_QKV, N_GATE, 256)):
            add_load([(0, 0, rows(w_in, 0, KD, c, 256))], KD, 256)
        n_proj = len(blocks)
        for j in range(0, KD, 2):
            for g in range(3):
                add_load([(0, 0, rows(w_in, 0, KD, N_GATE + g * D + j * P, 256))], KD, 256)
            add_load([(0, 0, rows(I["w_br_a"][0], 0, 2, j * P, 256)),
                      (2, 0, rows(I["w_br_b"][0], 0, 3, j * P, 256)),
                      (5, 0, rows(I["w_br_c"][0], 0, 3, j * P, 256))], KD, 256)
        n_merge = len(blocks)
        for j in range(0, KD, 2):
            add_load([(0, 0, rows(w_out, 0, KD, j * P, 256))], KD, 256)
        n_wout = len(blocks)
        for j in range(0, KF, 2):
            add_load([(0, 0, rows(w_gu, 0, KD, j * P, 256))], KD, 256)
            add_load([(0, 0, rows(w_gu, 0, KD, D_FF + j * P, 256))], KD, 256)
        n_gu = len(blocks)
        DOWN = ((0, 8), (8, 16), (16, 22))
        for j in range(0, KD, 2):
            for k0, k1 in DOWN:
                add_load([(0, 0, rows(w_dn, k0, k1, j * P, 256))], k1 - k0, 256)
        n_all = len(blocks)
        w_loaded = [sem(f"w_loaded{i}") for i in range(3)]
        loaded_count = []
        seen = [0, 0, 0]
        for n, (parts, _) in enumerate(loads):
            seen[n % 3] += 16 * len(parts)
            loaded_count.append(seen[n % 3])
        last_block = {}
        for w, b in enumerate(blocks):
            last_block[b[0]] = w
        w_hi_done, w_lo_done, w_used = sem("w_hi_done"), sem("w_lo_done"), sem("w_used")

        def raw_block(w):
            load, kts, ncol, off = blocks[w]
            v = raw[:, load % 3, 0:kts * ncol].rearrange("p (k n) -> p k n", n=ncol)
            return v[:, :, off:off + P]

        def split_block(t, w):
            return t[:, w % 2, 0:blocks[w][1] * P].rearrange("p (k n) -> p k n", n=P)

        def load_weights(sp, lo, hi):
            for n in range(lo, hi):
                parts, ncol = loads[n]
                if n >= 3:
                    sp.wait_ge(w_lo_done, last_block[n - 3] + 1)
                for k0, c0, src in parts:
                    k, m = src.shape[1], src.shape[2]
                    kk = 8 if n else 8
                    dst = raw[:, n % 3, k0 * ncol:(k0 + k) * ncol].rearrange("p (k n) -> p k n", n=ncol)
                    sp.dma_start(dst[:, :, c0:c0 + m], src).then_inc(w_loaded[n % 3], 16)

        def load_range(b0, b1):
            return blocks[b0][0], blocks[b1 - 1][0] + 1

        def split_hi(act, w):
            load = blocks[w][0]
            act.wait_ge(w_loaded[load % 3], loaded_count[load])
            if w >= 2:
                act.wait_ge(w_used, w - 1)
            nc.scalar.activation(split_block(w_hi, w), raw_block(w), ACT.Copy).then_inc(w_hi_done, 1)

        def split_lo(dve, w):
            dve.wait_ge(w_hi_done, w + 1)
            nc.vector.tensor_tensor(split_block(w_lo, w), raw_block(w), split_block(w_hi, w).bitcast(F32),
                                    ALU.subtract).then_inc(w_lo_done, 1)

        def products(pe, w, slot, x_hi, x_lo, kx, kts=None, first=True, last=True, k_from=0):
            n = blocks[w][1] if kts is None else kts
            hi, lo = split_block(w_hi, w), split_block(w_lo, w)
            for k in range(n):
                for c, (a, b) in enumerate(((hi, x_hi), (hi, x_lo), (lo, x_hi))):
                    for half in range(2):
                        ins = nc.tensor.matmul(
                            acc[:, slot, 512 * half:512 * half + H2], a[:, k_from + k, :],
                            b[:, kx + k, H2 * half:H2 * (half + 1)],
                            start=first and k == 0 and c == 0, stop=last and k == n - 1 and c == 2)
            return ins

        def block(no):
            return nc.Block()

        m0 = Map(region)
        x_tok = m0("x_tok", [P, NT + 1, D])
        vrow = m0("vrow", [26, P])
        oh = m0("oh", [33, 4, REV])
        rb = m0("rb", [33, HEADS])
        rbb = m0("rbb", [33, HEADS, P])
        tabs = m0("tabs", [P, HEADS, REV])
        rev_d = X["rev"]
        s_in, s_par, s_xin = sem("s_in"), sem("s_par"), sem("s_xin")
        with nc.Block() as blk:
            @blk.sync
            def _(sp):
                sp.dma_start(con[:, :], X["con"]).then_inc(s_in, 16)
                sp.dma_start(vrow[0:8, :], I["norm_mix"].rearrange("o (k p) -> (o k) p", p=P)).then_inc(s_in, 16)
                sp.dma_start(vrow[8:16, :], I["norm_ffn"].rearrange("o (k p) -> (o k) p", p=P)).then_inc(s_in, 16)
                sp.dma_start(vrow[16:24, :], I["norm_final"].rearrange("(k p) -> k p", p=P)).then_inc(s_in, 16)
                sp.dma_start(vrow[24:26, :], I["mlstm_gain"].rearrange("o (k p) -> (o k) p", p=P)).then_inc(s_in, 16)
                sp.dma_start(x_tok[:, 0:NT, :], I["x_prompt"][0].rearrange("(i p) d -> p i d", p=P)).then_inc(s_xin, 16)
                sp.dma_start(x_tok[0:TS, NT, :], I["x_sample"].rearrange("b t d -> (b t) d")).then_inc(s_xin, 16)
                sp.dma_start(rowc[:, :], X["rowc"]).then_inc(s_par, 16)
                sp.dma_start(oh[:, :, :], X["oh"]).then_inc(s_par, 16)
                sp.dma_start(rb[0:32, :], I["rel_bias"]).then_inc(s_par, 16)
                load_weights(sp, 0, 3)
                sp.wait_ge(sem("tabs_done"), HEADS)
                sp.dma_start(rev_d.rearrange("p (h u) -> p h u", u=REV), tabs[:, :, :]).then_inc(sem("rev_out"), 16)
                sp.wait_ge(sem("rev_out"), 16)

            @blk.gpsimd
            def _(pool):
                st = Steps(pool, sem("s_set"))
                st.then(nc.gpsimd.memset(ones[:, :], 1.0))
                st.then(nc.gpsimd.memset(eps[:, :], EPS))
                st.then(nc.gpsimd.memset(one[:, :], 1.0))
                st.then(nc.gpsimd.memset(rb[32:33, :], 1.0))

            @blk.tensor
            def _(pe):
                pe.wait_ge(s_in, 80)
                nc.tensor.transpose(acc[:, 3, 0:26], vrow[:, :], ident[0:26, 0:26]).then_inc(sem("v_tr"), 1)
                pe.wait_ge(s_xin, 32)
                for k in range(KD):
                    if k >= 2:
                        pe.wait_ge(sem("x_ev"), k - 1)
                    for i in range(NT + 1):
                        n = P if i < NT else TS
                        ins = nc.tensor.transpose(acc[:, k % 2, P * i:P * i + n],
                                                  x_tok[0:n, i, P * k:P * (k + 1)], ident[0:n, 0:n])
                    ins.then_inc(sem("x_tr"), 1)
                for h in range(HEADS):
                    if h == 0:
                        pe.wait_ge(sem("rbb_done"), 1)
                    if h >= 1:
                        pe.wait_ge(sem("tabs_done"), h)
                    nc.tensor.matmul(acc[:, 2, 0:512], rbb[:, h, :], oh[:, kind_of(h), 0:512], start=True, stop=True)
                    nc.tensor.matmul(acc[:, 2, 512:REV], rbb[:, h, :], oh[:, kind_of(h), 512:REV],
                                     start=True, stop=True).then_inc(sem("tab_mm"), 1)
                pe.wait_ge(sem("sq_used"), KD)
                for half in range(2):
                    ins = nc.tensor.matmul(acc[:, 3, 512 * half:512 * half + H2], ones[:, :],
                                           ssq[:, H2 * half:H2 * (half + 1)], start=True, stop=True)
                ins.then_inc(sem("ssq_mm"), 1)

            @blk.scalar
            def _(act):
                st = Steps(act, sem("act_st"))
                act.wait_ge(sem("v_tr"), 1)
                act.wait_ge(sem("s_set"), 4)
                st.then(nc.scalar.copy(vecs[:, :], acc[:, 3, 0:26]))
                for k in range(KD):
                    act.wait_ge(sem("x_tr"), k + 1)
                    nc.scalar.copy(xT[:, k, :], acc[:, k % 2, 0:T]).then_inc(sem("x_ev"), 1)
                    act.wait_ge(sem("x_ev"), k + 1)
                    nc.scalar.activation(h_hi[:, k, :], xT[:, k, :], ACT.Copy, scale=vecs[:, k:k + 1]).then_inc(sem("h_hi_done"), 1)
                    if k >= 2:
                        act.wait_ge(sem("sq_used"), k - 1)
                    nc.scalar.activation(sq[:, k % 2, :], xT[:, k, :], ACT.Square).then_inc(sem("sq_done"), 1)
                for h in range(HEADS):
                    act.wait_ge(sem("tab_mm"), h + 1)
                    nc.scalar.copy(tabs[:, h, :], acc[:, 2, 0:REV]).then_inc(sem("tabs_done"), 1)
                act.wait_ge(sem("ssq_mm"), 1)
                nc.scalar.activation(two(rstd[:, :]), halves(3), ACT.Sqrt, bias=eps[:, :], scale=1.0 / D).then_inc(sem("std_done"), 1)

            @blk.vector
            def _(dve):
                st = Steps(dve, sem("dve_st"))
                dve.wait_ge(s_par, 48)
                dve.wait_ge(sem("s_set"), 4)
                nc.vector.tensor_copy(rbb[:, :, :], rb[:, :].unsqueeze(2).broadcast_to([33, HEADS, P])).then_inc(sem("rbb_done"), 1)
                for k in range(KD):
                    dve.wait_ge(sem("h_hi_done"), k + 1)
                    dve.wait_ge(sem("act_st"), 1)
                    nc.vector.scalar_tensor_tensor(h_lo[:, k, :], xT[:, k, :], vecs[:, k:k + 1],
                                                   h_hi[:, k, :].bitcast(F32), ALU.mult, ALU.subtract)
                    dve.wait_ge(sem("sq_done"), k + 1)
                    if k == 0:
                        nc.vector.tensor_copy(ssq[:, :], sq[:, 0, :]).then_inc(sem("sq_used"), 1)
                    else:
                        dve.wait_ge(sem("sq_used"), k)
                        nc.vector.tensor_tensor(ssq[:, :], ssq[:, :], sq[:, k % 2, :], ALU.add).then_inc(sem("sq_used"), 1)
                dve.wait_ge(sem("std_done"), 1)
                st.then(nc.vector.reciprocal(rstd[:, :], rstd[:, :]))

        m1 = Map(region)
        qT = m1("qT", [P, 8, T])
        after_q = m1.at
        kT = m1("kT", [P, 8, T])
        oaT = m1("oaT", [P, 2, T])
        va_tok = m1("va_tok", [P, NT + 1, HA, HD + 1])
        ka_tok = m1("ka_tok", [P, NT + 1, HA * HD])
        v_tok = m1("v_tok", [P, NT + 1, HEADS * HD])
        grow0 = m1("i_row", [HA, T])
        frow = m1("f_row", [HA, T])
        bif = m1("bif", [HA, 2])
        after_kv = m1.at
        v_st = m1("v_st", [P, 2, T])
        k_st = m1("k_st", [P, 2, NT + 1, P])
        kinds = [("if", 0)] + [(n, i) for n, c in
                               (("qa", 2), ("ka", 2), ("va", 2), ("oa", 2), ("qb", 3), ("kb", 3), ("vb", 3),
                                ("qc", 3), ("kc", 3), ("vc", 3)) for i in range(c)]
        assert len(kinds) == n_proj
        Q0 = {"a": 0, "b": 2, "c": 5}
        turns = [w for w, (n, _) in enumerate(kinds) if n[0] in "kv"]
        (o_yp, o_ys, o_pC, o_pn, o_pm, o_sC, o_sn, o_sm, o_pkv1, o_pkv2, o_pkv3, o_skv1, o_skv2, o_skv3,
         o_pk, o_pv, o_sk, o_sv) = O
        o_pkv, o_skv = (o_pkv1, o_pkv2, o_pkv3), (o_skv1, o_skv2, o_skv3)
        LW = (128, 256, 256)
        caches = (I["cache_dsa_kv1"], I["cache_dsa_kv2"], I["cache_dsa_kv3"])

        def turned_from(t):
            name, i = kinds[turns[t]]
            if name[0] == "k":
                return kT[:, Q0[name[1]] + i, :]
            return v_st[:, sum(kinds[w][0][0] == "v" for w in turns[:t]) % 2, :]

        ev_mul = sem("proj_ev")
        k_turns = [t for t in range(len(turns)) if kinds[turns[t]][0][0] == "k"]
        k_stores = [t for t in k_turns if kinds[turns[t]][0] != "ka"]
        k_stored = [sem("k_stored0"), sem("k_stored1")]
        v_turns = [t for t in range(len(turns)) if kinds[turns[t]][0][0] == "v"]

        def store_tok(sp, t, prompt, sample):
            name, i = kinds[turns[t]]
            s = 0 if name[0] == "k" else 1
            done = k_stored[k_stores.index(t) % 2] if s == 0 else sem("v_stored")
            if name[1] == "b":
                lw = min((128, 512, 2048)[i], TP)
                dst = o_pkv[i][0, 0].rearrange("(i p) s h d -> p i s (h d)", p=P)[:, :, s, :]
                sp.dma_start(dst, prompt[:, NT - lw // P:NT, :]).then_inc(done, 16)
                n = LW[i]
                dst = o_skv[i][0, :, n - TB:n, s].rearrange("b t h d -> b t (h d)")
                sp.dma_start(dst, sample).then_inc(done, 16)
            else:
                o_p, o_s = ((o_pk, o_sk), (o_pv, o_sv))[s]
                dst = o_p[0, 0].rearrange("(i p) h d -> p i (h d)", p=P)[:, :, P * i:P * (i + 1)]
                sp.dma_start(dst, prompt).then_inc(done, 16)
                dst = o_s[0].rearrange("b t h d -> (b t) (h d)")[:, P * i:P * (i + 1)]
                sp.dma_start(dst, sample).then_inc(done, 16)

        def token_place(t):
            name, i = kinds[turns[t]]
            if name == "ka":
                v = ka_tok[:, :, P * i:P * (i + 1)]
            elif name == "va":
                v = va_tok[:, :, 2 * i:2 * i + 2, 0:HD]
            elif name[0] == "v":
                c = P * (i + (0 if name == "vb" else 3))
                v = v_tok[:, :, c:c + P]
            else:
                v = k_st[:, k_stores.index(t) % 2]
            return v[:, 0:NT], v[0:TS, NT]

        def copy_tok(act, t):
            act.wait_ge(sem("tok_tr"), t + 1)
            name, i = kinds[turns[t]]
            if t in k_stores and k_stores.index(t) >= 2:
                n = k_stores.index(t)
                act.wait_ge(k_stored[n % 2], 32 * (n // 2))
            pr, sa = token_place(t)
            src = acc[:, 2 + t % 2, 0:TP]
            ssrc = acc[0:TS, 2 + t % 2, TP:TP + P]
            if name == "va":
                src = src.rearrange("p (i h d) -> p i h d", h=2, d=HD)
                ssrc = ssrc.rearrange("p (h d) -> p h d", d=HD)
            else:
                src = src.rearrange("p (i c) -> p i c", c=P)
            nc.scalar.copy(pr, src)
            nc.scalar.copy(sa, ssrc).then_inc(sem("tok_done"), 1)

        with nc.Block() as blk:
            @blk.sync
            def _(sp):
                sp.dma_start(bif[:, :], I["b_if"].rearrange("o (c h) -> (o h) c", c=2),
                             allow_slow_non_contiguous=True).then_inc(sem("bif_in"), 16)
                for g in range(3):
                    n = LW[g]
                    sp.dma_start(o_skv[g][0, :, 0:n - TB].rearrange("b w s h d -> b (w s h d)"),
                                 caches[g][0, :, TB:n].rearrange("b w s h d -> b (w s h d)")).then_inc(sem("kv_out"), 16)
                lo, hi = load_range(0, n_proj)
                load_weights(sp, 3, hi)
                sp.wait_ge(sem("kv_out"), 16 * 3)

            @blk.scalar
            def _(act):
                for w in range(n_proj):
                    split_hi(act, w)
                    for t in [t for t in range(len(turns)) if turns[t] == w - 2]:
                        copy_tok(act, t)
                for t in [t for t in range(len(turns)) if turns[t] >= n_proj - 2]:
                    copy_tok(act, t)

            @blk.gpsimd
            def _(pool):
                nc.gpsimd.memset(va_tok[:, :, :, HD:HD + 1], 1.0).then_inc(sem("va_one"), 1)
                for t in [t for t in range(len(turns)) if kinds[turns[t]][0][1] != "a"]:
                    pool.wait_ge(sem("tok_done"), t + 1)
                    store_tok(pool, t, *token_place(t))
                for s in k_stored:
                    pool.wait_ge(s, 32 * 3)
                pool.wait_ge(sem("v_stored"), 32 * 6)

            @blk.vector
            def _(dve):
                split_lo(dve, 0)
                for w in range(n_proj):
                    if w + 1 < n_proj:
                        split_lo(dve, w + 1)
                    name, i = kinds[w]
                    dve.wait_ge(w_used, w + 1)
                    src = halves(w % 2)
                    if name == "if":
                        nc.vector.tensor_tensor(two(grow0[:, :]), src[0:HA], two(rstd[0:HA, :]), ALU.mult)
                        nc.vector.tensor_tensor(two(frow[:, :]), src[32:32 + HA], two(rstd[32:32 + HA, :]),
                                                ALU.mult).then_inc(ev_mul, 1)
                        continue
                    if name[0] == "v":
                        t = turns.index(w)
                        n = v_turns.index(t)
                        if n >= 2:
                            dve.wait_ge(sem("tok_tr"), v_turns[n - 2] + 1)
                        dst = v_st[:, n % 2, :]
                    elif name == "oa":
                        dst = oaT[:, i, :]
                    else:
                        dst = (qT if name[0] == "q" else kT)[:, Q0[name[1]] + i, :]
                    if name in ("ka", "qb", "qc"):
                        nc.vector.scalar_tensor_tensor(two(dst), src, SCALE, two(rstd[:, :]),
                                                       ALU.mult, ALU.mult).then_inc(ev_mul, 1)
                    else:
                        nc.vector.tensor_tensor(two(dst), src, two(rstd[:, :]), ALU.mult).then_inc(ev_mul, 1)

            @blk.tensor
            def _(pe):
                def turn(t):
                    pe.wait_ge(ev_mul, turns[t] + 1)
                    if t >= 2:
                        pe.wait_ge(sem("tok_done"), t - 1)
                    src = turned_from(t)
                    for i in range(NT + 1):
                        n = P if i < NT else TS
                        ins = nc.tensor.transpose(acc[0:n, 2 + t % 2, P * i:P * (i + 1)], src[:, P * i:P * i + n], ident)
                    ins.then_inc(sem("tok_tr"), 1)

                for w in range(n_proj):
                    pe.wait_ge(w_lo_done, w + 1)
                    if w >= 2:
                        pe.wait_ge(ev_mul, w - 1)
                    ins = products(pe, w, w % 2, h_hi, h_lo, 0)
                    ins.then_inc(w_used, 1)
                    for t in [t for t in range(len(turns)) if turns[t] == w - 1]:
                        turn(t)
                for t in [t for t in range(len(turns)) if turns[t] >= n_proj - 1]:
                    turn(t)

        m2 = Map(after_kv)
        rA = m2("rA", [HA, T])
        rB = frow
        b_row = m2("b_row", [HA, T])
        g_row = m2("g_row", [HA, T])
        m_row = m2("m_row", [HA, T])
        m0_row = m2("m0_row", [HA, NB])
        small = m2("small", [HA, 2 * TS + NB])
        hA = m2("hA", [P, NT + 1, HA, HD])
        by_tok = m2("by_tok", [P, 48])
        e_m = m2("e_m", [P, 20])
        ws = m2("ws", [P, 4 * NT])
        W = m2("W", [P, 2, TP])
        PT = m2("PT", [P, 1280])
        kw = m2("kw", [P, NT, HD])
        den = m2("den", [P, 8])
        st_o = m2("st_o", [HD, HD + 1])
        s_cn = Map(m2.at)("C0n", [P, NB, 2, HD + 1])
        m2.at += NB * 2 * (HD + 1) * 4
        m2.at += -m2.at % 64
        SPT = W[0:TS, 0, 0:HA * TS]
        Swt = W[0:TS, 1, 0:HA * TS]
        oA = m2("oA", [TS, HA * (HD + 1)])
        G = Map(raw_at)("G", [P, HA, TP])
        in_sq = Map(sq_at)
        QpA = in_sq("QpA", [P, 2, NB, TS])
        kws = m2("kws", [TS, HA * HD])
        Vb = in_sq("Vb", [TS, NB, HD + 1])
        rs = m2("rs", [P, (NT + 1) * HA])
        dcy = m2("dcy", [P, 2, NB])
        A_OFF = (0, 512, 896, 1152)

        def par(h):
            return HD * (h % 2)

        d2 = sem("d2")
        with nc.Block() as blk:
            @blk.sync
            def _(sp):
                sp.dma_start(m0_row[:, :], I["state_mlstm_m"].rearrange("o b h -> (o h) b"),
                             allow_slow_non_contiguous=True).then_inc(sem("st_in"), 16)
                for h in range(HA):
                    p = par(h)
                    sp.dma_start(s_cn[p:p + HD, :, h // 2, 0:HD], I["state_mlstm_C"][0, :, h].rearrange("b k v -> k b v")).then_inc(sem("st_in"), 16)
                    sp.dma_start(s_cn[p:p + HD, :, h // 2, HD], I["state_mlstm_n"][0, :, h].rearrange("b k -> k b"),
                                 allow_slow_non_contiguous=True).then_inc(sem("st_in"), 16)
                sp.wait_ge(sem("rows_done"), 1)
                sp.dma_start(o_pm.rearrange("o b h -> h (o b)"), m_row[:, TP - 1:TP], allow_slow_non_contiguous=True).then_inc(sem("a_out"), 16)
                sp.dma_start(o_sm.rearrange("o b h -> (o h) b"), m_row[:, TP + TB - 1:T:TB],
                             allow_slow_non_contiguous=True).then_inc(sem("a_out"), 16)
                for h in range(HA):
                    sp.wait_ge(sem("stp_ev"), h + 1)
                    sp.dma_start(o_pC[0, 0, h], st_o[:, 0:HD]).then_inc(sem("st_stored"), 16)
                    sp.dma_start(o_pn[0, 0, h].rearrange("(k o) -> k o", o=1), st_o[:, HD:HD + 1],
                                 allow_slow_non_contiguous=True).then_inc(sem("st_stored"), 16)
                for h in range(HA):
                    p = par(h)
                    sp.wait_ge(sem("cn_done"), h + 1)
                    sp.dma_start(o_sC[0, :, h].rearrange("b k v -> k b v"), s_cn[p:p + HD, :, h // 2, 0:HD]).then_inc(sem("a_out"), 16)
                    sp.dma_start(o_sn[0, :, h].rearrange("b k -> k b"), s_cn[p:p + HD, :, h // 2, HD],
                                 allow_slow_non_contiguous=True).then_inc(sem("a_out"), 16)
                sp.wait_ge(sem("a_out"), 160)
                sp.wait_ge(sem("st_stored"), 32 * HA)

            @blk.gpsimd
            def _(pool):
                st = Steps(pool, sem("pool2"))
                st.then(nc.gpsimd.memset(QpA[:, :, :, :], 0.0))
                st.then(nc.gpsimd.memset(hA[:, NT], 0.0))

            @blk.scalar
            def _(act):
                a2 = Steps(act, sem("a2"))
                act.wait_ge(sem("f_ready"), 1)
                a2.then(nc.scalar.activation(rB[:, :], rB[:, :], ACT.Exp))
                nc.scalar.activation(rB[:, :], rB[:, :], ACT.Ln, bias=one[0:HA, :]).then_inc(sem("ln_done"), 1)
                act.wait_ge(sem("rows_done"), 2)
                nc.scalar.activation(small[:, :], small[:, :], ACT.Exp).then_inc(sem("small_done"), 1)
                act.wait_ge(sem("tr2"), 1)
                a2.then(nc.scalar.copy(by_tok[:, 0:32], acc[:, 0, 0:32]))
                a2.then(nc.scalar.copy(by_tok[0:TS, 32:48], acc[0:TS, 0, 32:48]))
                a2.then(nc.scalar.activation(e_m[:, 0:16], by_tok[:, 16:32], ACT.Exp, scale=-1.0))
                nc.scalar.activation(e_m[0:TS, 16:20], by_tok[0:TS, 36:40], ACT.Exp, scale=-1.0).then_inc(sem("bytok_done"), 1)
                act.wait_ge(sem("g_mm"), 1)
                nc.scalar.copy(G[:, :, :], acc[:, 2:4].rearrange("p s (b n) -> p (s b) n", n=512)).then_inc(sem("g_ev"), 1)
                act.wait_ge(sem("ws_arg"), 1)
                nc.scalar.activation(ws[:, :], ws[:, :], ACT.Exp).then_inc(sem("ws_done"), 1)
                for u in range(HA * NT):
                    h, i = divmod(u, NT)
                    bias = by_tok[:, HA * i + h:HA * i + h + 1]
                    act.wait_ge(sem("w_arg"), u + 1)
                    Wb = W[:, u % 2]
                    if i < NT - 1:
                        nc.scalar.activation(Wb[:, P:TP - P * i], G[:, h, P * (i + 1):TP], ACT.Exp, bias=bias)
                    nc.scalar.activation(Wb[:, 0:P], Wb[:, 0:P], ACT.Exp, bias=bias).then_inc(sem("w_done"), 1)
                act.wait_ge(sem("sw_arg"), 1)
                for h in range(HA):
                    ins = nc.scalar.activation(Swt[:, TS * h:TS * (h + 1)], Swt[:, TS * h:TS * (h + 1)], ACT.Exp,
                                               bias=by_tok[0:TS, 32 + h:33 + h])
                ins.then_inc(sem("sw_done"), 1)
                act.wait_ge(sem("oa_arg"), 1)
                nc.scalar.activation(oaT[:, :, :], oaT[:, :, :], ACT.Sigmoid).then_inc(sem("oa_done"), 1)
                nc.scalar.activation(rs[:, :], rs[:, :], ACT.Sqrt, bias=eps[:, :], scale=1.0 / HD).then_inc(sem("oa_done"), 1)

            @blk.vector
            def _(dve):
                v = Steps(dve, d2)
                dve.wait_ge(sem("bif_in"), 16)
                dve.wait_ge(sem("st_in"), 16 * 9)
                v.do(nc.vector.tensor_scalar(grow0[:, :], grow0[:, :], bif[:, 0:1], None, ALU.add))
                v.then(nc.vector.tensor_scalar(rA[:, :], frow[:, :], bif[:, 1:2], 0.0, ALU.add, ALU.min))
                v.then(nc.vector.tensor_scalar(rB[:, :], frow[:, :], bif[:, 1:2], None, ALU.add))
                v.then(nc.vector.scalar_tensor_tensor(rB[:, :], rB[:, :], -1.0, rB[:, :], ALU.mult, ALU.min))
                nc.vector.nop().then_inc(sem("f_ready"), 1)
                dve.wait_ge(sem("ln_done"), 1)
                v.then(nc.vector.tensor_tensor(rA[:, :], rA[:, :], rB[:, :], ALU.subtract))
                v.then(nc.vector.tensor_tensor_scan(b_row[:, :], rowc[:, R_RS:R_RS + T], rA[:, :], 0.0, ALU.mult, ALU.add))
                v.then(nc.vector.tensor_tensor(rA[:, :], grow0[:, :], b_row[:, :], ALU.subtract))
                v.then(nc.vector.tensor_copy(rB[:, :], rA[:, :]))
                v.do(nc.vector.tensor_scalar(rB[:, 0:1], rB[:, 0:1], 0.0, None, ALU.max))
                v.then(nc.vector.tensor_tensor(rB[:, TP:T:TB], rB[:, TP:T:TB], m0_row[:, :], ALU.max))
                v.then(nc.vector.tensor_tensor_scan(g_row[:, :], rowc[:, R_RM:R_RM + T], rB[:, :], 0.0, ALU.add, ALU.max))
                v.then(nc.vector.tensor_tensor(m_row[:, :], b_row[:, :], g_row[:, :], ALU.add))
                gs = g_row[:, TP:T].rearrange("h (b t) -> h b t", t=TB)
                nc.vector.nop().then_inc(sem("rows_done"), 1)
                v.do(nc.vector.tensor_tensor(small[:, 0:TS].rearrange("h (b t) -> h b t", t=TB),
                                             m0_row[:, :].unsqueeze(2).broadcast_to([HA, NB, TB]), gs, ALU.subtract))
                v.do(nc.vector.tensor_tensor(small[:, TS:2 * TS].rearrange("h (b t) -> h b t", t=TB),
                                             rA[:, TP:T].rearrange("h (b t) -> h b t", t=TB),
                                             gs[:, :, TB - 1:TB].broadcast_to([HA, NB, TB]), ALU.subtract))
                v.then(nc.vector.tensor_tensor(small[:, 2 * TS:], m0_row[:, :], g_row[:, TP + TB - 1:T:TB], ALU.subtract))
                nc.vector.nop().then_inc(sem("rows_done"), 1)
                dve.wait_ge(sem("bytok_done"), 1)
                dve.wait_ge(sem("g_ev"), 1)
                gT = G[:, :, TP - 1]
                v.then(nc.vector.tensor_tensor(ws[:, :].rearrange("p (i h) -> p i h", h=HA),
                                               by_tok[:, 0:16].rearrange("p (i h) -> p i h", h=HA),
                                               gT.unsqueeze(1).broadcast_to([P, NT, HA]), ALU.add))
                nc.vector.nop().then_inc(sem("ws_arg"), 1)
                dve.wait_ge(sem("ws_done"), 1)
                dve.wait_ge(sem("va_one"), 1)
                for h in range(HA):

                    def arg(u):
                        i = u % NT
                        hh = u // NT
                        nc.vector.tensor_tensor(W[:, u % 2, 0:P], G[:, hh, P * i:P * (i + 1)], con[:, C_CM:C_CM + P],
                                                ALU.add).then_inc(sem("w_arg"), 1)
                    if h == 0:
                        arg(0)
                    for i in range(NT):
                        u = NT * h + i
                        if u + 1 < HA * NT:
                            if u >= 1:
                                dve.wait_ge(sem("pt_done"), u)
                            arg(u + 1)
                        dve.wait_ge(sem("w_done"), u + 1)
                        dve.wait_ge(sem("a_s"), u + 1)
                        if i == 0 and h >= 1:
                            dve.wait_ge(sem("a_o"), h)
                        n = TP - P * i
                        nc.vector.tensor_tensor(PT[:, A_OFF[i]:A_OFF[i] + n], acc[:, 0, 512 * (u % 2):512 * (u % 2) + n],
                                                W[:, u % 2, 0:n], ALU.mult).then_inc(sem("pt_done"), 1)
                    if h >= 1:
                        dve.wait_ge(sem("a_st"), h)
                    nc.vector.tensor_tensor(kw[:, :, :], ka_tok[:, 0:NT, HD * h:HD * (h + 1)],
                                            ws[:, h:16:HA].unsqueeze(2).broadcast_to([P, NT, HD]), ALU.mult).then_inc(sem("kw_done"), 1)
                    dve.wait_ge(sem("a_o"), h + 1)
                    o = acc[:, 1, 0:NT * (HD + 1)].rearrange("p (i c) -> p i c", c=HD + 1)
                    v.then(nc.vector.tensor_copy(den[:, 0:NT], o[:, :, HD]))
                    v.then(nc.vector.scalar_tensor_tensor(den[:, 0:NT], den[:, 0:NT], -1.0, den[:, 0:NT], ALU.mult, ALU.max))
                    v.then(nc.vector.tensor_tensor(den[:, 0:NT], den[:, 0:NT], e_m[:, h:16:HA], ALU.max))
                    v.then(nc.vector.reciprocal(den[:, 0:NT], den[:, 0:NT]))
                    v.then(nc.vector.tensor_tensor(hA[:, 0:NT, h, :], o[:, :, 0:HD],
                                                   den[:, 0:NT].unsqueeze(2).broadcast_to([P, NT, HD]), ALU.mult))
                    nc.vector.nop().then_inc(sem("h_done"), 1)
                    dve.wait_ge(sem("a_st"), h + 1)
                    if h >= 1:
                        dve.wait_ge(sem("st_stored"), 32 * h)
                    nc.vector.tensor_copy(st_o[:, :], acc[0:HD, 1, 512:512 + HD + 1]).then_inc(sem("stp_ev"), 1)
                dve.wait_ge(sem("pool2"), 2)
                for h in range(HA):
                    p = par(h)
                    at = QpA[p:p + HD, h // 2, 0, 0:1]
                    v.do(nc.vector.tensor_copy(
                        bass.AP(at.tensor, at.offset, [at.ap[0], [TS + TB, NB], [1, TB]]),
                        qT[p:p + HD, h // 2, TP:T].rearrange("p (b t) -> p b t", t=TB)))
                v.sync()
                nc.vector.nop().then_inc(sem("qp_done"), 1)
                dve.wait_ge(sem("sg_mm"), 1)
                nc.vector.tensor_tensor(Swt.rearrange("p (h t) -> p h t", t=TS),
                                        acc[0:TS, 2, 0:HA * TS].rearrange("p (h t) -> p h t", t=TS),
                                        con[0:TS, C_SM:C_SM + TS].unsqueeze(1).broadcast_to([TS, HA, TS]),
                                        ALU.add).then_inc(sem("sw_arg"), 1)
                dve.wait_ge(sem("sw_done"), 1)
                dve.wait_ge(sem("pe_order"), 2)
                nc.vector.tensor_tensor(SPT, acc[0:TS, 2, 512:512 + HA * TS], Swt, ALU.mult).then_inc(sem("spt_done"), 1)
                v.do(nc.vector.tensor_tensor(kws[:, :].rearrange("p (h d) -> p h d", d=HD),
                                             ka_tok[0:TS, NT, :].rearrange("p (h d) -> p h d", d=HD),
                                             by_tok[0:TS, 44:48].unsqueeze(2).broadcast_to([TS, HA, HD]), ALU.mult))
                dve.wait_ge(sem("so_mm"), 1)
                v.then(nc.vector.tensor_copy(oA[:, :], acc[0:TS, 0, 0:HA * (HD + 1)]))
                for h in range(HA):
                    c = h * (HD + 1)
                    v.do(nc.vector.scalar_tensor_tensor(oA[:, c:c + HD + 1], acc[0:TS, 0, 512 + c:512 + c + HD + 1],
                                                        by_tok[0:TS, 40 + h:41 + h], oA[:, c:c + HD + 1], ALU.mult, ALU.add))
                v.sync()
                o = oA[:, :].rearrange("p (h c) -> p h c", c=HD + 1)
                v.then(nc.vector.scalar_tensor_tensor(den[0:TS, 0:HA], o[:, :, HD], -1.0, o[:, :, HD], ALU.mult, ALU.max))
                v.then(nc.vector.tensor_tensor(den[0:TS, 0:HA], den[0:TS, 0:HA], e_m[0:TS, 16:20], ALU.max))
                v.then(nc.vector.reciprocal(den[0:TS, 0:HA], den[0:TS, 0:HA]))
                v.then(nc.vector.tensor_tensor(hA[0:TS, NT], o[:, :, 0:HD], den[0:TS, 0:HA].unsqueeze(2).broadcast_to([TS, HA, HD]), ALU.mult))
                dve.wait_ge(sem("dc_mm"), 1)
                v.then(nc.vector.tensor_scalar(dcy[:, :, :], acc[:, 3, 0:2 * NB].rearrange("p (a b) -> p a b", b=NB), -1.0, None, ALU.mult))
                for h in range(HA):
                    p = par(h)
                    if h >= 1:
                        dve.wait_ge(sem("sst_mm"), h)
                    v.then(nc.vector.tensor_tensor(Vb[:, :, :], va_tok[0:TS, NT, h, :].unsqueeze(1).broadcast_to([TS, NB, HD + 1]),
                                                   con[0:TS, C_BM:C_BM + NB].unsqueeze(2).broadcast_to([TS, NB, HD + 1]), ALU.mult))
                    nc.vector.nop().then_inc(sem("vb_done"), 1)
                    cn = s_cn[p:p + HD, :, h // 2, :]
                    v.then(nc.vector.tensor_tensor(cn, cn, dcy[p:p + HD, h // 2, :].unsqueeze(2).broadcast_to([HD, NB, HD + 1]), ALU.mult))
                    dve.wait_ge(sem("sst_mm"), h + 1)
                    for half in range(2):
                        v.do(nc.vector.tensor_tensor(
                            cn[:, 4 * half:4 * half + 4], cn[:, 4 * half:4 * half + 4],
                            acc[p:p + HD, 1, 512 * half:512 * half + 4 * (HD + 1)].rearrange("p (b c) -> p b c", c=HD + 1), ALU.add))
                    v.sync()
                    nc.vector.nop().then_inc(sem("cn_done"), 1)
                hh = hA[:, :, :, :].rearrange("p i h d -> p (i h) d")
                hsq = PT[:, 0:(NT + 1) * HA * HD].rearrange("p (n d) -> p n d", d=HD)
                dve.wait_ge(sem("a_o"), HA)
                v.then(nc.vector.tensor_tensor(hsq, hh, hh, ALU.mult))
                v.then(nc.vector.tensor_reduce(rs[:, :], hsq, AXX, ALU.add))
                nc.vector.nop().then_inc(sem("oa_arg"), 1)
                dve.wait_ge(sem("oa_done"), 2)
                v.then(nc.vector.reciprocal(rs[:, :], rs[:, :]))
                v.then(nc.vector.tensor_tensor(hh, hh, rs[:, :].unsqueeze(2).broadcast_to([P, (NT + 1) * HA, HD]), ALU.mult))
                nc.vector.nop().then_inc(sem("hn_done"), 1)
                for pr in range(2):
                    dve.wait_ge(sem("ya_tr"), pr + 1)
                    v.do(nc.vector.scalar_tensor_tensor(qT[:, pr, :], acc[:, pr, 0:T], vecs[:, 24 + pr:25 + pr],
                                                        oaT[:, pr, :], ALU.mult, ALU.mult))

            @blk.tensor
            def _(pe):
                pe.wait_ge(sem("rows_done"), 2)
                for i in range(NT):
                    nc.tensor.transpose(acc[:, 0, HA * i:HA * (i + 1)], rA[:, P * i:P * (i + 1)], ident[0:HA, 0:HA])
                    nc.tensor.transpose(acc[:, 0, 16 + HA * i:16 + HA * (i + 1)], m_row[:, P * i:P * (i + 1)], ident[0:HA, 0:HA])
                nc.tensor.transpose(acc[0:TS, 0, 32:36], rA[:, TP:T], ident[0:HA, 0:HA])
                nc.tensor.transpose(acc[0:TS, 0, 36:40], m_row[:, TP:T], ident[0:HA, 0:HA])
                pe.wait_ge(sem("small_done"), 1)
                nc.tensor.transpose(acc[0:TS, 0, 40:44], small[:, 0:TS], ident[0:HA, 0:HA])
                nc.tensor.transpose(acc[0:TS, 0, 44:48], small[:, TS:2 * TS], ident[0:HA, 0:HA]).then_inc(sem("tr2"), 1)
                for h in range(HA):
                    ins = nc.tensor.matmul(acc[:, 2 + h // 2, 512 * (h % 2):512 * (h % 2) + TP],
                                           rowc[:, R_SEL + P * h:R_SEL + P * (h + 1)], g_row[:, 0:TP], start=True, stop=True)
                ins.then_inc(sem("g_mm"), 1)
                pe.wait_ge(sem("bytok_done"), 1)
                for u in range(HA * NT):
                    h, i = divmod(u, NT)
                    p = par(h)
                    if u >= 2:
                        pe.wait_ge(sem("pt_done"), u - 1)
                    nc.tensor.matmul(acc[:, 0, 512 * (u % 2):512 * (u % 2) + TP - P * i],
                                     kT[p:p + HD, h // 2, P * i:P * (i + 1)], qT[p:p + HD, h // 2, P * i:TP],
                                     start=True, stop=True).then_inc(sem("a_s"), 1)
                    if i == NT - 1:
                        pe.wait_ge(sem("pt_done"), u + 1)
                        if h >= 1:
                            pe.wait_ge(sem("h_done"), h)
                        for j in range(NT):
                            for s in range(j + 1):
                                o = A_OFF[s] + P * (j - s)
                                ins = nc.tensor.matmul(acc[:, 1, (HD + 1) * j:(HD + 1) * (j + 1)], PT[:, o:o + P],
                                                       va_tok[:, s, h, :], start=s == 0, stop=s == j)
                        ins.then_inc(sem("a_o"), 1)
                        pe.wait_ge(sem("kw_done"), h + 1)
                        if h >= 1:
                            pe.wait_ge(sem("stp_ev"), h)
                        for s in range(NT):
                            ins = nc.tensor.matmul(acc[0:HD, 1, 512:512 + HD + 1], kw[:, s, :], va_tok[:, s, h, :],
                                                   start=s == 0, stop=s == NT - 1)
                        ins.then_inc(sem("a_st"), 1)
                for h in range(HA):
                    ins = nc.tensor.matmul(acc[0:TS, 2, TS * h:TS * (h + 1)], rowc[:, R_SEL + P * h:R_SEL + P * h + TS],
                                           g_row[:, TP:T], start=True, stop=True)
                ins.then_inc(sem("sg_mm"), 1)
                order = Steps(pe, sem("pe_order"))
                for h in (0, 2, 1, 3):
                    p = par(h)
                    ins = nc.tensor.matmul(acc[0:TS, 2, 512 + TS * h:512 + TS * (h + 1)], kT[p:p + HD, h // 2, TP:T],
                                           qT[p:p + HD, h // 2, TP:T], start=True, stop=True)
                    if h >= 2:
                        order.then(ins)
                pe.wait_ge(sem("spt_done"), 1)
                pe.wait_ge(sem("qp_done"), 1)
                pe.wait_ge(sem("st_in"), 16 * 9)
                for h in range(HA):
                    c = h * (HD + 1)
                    nc.tensor.matmul(acc[0:TS, 0, c:c + HD + 1], SPT[:, TS * h:TS * (h + 1)], va_tok[0:TS, NT, h, :],
                                     start=True, stop=True)
                for h in (0, 2, 1, 3):
                    p = par(h)
                    c = h * (HD + 1)
                    for b in range(NB):
                        ins = nc.tensor.matmul(acc[0:TS, 0, 512 + c:512 + c + HD + 1], QpA[p:p + HD, h // 2, b, :],
                                               s_cn[p:p + HD, b, h // 2, :], start=b == 0, stop=b == NB - 1)
                    if h == 2:
                        order.then(ins)
                ins.then_inc(sem("so_mm"), 1)
                for h in range(HA):
                    p = par(h)
                    ins = nc.tensor.matmul(acc[p:p + HD, 3, NB * (h // 2):NB * (h // 2 + 1)],
                                           rowc[:, R_SEL + P * h:R_SEL + P * h + HD], small[:, 2 * TS:], start=True, stop=True)
                ins.then_inc(sem("dc_mm"), 1)
                for h in range(HA):
                    p = par(h)
                    pe.wait_ge(sem("vb_done"), h + 1)
                    if h >= 1:
                        pe.wait_ge(sem("cn_done"), h)
                    for half in range(2):
                        ins = nc.tensor.matmul(acc[p:p + HD, 1, 512 * half:512 * half + 4 * (HD + 1)], kws[:, HD * h:HD * (h + 1)],
                                               Vb[:, 4 * half:4 * half + 4, :], start=True, stop=True)
                    ins.then_inc(sem("sst_mm"), 1)
                pe.wait_ge(sem("hn_done"), 1)
                for pr in range(2):
                    for i in range(NT + 1):
                        n = P if i < NT else TS
                        ins = nc.tensor.transpose(acc[:, pr, P * i:P * i + n],
                                                  hA[0:n, i, 2 * pr:2 * pr + 2, :].rearrange("p h d -> p (h d)"), ident[0:n, 0:n])
                    ins.then_inc(sem("ya_tr"), 1)

        units = []
        for i in range(NT):
            for j in range(2):
                units.append((i, [2 * g + j for g in range(3)]))
        for i in range(NT):
            for h in range(6, HEADS):
                units.append((i, [h]))
        segs, unit_segs, widths = [], [], []
        for u, (i, heads) in enumerate(units):
            off, mine = 0, []
            for h in heads:
                k0 = max(0, i - 1) if kind_of(h) == 1 else 0
                mine.append(len(segs))
                segs.append((u, i, h, k0, off))
                off += P * (i + 1 - k0)
            unit_segs.append(mine)
            widths.append(off)
        m3 = Map(after_kv)
        Sb = m3("Sb", [P, 2, 1280])
        PTs = m3("PTs", [P, 2, TP])
        mx = m3("mx", [P, 2])
        dn = m3("dn", [P, 2])
        TT = Map(raw_at)("TT", [P, HEADS, TP])
        NU = len(units)
        with nc.Block() as blk:
            @blk.sync
            def _(sp):
                sp.dma_start(TT[:, :, :], bass.AP(rev_d.tensor, 127, [[HEADS * REV - 1, P], [REV, HEADS], [1, TP]])
                             ).then_inc(sem("tt_in"), 16)

            @blk.tensor
            def _(pe):
                def scores(u):
                    for n in unit_segs[u]:
                        _, i, h, k0, off = segs[n]
                        if n >= 4:
                            pe.wait_ge(sem("s_used"), n - 3)
                        p, t = HD * (h % 2), 2 + h // 2
                        nc.tensor.matmul(acc[:, (n % 4) // 2, 512 * (n % 2):512 * (n % 2) + P * (i + 1 - k0)],
                                         qT[p:p + HD, t, P * i:P * (i + 1)], kT[p:p + HD, t, P * k0:P * (i + 1)],
                                         start=True, stop=True).then_inc(sem("s_mm"), 1)

                def turn_p(n):
                    u, i, h, k0, off = segs[n]
                    pe.wait_ge(sem("p_done"), u + 1)
                    if n >= 2:
                        pe.wait_ge(sem("pt_ev"), n - 1)
                    for k in range(i + 1 - k0):
                        ins = nc.tensor.transpose(acc[:, 2, 512 * (n % 2) + P * k:512 * (n % 2) + P * (k + 1)],
                                                  Sb[:, u % 2, off + P * k:off + P * (k + 1)], ident)
                    ins.then_inc(sem("pt_tr"), 1)

                def outputs(n):
                    u, i, h, k0, off = segs[n]
                    pe.wait_ge(sem("pt_ev"), n + 1)
                    if n >= 2:
                        pe.wait_ge(sem("o_ev"), n - 1)
                    p = HD * (h % 2)
                    for k in range(i + 1 - k0):
                        ins = nc.tensor.matmul(acc[p:p + HD, 3, 512 * (n % 2):512 * (n % 2) + P],
                                               v_tok[:, k0 + k, HD * h:HD * (h + 1)], PTs[:, n % 2, P * k:P * (k + 1)],
                                               start=k == 0, stop=k == i - k0)
                    ins.then_inc(sem("o_mm"), 1)

                scores(0)
                for u in range(NU):
                    if u + 1 < NU:
                        scores(u + 1)
                    for n in unit_segs[u]:
                        turn_p(n)
                        if n >= 1:
                            outputs(n - 1)
                outputs(len(segs) - 1)

            @blk.vector
            def _(dve):
                v = Steps(dve, sem("d3"))
                dve.wait_ge(sem("tt_in"), 16)

                def biased(u):
                    i, heads = units[u]
                    for n in unit_segs[u]:
                        _, i, h, k0, off = segs[n]
                        w = P * (i + 1 - k0)
                        dve.wait_ge(sem("s_mm"), n + 1)
                        if u >= 2 and n == unit_segs[u][0]:
                            dve.wait_ge(sem("pt_tr"), unit_segs[u - 2][-1] + 1)
                        c0 = P * (NT - 1 - i + k0)
                        nc.vector.tensor_tensor(Sb[:, u % 2, off:off + w], acc[:, (n % 4) // 2, 512 * (n % 2):512 * (n % 2) + w],
                                                TT[:, h, c0:c0 + w], ALU.add).then_inc(sem("s_used"), 1)
                    dve.wait_ge(sem("s_used"), unit_segs[u][-1] + 1)
                    if u >= 2:
                        dve.wait_ge(sem("e_done"), u - 1)
                    nc.vector.tensor_reduce(mx[:, u % 2:u % 2 + 1], Sb[:, u % 2, 0:widths[u]], AXX, ALU.max,
                                            negate=True).then_inc(sem("m_done"), 1)

                def normal(u):
                    dve.wait_ge(sem("e_done"), u + 1)
                    v.then(nc.vector.reciprocal(dn[:, u % 2:u % 2 + 1], dn[:, u % 2:u % 2 + 1]))
                    nc.vector.tensor_scalar(Sb[:, u % 2, 0:widths[u]], Sb[:, u % 2, 0:widths[u]], dn[:, u % 2:u % 2 + 1], None,
                                            ALU.mult).then_inc(sem("p_done"), 1)

                def collect(n):
                    _, i, h, k0, off = segs[n]
                    p = HD * (h % 2)
                    dve.wait_ge(sem("o_mm"), n + 1)
                    nc.vector.tensor_copy(qT[p:p + HD, 2 + h // 2, P * i:P * (i + 1)],
                                          acc[p:p + HD, 3, 512 * (n % 2):512 * (n % 2) + P]).then_inc(sem("o_ev"), 1)

                biased(0)
                for u in range(NU):
                    normal(u)
                    if u + 1 < NU:
                        biased(u + 1)
                    for n in unit_segs[u]:
                        if n >= 1:
                            collect(n - 1)
                collect(len(segs) - 1)

            @blk.scalar
            def _(act):
                def turned(n):
                    u, i, h, k0, off = segs[n]
                    act.wait_ge(sem("pt_tr"), n + 1)
                    if n >= 2:
                        act.wait_ge(sem("o_mm"), n - 1)
                    w = P * (i + 1 - k0)
                    nc.scalar.copy(PTs[:, n % 2, 0:w], acc[:, 2, 512 * (n % 2):512 * (n % 2) + w]).then_inc(sem("pt_ev"), 1)

                def exps(u):
                    act.wait_ge(sem("m_done"), u + 1)
                    if u >= 2:
                        act.wait_ge(sem("p_done"), u - 1)
                    nc.scalar.activation(Sb[:, u % 2, 0:widths[u]], Sb[:, u % 2, 0:widths[u]], ACT.Exp, bias=mx[:, u % 2:u % 2 + 1],
                                         accum_out=dn[:, u % 2:u % 2 + 1]).then_inc(sem("e_done"), 1)

                exps(0)
                for u in range(NU):
                    if u + 1 < NU:
                        exps(u + 1)
                    for n in unit_segs[u]:
                        turned(n)

        in_sq4 = Map(sq_at)
        kTn = in_sq4("kTn", [P, 6, TS])
        vn = in_sq4("vn", [TS, HEADS * HD])
        m4 = Map(after_q)
        KB = m4("KB", [P, 40, P])
        Vpg = m4("Vpg", [P, 16, 384])
        Qpad = m4("Qpad", [P, 6, NB, 2 * TS])
        Qs = m4("Qs", [P, 6, 2 * TS])
        oh4 = m4("oh4", [33, 4, REV])
        RBs = m4("RBs", [33, TB, HEADS, TS])
        KTs = m4("KTs", [P, 2, 256])
        S4 = m4("S4", [P, 3, 288])
        PT4 = Map(whi_at)("PT4", [P, 3, 3, P])
        mx4 = m4("mx4", [P, 4])
        dn4 = m4("dn4", [P, 4])
        rb4 = m4("rb4", [33, HEADS])
        VB = Map(after_q)("VB", [P, 40, P])
        Kpg = Map(raw_at)("Kpg", [P, 16, 384])
        B0 = (0, 8, 24)
        NC4 = (1, 2, 2, 2, 2, 2)

        def banks(lo, n):
            return acc[:, :, :].rearrange("p s (b n) -> p (s b) n", n=512)[:, lo:lo + n]

        ALLB = banks(0, 8)
        with nc.Block() as blk:
            @blk.sync
            def _(sp):
                sp.dma_start(oh4[:, :, :], X["oh"]).then_inc(sem("in4"), 16)
                sp.dma_start(rb4[0:32, :], I["rel_bias"]).then_inc(sem("in4"), 16)
                pages = [sp.value_load(I["page_table"][n // 2:n // 2 + 1, n % 2:n % 2 + 1], min_val=0, max_val=19)
                         for n in range(16)]
                sp.wait_ge(sem("new4"), 2)
                for g in range(3):
                    c = LW[g] // P
                    src = caches[g].rearrange("o b (c p) s h d -> p (o b c) s (h d)", p=P)
                    sp.dma_start(KB[:, B0[g]:B0[g] + NB * c, :], src[:, :, 0, :]).then_inc(sem(f"kb_in{g}"), 16)
                for n, page in enumerate(pages):
                    sp.dma_start(Kpg[:, n, :], I["cache_moba_k"][0, bass.ds(page, 1)].rearrange("o p h d -> p (o h d)")
                                 ).then_inc(sem("kp_in"), 16)
                for n, page in enumerate(pages):
                    sp.dma_start(Vpg[:, n, :], I["cache_moba_v"][0, bass.ds(page, 1)].rearrange("o p h d -> p (o h d)")
                                 ).then_inc(sem("vp_in"), 16)
                sp.wait_ge(sem("kt_ev"), 3 * NB)
                for g in range(3):
                    c = LW[g] // P
                    src = caches[g].rearrange("o b (c p) s h d -> p (o b c) s (h d)", p=P)
                    sp.dma_start(VB[:, B0[g]:B0[g] + NB * c, :], src[:, :, 1, :]).then_inc(sem("vb_in"), 16)

            @blk.gpsimd
            def _(pool):
                st = Steps(pool, sem("pool4"))
                pool.wait_ge(sem("new4"), 2)
                st.then(nc.gpsimd.memset(Qs[:, :, :], 0.0))
                st.then(nc.gpsimd.memset(Qpad[:, :, :, :], 0.0))
                st.then(nc.gpsimd.memset(RBs[:, :, :, :], 0.0))
                st.then(nc.gpsimd.memset(rb4[32:33, :], 1.0))

            @blk.vector
            def _(dve):
                v = Steps(dve, sem("d4"))
                nc.vector.tensor_copy(kTn[:, :, :], kT[:, 2:8, TP:T]).then_inc(sem("new4"), 1)
                nc.vector.tensor_copy(vn[:, :], v_tok[0:TS, NT, :]).then_inc(sem("new4"), 1)
                dve.wait_ge(sem("pool4"), 4)
                dve.wait_ge(sem("in4"), 32)
                for h in range(2):
                    p = HD * h
                    v.do(nc.vector.tensor_copy(Qs[p:p + HD, :, TS * h:TS * (h + 1)], qT[p:p + HD, 2:8, TP:T]))
                    for q in range(6):
                        at = Qpad[p:p + HD, q, 0, TS * h:TS * h + 1]
                        v.do(nc.vector.tensor_copy(
                            bass.AP(at.tensor, at.offset, [at.ap[0], [2 * TS + TB, NB], [1, TB]]),
                            qT[p:p + HD, 2 + q, TP:T].rearrange("p (b t) -> p b t", t=TB)))
                for t in range(TB):
                    v.do(nc.vector.tensor_copy(RBs[:, t, :, :].rearrange("p h (b t) -> p h b t", t=TB)[:, :, :, t],
                                               rb4[:, :].unsqueeze(2).broadcast_to([33, HEADS, NB])))
                v.sync()
                nc.vector.nop().then_inc(sem("q4"), 1)
                dve.wait_ge(sem("qk4"), 6 * NB)
                v.do(nc.vector.tensor_copy(S4[:, :, 0:256], ALLB[:, 0:3, 0:256]))
                v.then(nc.vector.tensor_tensor(S4[:, :, 256:288], ALLB[:, 3, 0:96].rearrange("p (g n) -> p g n", n=TS),
                                               con[:, C_NEW:C_NEW + TS].unsqueeze(1).broadcast_to([P, 3, TS]), ALU.add))
                v.then(nc.vector.tensor_reduce(mx4[:, 0:3], S4[:, :, :], AXX, ALU.max))
                v.then(nc.vector.tensor_reduce(mx4[0:HD, 3:4], mx4[0:HD, 0:3], AXX, ALU.max))
                v.then(nc.vector.tensor_copy(mx4[0:HD, 0:3], mx4[0:HD, 3:4].broadcast_to([HD, 3])))
                v.then(nc.vector.tensor_scalar(mx4[:, 0:3], mx4[:, 0:3], -1.0, None, ALU.mult))
                nc.vector.nop().then_inc(sem("mx4"), 1)
                dve.wait_ge(sem("e4"), 3)
                v.then(nc.vector.tensor_reduce(dn4[0:HD, 3:4], dn4[0:HD, 0:3], AXX, ALU.add))
                v.then(nc.vector.tensor_copy(dn4[0:HD, 0:3], dn4[0:HD, 3:4].broadcast_to([HD, 3])))
                v.then(nc.vector.reciprocal(dn4[:, 0:3], dn4[:, 0:3]))
                nc.vector.tensor_tensor(S4[:, :, :], S4[:, :, :], dn4[:, 0:3].unsqueeze(2).broadcast_to([P, 3, 288]),
                                        ALU.mult).then_inc(sem("p4"), 1)
                dve.wait_ge(sem("o4"), 6)
                for h in range(2):
                    p = HD * h
                    nc.vector.tensor_copy(qT[p:p + HD, 2:8, TP:T],
                                          ALLB[p:p + HD, 7, 0:384].rearrange("p (q n) -> p q n", n=2 * TS)[:, :, TS * h:TS * (h + 1)]
                                          ).then_inc(sem("y4"), 1)

            @blk.scalar
            def _(act):
                for n in range(6 * NB):
                    act.wait_ge(sem("kt_tr"), n + 1)
                    if n >= 2:
                        act.wait_ge(sem("qk4"), n - 1)
                    w = P * NC4[n // NB]
                    nc.scalar.copy(KTs[:, n % 2, 0:w], ALLB[:, 4 + n % 2, 0:w]).then_inc(sem("kt_ev"), 1)
                act.wait_ge(sem("mx4"), 1)
                for g in range(3):
                    nc.scalar.activation(S4[:, g, :], S4[:, g, :], ACT.Exp, bias=mx4[:, g:g + 1],
                                         accum_out=dn4[:, g:g + 1]).then_inc(sem("e4"), 1)
                act.wait_ge(sem("pt4"), 1)
                nc.scalar.copy(PT4[:, :, 0:2, :], ALLB[:, 4:7, 0:256].rearrange("p g (c n) -> p g c n", n=P)).then_inc(sem("pt4_ev"), 1)
                nc.scalar.copy(PT4[0:TS, :, 2, :], ALLB[0:TS, 4:7, 256:384]).then_inc(sem("pt4_ev"), 1)

            @blk.tensor
            def _(pe):
                pe.wait_ge(sem("q4"), 1)

                def turn_k(n):
                    q, b = divmod(n, NB)
                    if n >= 2:
                        pe.wait_ge(sem("kt_ev"), n - 1)
                    if q < 3:
                        pe.wait_ge(sem(f"kb_in{q}"), 16)
                    else:
                        pe.wait_ge(sem("kp_in"), 256)
                    for c in range(NC4[q]):
                        src = KB[:, B0[q] + NC4[q] * b + c, :] if q < 3 else Kpg[:, 2 * b + c, P * (q - 3):P * (q - 2)]
                        ins = nc.tensor.transpose(ALLB[:, 4 + n % 2, P * c:P * (c + 1)], src, ident)
                    ins.then_inc(sem("kt_tr"), 1)

                turn_k(0)
                for q in range(6):
                    g, lo = q % 3, HD * (q // 3)
                    kind = 1 + q if q < 3 else 0
                    u0 = TP - 1 - P * NC4[q]
                    S = ALLB[lo:lo + HD, g, 0:256]
                    new = ALLB[lo:lo + HD, 3, TS * g:TS * (g + 1)]
                    for t in range(TB):
                        rbt = RBs[:, t, 2 * q:2 * q + 2, :].rearrange("p h n -> p (h n)")
                        nc.tensor.matmul(S, rbt, oh4[:, kind, u0 - t:u0 - t + 256], start=t == 0, stop=False)
                    for t in range(TB):
                        rbt = RBs[:, t, 2 * q:2 * q + 2, :].rearrange("p h n -> p (h n)")
                        nc.tensor.matmul(new.rearrange("p (b t) -> p b t", t=TB), rbt,
                                         oh4[:, kind, TP - 1 - t:TP - 1 - t + TB].unsqueeze(1).broadcast_to([33, NB, TB]),
                                         start=t == 0, stop=False)
                    nc.tensor.matmul(new, Qs[:, q, :], kTn[:, q, :], start=False, stop=True)
                    for b in range(NB):
                        n = NB * q + b
                        if n + 1 < 6 * NB:
                            turn_k(n + 1)
                        pe.wait_ge(sem("kt_ev"), n + 1)
                        w = P * NC4[q]
                        ins = nc.tensor.matmul(ALLB[lo:lo + HD, g, 0:w], Qpad[:, q, b, :], KTs[:, n % 2, 0:w],
                                               start=False, stop=b == NB - 1)
                        ins.then_inc(sem("qk4"), 1)
                pe.wait_ge(sem("p4"), 1)
                for g in range(3):
                    for c in range(2):
                        nc.tensor.transpose(ALLB[:, 4 + g, P * c:P * (c + 1)], S4[:, g, P * c:P * (c + 1)], ident)
                    ins = nc.tensor.transpose(ALLB[0:TS, 4 + g, 256:384], S4[:, g, 256:288], ident)
                ins.then_inc(sem("pt4"), 1)
                pe.wait_ge(sem("pt4_ev"), 2)
                pe.wait_ge(sem("vb_in"), 48)
                pe.wait_ge(sem("vp_in"), 256)
                for q in range(6):
                    g, lo = q % 3, HD * (q // 3)
                    out = ALLB[:, 7, 2 * TS * q:2 * TS * (q + 1)]
                    nc.tensor.matmul(out, vn[:, P * q:P * (q + 1)], PT4[0:TS, g, 2, lo:lo + HD], start=True, stop=False)
                    for b in range(NB):
                        for c in range(NC4[q]):
                            vt = VB[:, B0[q] + NC4[q] * b + c, :] if q < 3 else Vpg[:, 2 * b + c, P * (q - 3):P * (q - 2)]
                            ins = nc.tensor.matmul(out.rearrange("p (h n) -> p h n", h=2)[:, :, TB * b:TB * (b + 1)], vt,
                                                   PT4[:, g, c, lo:lo + HD].rearrange("p (h n) -> p h n", h=2)[:, :, TB * b:TB * (b + 1)],
                                                   start=False, stop=b == NB - 1 and c == NC4[q] - 1)
                    ins.then_inc(sem("o4"), 1)

        m5 = Map(after_q)
        y_hi = m5("y_hi", [P, 8, T], F32R)
        y_lo = m5("y_lo", [P, 8, T], F32R)
        gsig = m5("gsig", [P, 6, T])
        mg_hi = m5("mg_hi", [P, KD, T], F32R)
        mt = m5("mt", [P, 2, T])
        mg_lo = Map(region)("mg_lo", [P, KD, T], F32R)
        m7 = Map(region)
        s_hi = m7("s_hi", [P, KF, T], F32R)
        s_lo = m7("s_lo", [P, KF, T], F32R)
        sg = m7("sg", [P, 2, T])
        gx = sq
        o_st = Map(region)("o_st", [P, NT + 1, D])
        rt = Map(region + 4 * (NT + 1) * D)("rt", [P, 8])

        acc_mm, acc_ev = sem("acc_mm"), sem("acc_ev")
        def merge_accs(w):
            j, r = divmod(w - n_proj, 8)
            return (12 * j + r, 1) if r < 6 else (12 * j + 6 + 3 * (r - 6), 3)

        A_WOUT = 12 * 4
        A_GU = A_WOUT + 8
        A_DN = A_GU + 44
        A_END = A_DN + 8
        with nc.Block() as blk:
            @blk.sync
            def _(sp):
                load_weights(sp, load_range(n_proj, n_all)[0], len(loads))
                for i in range(NT + 1):
                    sp.wait_ge(sem("y_out_ready"), i + 1)
                    if i < NT:
                        sp.dma_start(o_yp[0, P * i:P * (i + 1), :], o_st[:, i, :]).then_inc(sem("y_stored"), 16)
                    else:
                        sp.dma_start(o_ys.rearrange("b t d -> (b t) d"), o_st[0:TS, i, :]).then_inc(sem("y_stored"), 16)
                sp.wait_ge(sem("y_stored"), 16 * (NT + 1))

            @blk.tensor
            def _(pe):
                def start_acc(a):
                    if a >= 4:
                        pe.wait_ge(acc_ev, a - 3)

                for w in range(n_proj, n_merge):
                    pe.wait_ge(w_lo_done, w + 1)
                    a, n = merge_accs(w)
                    if n == 1:
                        start_acc(a)
                        ins = products(pe, w, a % 4, h_hi, h_lo, 0)
                        ins.then_inc(w_used, 1)
                    else:
                        pe.wait_ge(sem("y_lo_done"), 8)
                        for c, (k, m) in enumerate(((0, 2), (2, 3), (5, 3))):
                            start_acc(a + c)
                            ins = products(pe, w, (a + c) % 4, y_hi, y_lo, k, kts=m, k_from=k)
                            ins.then_inc(sem("br_mm"), 1)
                        pe.wait_ge(sem("br_mm"), 3 * (2 * ((w - n_proj) // 8) + (w - n_proj) % 8 - 5))
                        nc.tensor.nop().then_inc(w_used, 1)
                for w in range(n_merge, n_wout):
                    pe.wait_ge(w_lo_done, w + 1)
                    pe.wait_ge(sem("mg_lo_done"), KD)
                    start_acc(A_WOUT + w - n_merge)
                    products(pe, w, (w - n_merge) % 4, mg_hi, mg_lo, 0).then_inc(w_used, 1)
                for w in range(n_wout, n_gu):
                    pe.wait_ge(w_lo_done, w + 1)
                    a = A_GU + w - n_wout
                    start_acc(a)
                    pe.wait_ge(sem("h2_lo_done"), KD)
                    products(pe, w, a % 4, h_hi, h_lo, 0).then_inc(w_used, 1)
                    if w == n_wout:
                        pe.wait_ge(sem("ssq2_done"), KD)
                        pe.wait_ge(acc_ev, A_GU)
                        for half in range(2):
                            ins = nc.tensor.matmul(acc[:, 3, 512 * half:512 * half + H2], ones[:, :],
                                                   ssq[:, H2 * half:H2 * (half + 1)], start=True, stop=True)
                        ins.then_inc(sem("ssq_mm"), 1)
                        pe.wait_ge(sem("std_done"), 2)
                for w in range(n_gu, n_all):
                    pe.wait_ge(w_lo_done, w + 1)
                    j, r = divmod(w - n_gu, 6)
                    c, n = divmod(r, 2)
                    a = A_DN + 2 * j + n
                    if c == 0:
                        start_acc(a)
                    k0, k1 = DOWN[c]
                    pe.wait_ge(sem("s_lo_done"), k1)
                    products(pe, w, a % 4, s_hi, s_lo, k0, first=c == 0, last=c == 2).then_inc(w_used, 1)
                pe.wait_ge(sem("xg_done"), KD)
                pe.wait_ge(sem("ssq3_done"), KD)
                for i in range(NT + 1):
                    n = P if i < NT else TS
                    ins = nc.tensor.matmul(acc[0:n, 2, i:i + 1], ssq[:, P * i:P * i + n], ones[:, 0:1], start=True, stop=True)
                ins.then_inc(sem("rt_mm"), 1)
                for i in range(NT + 1):
                    n = P if i < NT else TS
                    if i >= 2:
                        pe.wait_ge(sem("y_out_ready"), i - 1)
                    for k in range(KD):
                        ins = nc.tensor.transpose(acc[0:n, i % 2, P * k:P * (k + 1)], xT[:, k, P * i:P * i + n], ident)
                    ins.then_inc(sem("y_tr"), 1)

            @blk.scalar
            def _(act):
                for k in range(8):
                    nc.scalar.copy(y_hi[:, k, :], qT[:, k, :]).then_inc(sem("y_hi_done"), 1)
                split_hi(act, n_proj)
                for w in range(n_proj, n_all):
                    if w + 1 < n_all:
                        split_hi(act, w + 1)
                    if w < n_merge:
                        j, r = divmod(w - n_proj, 8)
                        if r < 6:
                            act.wait_ge(sem("g_pre"), 6 * j + r + 1)
                            nc.scalar.activation(gsig[:, r, :], gsig[:, r, :], ACT.Sigmoid).then_inc(sem("g_sig"), 1)
                        else:
                            k = 2 * j + r - 6
                            act.wait_ge(sem("mg_done"), k + 1)
                            nc.scalar.copy(mg_hi[:, k, :], mt[:, 0, :]).then_inc(sem("mg_hi_done"), 1)
                    elif w < n_wout:
                        k = w - n_merge
                        act.wait_ge(acc_ev, A_WOUT + k + 1)
                        nc.scalar.activation(h_hi[:, k, :], xT[:, k, :], ACT.Copy, scale=vecs[:, 8 + k:9 + k]).then_inc(sem("h2_hi_done"), 1)
                        if k >= 2:
                            act.wait_ge(sem("ssq2_done"), k - 1)
                        nc.scalar.activation(sq[:, k % 2, :], xT[:, k, :], ACT.Square).then_inc(sem("sq2_done"), 1)
                    elif w < n_gu:
                        j, r = divmod(w - n_wout, 4)
                        if w == n_wout:
                            act.wait_ge(sem("ssq_mm"), 2)
                            nc.scalar.activation(two(rstd[:, :]), halves(3), ACT.Sqrt, bias=eps[:, :],
                                                 scale=1.0 / D).then_inc(sem("std_done"), 1)
                        if r < 2:
                            act.wait_ge(sem("gx_done"), 2 * j + r + 1)
                            nc.scalar.activation(sg[:, r, :], gx[:, r, :], ACT.Sigmoid).then_inc(sem("sg_done"), 1)
                        else:
                            k = 2 * j + r - 2
                            act.wait_ge(sem("s_done"), k + 1)
                            nc.scalar.copy(s_hi[:, k, :], gx[:, r - 2, :]).then_inc(sem("s_hi_done"), 1)
                    else:
                        j, r = divmod(w - n_gu, 6)
                        if r >= 4:
                            k = 2 * j + r - 4
                            act.wait_ge(acc_ev, A_DN + k + 1)
                            if k >= 2:
                                act.wait_ge(sem("ssq3_done"), k - 1)
                            nc.scalar.activation(sq[:, k % 2, :], xT[:, k, :], ACT.Square).then_inc(sem("sq3_done"), 1)
                            nc.scalar.activation(xT[:, k, :], xT[:, k, :], ACT.Copy, scale=vecs[:, 16 + k:17 + k]).then_inc(sem("xg_done"), 1)
                act.wait_ge(sem("rt_mm"), 1)
                act.wait_ge(sem("rt_set"), 1)
                nc.scalar.activation(rt[:, 0:NT], acc[:, 2, 0:NT], ACT.Sqrt, bias=eps[:, :], scale=1.0 / D).then_inc(sem("rt_std"), 1)
                nc.scalar.activation(rt[0:TS, NT:NT + 1], acc[0:TS, 2, NT:NT + 1], ACT.Sqrt, bias=eps[0:TS, :],
                                     scale=1.0 / D).then_inc(sem("rt_std"), 1)
                act.wait_ge(sem("rt_done"), 1)
                for i in range(NT + 1):
                    n = P if i < NT else TS
                    act.wait_ge(sem("y_tr"), i + 1)
                    nc.scalar.activation(o_st[0:n, i, :], acc[0:n, i % 2, :], ACT.Copy, scale=rt[0:n, i:i + 1]).then_inc(sem("y_out_ready"), 1)

            @blk.vector
            def _(dve):
                v = Steps(dve, sem("d5"))
                for k in range(8):
                    dve.wait_ge(sem("y_hi_done"), k + 1)
                    nc.vector.tensor_tensor(y_lo[:, k, :], qT[:, k, :], y_hi[:, k, :].bitcast(F32), ALU.subtract).then_inc(sem("y_lo_done"), 1)
                split_lo(dve, n_proj)
                for w in range(n_proj, n_all):
                    if w + 1 < n_all:
                        split_lo(dve, w + 1)
                    if w < n_merge:
                        j, r = divmod(w - n_proj, 8)
                        a, n = merge_accs(w)
                        if r < 6:
                            if j >= 1:
                                v.sync()
                            dve.wait_ge(w_used, w + 1)
                            v.then(nc.vector.tensor_tensor(two(gsig[:, r, :]), halves(a % 4), two(rstd[:, :]), ALU.mult))
                            nc.vector.nop().then_inc(acc_ev, 1)
                            nc.vector.nop().then_inc(sem("g_pre"), 1)
                            continue
                        k = 2 * j + r - 6
                        if k >= 1:
                            dve.wait_ge(sem("mg_hi_done"), k)
                        dve.wait_ge(sem("g_sig"), 6 * j + 6)
                        for c in range(3):
                            dve.wait_ge(sem("br_mm"), 3 * k + c + 1)
                            v.then(nc.vector.tensor_tensor(two(mt[:, min(c, 1), :]), halves((a + c) % 4),
                                                           two(gsig[:, 2 * c + r - 6, :]), ALU.mult))
                            nc.vector.nop().then_inc(acc_ev, 1)
                            if c:
                                v.then(nc.vector.tensor_tensor(mt[:, 0, :], mt[:, 0, :], mt[:, 1, :], ALU.add))
                        nc.vector.nop().then_inc(sem("mg_done"), 1)
                        dve.wait_ge(sem("mg_hi_done"), k + 1)
                        v.do(nc.vector.tensor_tensor(mg_lo[:, k, :], mt[:, 0, :], mg_hi[:, k, :].bitcast(F32), ALU.subtract))
                        v.sync()
                        nc.vector.nop().then_inc(sem("mg_lo_done"), 1)
                    elif w < n_wout:
                        k = w - n_merge
                        dve.wait_ge(w_used, w + 1)
                        v.then(nc.vector.tensor_tensor(two(xT[:, k, :]), halves(k % 4), two(xT[:, k, :]), ALU.add))
                        nc.vector.nop().then_inc(acc_ev, 1)
                        dve.wait_ge(sem("h2_hi_done"), k + 1)
                        nc.vector.scalar_tensor_tensor(h_lo[:, k, :], xT[:, k, :], vecs[:, 8 + k:9 + k],
                                                       h_hi[:, k, :].bitcast(F32), ALU.mult, ALU.subtract).then_inc(sem("h2_lo_done"), 1)
                        dve.wait_ge(sem("sq2_done"), k + 1)
                        if k == 0:
                            nc.vector.tensor_copy(ssq[:, :], sq[:, 0, :]).then_inc(sem("ssq2_done"), 1)
                        else:
                            dve.wait_ge(sem("ssq2_done"), k)
                            nc.vector.tensor_tensor(ssq[:, :], ssq[:, :], sq[:, k % 2, :], ALU.add).then_inc(sem("ssq2_done"), 1)
                    elif w < n_gu:
                        j, r = divmod(w - n_wout, 4)
                        a = A_GU + w - n_wout
                        if w == n_wout:
                            dve.wait_ge(sem("std_done"), 2)
                            v.then(nc.vector.reciprocal(rstd[:, :], rstd[:, :]))
                        dve.wait_ge(w_used, w + 1)
                        if r < 2:
                            if j >= 1:
                                dve.wait_ge(sem("s_lo_done"), 2 * (j - 1) + r + 1)
                            v.then(nc.vector.tensor_tensor(two(gx[:, r, :]), halves(a % 4), two(rstd[:, :]), ALU.mult))
                            nc.vector.nop().then_inc(acc_ev, 1)
                            nc.vector.nop().then_inc(sem("gx_done"), 1)
                        else:
                            k, b = 2 * j + r - 2, r - 2
                            dve.wait_ge(sem("sg_done"), k + 1)
                            v.then(nc.vector.tensor_tensor(gx[:, b, :], gx[:, b, :], sg[:, b, :], ALU.mult))
                            v.then(nc.vector.tensor_tensor(two(sg[:, b, :]), halves(a % 4), two(rstd[:, :]), ALU.mult))
                            nc.vector.nop().then_inc(acc_ev, 1)
                            v.then(nc.vector.tensor_tensor(gx[:, b, :], gx[:, b, :], sg[:, b, :], ALU.mult))
                            nc.vector.nop().then_inc(sem("s_done"), 1)
                            dve.wait_ge(sem("s_hi_done"), k + 1)
                            nc.vector.tensor_tensor(s_lo[:, k, :], gx[:, b, :], s_hi[:, k, :].bitcast(F32), ALU.subtract).then_inc(sem("s_lo_done"), 1)
                    else:
                        j, r = divmod(w - n_gu, 6)
                        if r < 4:
                            continue
                        k = 2 * j + r - 4
                        dve.wait_ge(w_used, w + 1)
                        v.then(nc.vector.tensor_tensor(two(xT[:, k, :]), halves((A_DN + k) % 4), two(xT[:, k, :]), ALU.add))
                        nc.vector.nop().then_inc(acc_ev, 1)
                        dve.wait_ge(sem("sq3_done"), k + 1)
                        if k == 0:
                            nc.vector.tensor_copy(ssq[:, :], sq[:, 0, :]).then_inc(sem("ssq3_done"), 1)
                        else:
                            dve.wait_ge(sem("ssq3_done"), k)
                            nc.vector.tensor_tensor(ssq[:, :], ssq[:, :], sq[:, k % 2, :], ALU.add).then_inc(sem("ssq3_done"), 1)
                dve.wait_ge(w_used, n_all)
                nc.vector.memset(rt[:, :], 1.0).then_inc(sem("rt_set"), 1)
                dve.wait_ge(sem("rt_std"), 2)
                nc.vector.reciprocal(rt[:, :], rt[:, :]).then_inc(sem("rt_done"), 1)

    return nc


OUT_SHAPES = [
    (1, TP, D), (NB, TB, D), (1, 1, HA, HD, HD), (1, 1, HA, HD), (1, 1, HA),
    (1, NB, HA, HD, HD), (1, NB, HA, HD), (1, NB, HA),
    (1, 1, 128, 2, 2, HD), (1, 1, 512, 2, 2, HD), (1, 1, 512, 2, 2, HD),
    (1, NB, 128, 2, 2, HD), (1, NB, 256, 2, 2, HD), (1, NB, 256, 2, 2, HD),
    (1, 1, TP, 6, HD), (1, 1, TP, 6, HD), (1, NB, TB, 6, HD), (1, NB, TB, 6, HD)]


def kernel(**inputs):
    import concourse.bacc as bacc
    from concourse.bass_utils import run_bass_kernel_spmd

    nc = bacc.Bacc("TRN2", target_bir_lowering=False, num_devices=1)
    arrays = {name: np.ascontiguousarray(a) for name, a in inputs.items()}
    arrays.update(con=wide_constants(), rowc=row_constants(), oh=bias_selectors())
    aps = {name: nc.dram_tensor("in_" + name, a.shape, mybir.dt.from_np(a.dtype), kind="ExternalInput").ap()
           for name, a in arrays.items()}
    outs = [nc.dram_tensor(f"out_{i}", shape, F32, kind="ExternalOutput").ap()
            for i, shape in enumerate(OUT_SHAPES)]
    aps["rev"] = nc.dram_tensor("rev", (P, HEADS * REV), F32, kind="Internal").ap()
    build(nc, aps, outs, aps)
    got = run_bass_kernel_spmd(nc, [{"in_" + n: a for n, a in arrays.items()}], core_ids=[0]).results[0]
    return tuple(got[f"out_{i}"] for i in range(len(OUT_SHAPES)))
```

```python
from contextlib import ExitStack

import numpy as np

import concourse.bass as bass
from concourse import mybir

ALU = mybir.AluOpType
ACT = mybir.ActivationFunctionType
AXX = mybir.AxisListType.X
F32 = mybir.dt.float32
F32R = mybir.dt.float32r

P = 128
D = 1024
KD = D // P
TP, NB, TB = 512, 8, 4
TS = NB * TB
T = TP + TS
H2 = T // 2
NT = TP // P
HD = 64
HA = 4
D_FF = 2816
KF = D_FF // P
N_QKV = 1032
N_GATE = 3336
REV = 640
NEG = -1e30
EPS = 1e-6
SCALE = HD ** -0.5
HEADS = 12


def kind_of(head):
    return 1 + head // 2 if head < 6 else 0


def rel_bucket(dist):
    dist = np.maximum(dist, 0)
    ratio = np.log(np.maximum(dist, 1).astype(np.float64) / 16) / np.log(2048 / 16)
    large = np.minimum(16 + (ratio * 16).astype(np.int64), 31)
    return np.where(dist < 16, dist, large)


def bias_selectors():
    dist = TP - 1 - np.arange(REV)
    out = np.zeros((33, 4, REV), np.float32)
    for kind in range(4):
        ok = dist >= 0
        if kind:
            win, dil = ((128, 1), (512, 4), (2048, 16))[kind - 1]
            ok = ok & (dist <= win) & (dist % dil == 0)
        out[rel_bucket(dist), kind, np.arange(REV)] = ok
        out[32, kind] = np.where(ok, 0.0, NEG)
    return out


C_ID, C_CM, C_NEW, C_SM, C_BM = 0, 128, 256, 288, 320
C_W = 328
R_SEL, R_W = 0, HA * P


def wide_constants():
    out = np.zeros((P, C_W), np.float32)
    r = np.arange(P)
    out[:, C_ID:C_ID + P] = np.eye(P)
    out[:, C_CM:C_CM + P] = np.where(r[None, :] >= r[:, None], 0.0, NEG)
    s = np.arange(TS)
    out[:, C_NEW:C_NEW + TS] = np.where((r[:, None] % TS) // TB == s[None, :] // TB, 0.0, NEG)
    same = (s[:, None] // TB == s[None, :] // TB) & (s[None, :] >= s[:, None])
    out[:TS, C_SM:C_SM + TS] = np.where(same, 0.0, NEG)
    out[:TS, C_BM:C_BM + NB] = s[:, None] // TB == np.arange(NB)[None, :]
    return out


def row_constants():
    out = np.zeros((HA, R_W), np.float32)
    for h in range(HA):
        out[h, R_SEL + P * h:R_SEL + P * (h + 1)] = -1.0
    return out


def scan_constants():
    out = np.zeros((HA, 2, T), np.float32)
    starts = np.concatenate([[0], TP + TB * np.arange(NB)])
    out[:, 0] = 1.0
    out[:, 0, starts] = 0.0
    out[:, 1, starts] = NEG
    return out


class Steps:

    def __init__(self, eng, sem):
        self.eng, self.sem, self.n = eng, sem, 0

    def do(self, ins):
        ins.then_inc(self.sem, 1)
        self.n += 1
        return self.n

    def sync(self):
        self.eng.wait_ge(self.sem, self.n)

    def then(self, ins):
        self.do(ins)
        self.sync()


class Side:

    END = 1e9

    def __init__(self, *programs):
        self.programs = [[next(p, self.END), p] for p in programs]

    def until(self, time):
        while True:
            first = min(self.programs, key=lambda p: p[0])
            if first[0] > time:
                return
            first[0] = next(first[1], self.END)


def build(nc, I, O, X):
    with ExitStack() as ctx:
        low = nc.sbuf_base
        low += -low % 64
        top = nc.sbuf_top
        ctx.enter_context(nc.sbuf_tensor("whole", [P, (top - low) // 4 - 16], F32))
        sems = {}

        def sem(name):
            if name not in sems:
                sems[name] = ctx.enter_context(nc.semaphore(name))
            return sems[name]

        class Map:

            def __init__(self, at, size=None):
                self.at = at
                self.end = top - 64 if size is None else at + size

            def __call__(self, name, shape, dt=F32):
                n = 4 * int(np.prod(shape[1:]))
                assert self.at + n <= self.end, (name, self.at, n, self.end)
                t = nc.alloc_sbuf_tensor_at(name, shape, dt, offset=self.at)
                self.at += n + (-n % 64)
                return t

        keep = Map(low)
        con = keep("con", [P, C_W])
        ident = con[:, C_ID:C_ID + P]
        rowc = keep("rowc", [HA, R_W])
        vecs = keep("vecs", [P, 26])
        ones = keep("ones", [P, P])
        eps = keep("eps", [P, 1])
        one = keep("one", [P, 1])
        rstd = keep("rstd", [P, T])
        ssq = keep("ssq", [P, T])
        xT = keep("xT", [P, KD, T])
        h_hi = keep("h_hi", [P, KD, T], F32R)
        h_lo = keep("h_lo", [P, KD, T], F32R)
        raw = keep("raw", [P, 3, 2048])
        w_hi = keep("w_hi", [P, 2, 1024], F32R)
        w_lo = keep("w_lo", [P, 2, 1024], F32R)
        sq_at = keep.at
        sq = keep("sq", [P, 2, T])
        region = keep.at

        TB4 = 4 * T
        a_q = region
        a_g0 = a_q + 8 * TB4
        a_k = a_g0 + 13824
        a_v = a_k + 8 * TB4
        a_a = a_v + 15360
        a_b = a_a + 14720
        a_s = a_b + 12288
        qT = Map(a_q)("qT", [P, 8, T])
        m = Map(a_g0, 13824)
        i_row, f_row = m("i_row", [HA, T]), m("f_row", [HA, T])
        v_st = m("v_st", [P, 2, T])
        k_st = m("k_st", [P, 2, NT + 1, P])
        gs = [Map(a_g0)("gs0", [P, 6, T]), Map(a_k)("gs1", [P, 6, T])]
        kT = Map(a_k)("kT", [P, 8, T])
        v_tok = Map(a_v)("v_tok", [P, NT + 1, HEADS * HD])
        m = Map(a_a, 14720)
        oaT = m("oaT", [P, 2, T])
        va_tok = m("va_tok", [P, NT + 1, HA, HD + 1])
        ka_tok = m("ka_tok", [P, NT + 1, HA * HD])
        TTb = Map(a_b)("TTb", [P, 6, TP])
        TTc = Map(a_a)("TTc", [P, 6, TP])
        m = Map(a_s)
        Sb = m("Sb", [P, 2, 1280])
        Sc = Map(a_s)("Sc", [P, 5, TP])
        PTs = m("PTs", [P, 2, TP])
        mx = m("mx", [P, 4])
        dn = m("dn", [P, 4])
        m = Map(a_a)
        x_tok = m("x_tok", [P, NT + 1, D])
        xg = m("xg", [P, 2, KD, P])
        xsq = m("xsq", [P, 2, KD, P])
        vrow = m("vrow", [26, P])
        m = Map(a_v, 15360)
        oh = m("oh", [33, 4, REV])
        rb = m("rb", [33, HEADS])
        tab = Map(a_k + 2 * TB4, 6 * TB4)("tab", [6, 4, REV])
        m = Map(a_v, 15360)
        G = m("G", [P, HA, TP])
        W = m("W", [P, 2, TP])
        kw = m("kw", [P, NT, HD])
        oA = m("oA", [TS, HA * (HD + 1)])
        m = Map(a_b, 12288)
        rA, b_row, g_row = (m(n, [HA, T]) for n in ("rA", "b_row", "g_row"))
        PT = m("PT", [P, 1280])
        rB = f_row
        m = Map(a_s)
        m_row = m("m_row", [HA, T])
        hA = m("hA", [P, NT + 1, HA, HD])
        C0n = m("C0n", [P, NB, 2, HD + 1])
        QpA = m("QpA", [P, 2, NB, TS])
        tails = m("tails", [HA, 2 * TS + NB])
        m0_row = m("m0_row", [HA, NB])
        by_tok = m("by_tok", [P, 48])
        e_m = m("e_m", [P, 20])
        ws = m("ws", [P, 4 * NT])
        den = m("den", [P, 8])
        rs = m("rs", [P, (NT + 1) * HA])
        dcy = m("dcy", [P, 2, NB])
        st_o = m("st_o", [HD, 2, HD + 1])
        bif = m("bif", [HA, 2])
        m = Map(a_q + 5 * TB4, 3 * TB4)
        scan = m("scan", [HA, 2, T])
        Vb = m("Vb", [TS, NB, HD + 1])
        m = Map(a_k + 5 * TB4, 3 * TB4)
        kws = m("kws", [TS, HA * HD])
        hsq = m("hsq", [P, (NT + 1) * HA, HD])
        OH0, OHN = 252, 264
        oh4 = Map(sq_at)("oh4", [33, 4, OHN])
        m = Map(a_b, 12288)
        RBs = m("RBs", [33, TB, HEADS, TS])
        kTn = m("kTn", [P, 6, TS])
        vn = m("vn", [TS, HEADS * HD])
        Qs = m("Qs", [P, 6, 2 * TS])
        rb4 = m("rb4", [33, HEADS])
        PT4 = Map(a_b, 6144)("PT4", [P, 3, 3, P])
        ring = [Map(a_v)("ring0", [P, 16, P]), Map(a_v + 8192)("ring1", [P, 16, P]),
                Map(a_v + 16384)("ring2", [P, 16, P]), Map(a_s)("ring3", [P, 16, P])]
        Qpad = Map(a_k + 6 * TB4, 2 * TB4)("Qpad", [P, 2, NB, 2 * TS])
        KTs = Map(a_s + 8192, 2048)("KTs", [P, 2, 256])
        S4 = Map(a_s + 10240, 4096)("S4", [P, 3, 288])
        mx4 = Map(a_s + 14464)("mx4", [P, 4])
        dn4 = Map(a_s + 14528)("dn4", [P, 4])
        m = Map(a_v)
        y_hi, y_lo = (m(n, [P, 8, T], F32R) for n in ("y_hi", "y_lo"))
        mg_hi = m("mg_hi", [P, KD, T], F32R)
        mt = m("mt", [P, 2, T])
        mg_lo = Map(a_q)("mg_lo", [P, KD, T], F32R)
        m = Map(region)
        s_hi, s_lo = (m(n, [P, KF, T], F32R) for n in ("s_hi", "s_lo"))
        sg = m("sg", [P, 2, T])
        gx = sq
        o_st = Map(region)("o_st", [P, NT + 1, D])
        rt = Map(region + 4 * (NT + 1) * D)("rt", [P, 8])

        acc = ctx.enter_context(nc.psum_tensor("acc", [P, 8, 512], F32))

        def two(ap, half):
            return ap[:, H2 * half:H2 * (half + 1)]

        w_in, w_gu, w_dn, w_out = I["w_in"][0], I["w_gate_up"][0], I["w_down"][0], I["w_out"][0]

        def rows(w, k0, k1, c0, n):
            return w[k0 * P:k1 * P, c0:c0 + n].rearrange("(k p) n -> p k n", p=P)

        loads = []
        blocks = []

        def add_load(parts, kts):
            loads.append((parts, 2 * P))
            blocks.extend((len(loads) - 1, kts, 2 * P, j * P) for j in range(2))

        loads.append(([(0, 0, rows(w_in, 0, KD, 1024, 32)), (0, 32, rows(w_in, 0, KD, 1028, 96))], P))
        blocks.append((0, KD, P, 0))
        for c in list(range(0, 1024, 256)) + list(range(N_QKV, N_GATE, 256)):
            add_load([(0, 0, rows(w_in, 0, KD, c, 256))], KD)
        n_proj = len(blocks)

        info = {}

        def gates(j):
            for g in range(3):
                for n in range(2):
                    info[len(blocks) + n] = ("gate", j, 2 * g + n)
                add_load([(0, 0, rows(w_in, 0, KD, N_GATE + g * D + 2 * j * P, 256))], KD)

        def branches(j):
            for n in range(2):
                info[len(blocks) + n] = ("br", 2 * j + n, 0)
            c = 2 * j * P
            add_load([(0, 0, rows(I["w_br_a"][0], 0, 2, c, 256)), (2, 0, rows(I["w_br_b"][0], 0, 3, c, 256)),
                      (5, 0, rows(I["w_br_c"][0], 0, 3, c, 256))], KD)

        gates(0), gates(1), branches(0), branches(1), gates(2), branches(2), gates(3), branches(3)
        n_merge = len(blocks)
        for j in range(0, KD, 2):
            add_load([(0, 0, rows(w_out, 0, KD, j * P, 256))], KD)
        n_wout = len(blocks)
        for j in range(0, KF, 2):
            add_load([(0, 0, rows(w_gu, 0, KD, j * P, 256))], KD)
            add_load([(0, 0, rows(w_gu, 0, KD, D_FF + j * P, 256))], KD)
        n_gu = len(blocks)
        DOWN = ((0, 8), (8, 16), (16, 22))
        for j in range(0, KD, 2):
            for k0, k1 in DOWN:
                add_load([(0, 0, rows(w_dn, k0, k1, j * P, 256))], k1 - k0)
        n_all = len(blocks)
        w_loaded = [sem(f"w_loaded{i}") for i in range(3)]
        loaded_count, seen = [], [0, 0, 0]
        for n, (parts, _) in enumerate(loads):
            seen[n % 3] += 16 * len(parts)
            loaded_count.append(seen[n % 3])
        last_block = {b[0]: w for w, b in enumerate(blocks)}

        groups = []
        mm_at = [0]
        holder, before = {}, {}
        n_sum = 0
        sum_at = {}

        down = {}

        def allot(w):
            nonlocal n_sum
            bank = n_sum % 6 if w >= n_proj + 12 else n_sum % 4 if w < 3 else n_sum % 2
            before[n_sum] = holder.get(bank)
            holder[bank] = n_sum
            n_sum += 1
            return n_sum - 1, bank

        for w in range(n_all):
            sum_at[w] = n_sum
            g = []
            if info.get(w, ("",))[0] == "br":
                for k0, k1 in ((0, 2), (2, 5), (5, 8)):
                    for half in range(2):
                        g.append(allot(w) + (True, True, half, k0, k1))
            elif w < n_gu:
                for half in range(2):
                    g.append(allot(w) + (True, True, half, 0, KD))
            else:
                c, n = divmod((w - n_gu) % 6, 2)
                for half in range(2):
                    if c == 0:
                        down[n, half] = allot(w)
                    g.append(down[n, half] + (c == 0, c == 2, half, 0, DOWN[c][1] - DOWN[c][0]))
            groups.append(g)
            mm_at.append(mm_at[-1] + len(g))
        mm_done, acc_ev, w_hi_done, w_lo_done = sem("mm_done"), sem("acc_ev"), sem("w_hi_done"), sem("w_lo_done")

        def raw_block(w):
            load, kts, ncol, off = blocks[w]
            v = raw[:, load % 3, 0:kts * ncol].rearrange("p (k n) -> p k n", n=ncol)
            return v[:, :, off:off + P]

        def split_block(t, w):
            return t[:, w % 2, 0:blocks[w][1] * P].rearrange("p (k n) -> p k n", n=P)

        def load_weights(sp, n):
            parts, ncol = loads[n]
            if n >= 3:
                sp.wait_ge(w_lo_done, last_block[n - 3] + 1)
            for k0, c0, src in parts:
                k, mcol = src.shape[1], src.shape[2]
                dst = raw[:, n % 3, k0 * ncol:(k0 + k) * ncol].rearrange("p (k n) -> p k n", n=ncol)
                sp.dma_start(dst[:, :, c0:c0 + mcol], src).then_inc(w_loaded[n % 3], 16)

        def split_hi(act, w):
            load = blocks[w][0]
            act.wait_ge(w_loaded[load % 3], loaded_count[load])
            if w >= 2:
                act.wait_ge(mm_done, mm_at[w - 1])
            nc.scalar.activation(split_block(w_hi, w), raw_block(w), ACT.Copy).then_inc(w_hi_done, 1)

        def split_lo(dve, w):
            dve.wait_ge(w_hi_done, w + 1)
            nc.vector.tensor_tensor(split_block(w_lo, w), raw_block(w), split_block(w_hi, w).bitcast(F32),
                                    ALU.subtract).then_inc(w_lo_done, 1)

        def products(pe, side, w, x_hi, x_lo, kx=0, part=None):
            hi, lo = split_block(w_hi, w), split_block(w_lo, w)
            places = sum(g[6] - g[5] for g in groups[w])
            place = 0
            for idx, bank, first, last, half, k0, k1 in groups[w]:
                if first and before[idx] is not None:
                    pe.wait_ge(acc_ev, before[idx] + 1)
                for k in range(k0, k1):
                    side.until(w + place / places)
                    if part is not None:
                        part(half, kx + k)
                    for c, (a, b) in enumerate(((hi, x_hi), (hi, x_lo), (lo, x_hi))):
                        ins = nc.tensor.matmul(acc[:, bank, 0:H2], a[:, k, :], two(b[:, kx + k, :], half),
                                               start=first and k == k0 and c == 0,
                                               stop=last and k == k1 - 1 and c == 2)
                    if k == k1 - 1:
                        ins.then_inc(mm_done, 1)
                    place += 1

        def summed(w, n):
            idx, bank = groups[w][n][0:2]
            return idx, acc[:, bank, 0:H2], mm_at[w] + n + 1

        def par(h):
            return HD * (h % 2)


        kinds = [("if", 0)] + [(n, i) for n, c in
                               (("qa", 2), ("ka", 2), ("va", 2), ("oa", 2), ("qb", 3), ("kb", 3), ("vb", 3),
                                ("qc", 3), ("kc", 3), ("vc", 3)) for i in range(c)]
        assert len(kinds) == n_proj
        Q0 = {"a": 0, "b": 2, "c": 5}
        turns = [w for w, (n, _) in enumerate(kinds) if n[0] in "kv"]
        k_stores = [t for t, w in enumerate(turns) if kinds[w][0] in ("kb", "kc")]
        v_turns = [t for t, w in enumerate(turns) if kinds[w][0][0] == "v"]
        (o_yp, o_ys, o_pC, o_pn, o_pm, o_sC, o_sn, o_sm, o_pkv1, o_pkv2, o_pkv3, o_skv1, o_skv2, o_skv3,
         o_pk, o_pv, o_sk, o_sv) = O
        o_pkv, o_skv = (o_pkv1, o_pkv2, o_pkv3), (o_skv1, o_skv2, o_skv3)
        LW = (128, 256, 256)
        caches = (I["cache_dsa_kv1"], I["cache_dsa_kv2"], I["cache_dsa_kv3"])
        k_stored = [sem("k_stored0"), sem("k_stored1")]

        def turned_from(t):
            name, i = kinds[turns[t]]
            return kT[:, Q0[name[1]] + i, :] if name[0] == "k" else v_st[:, v_turns.index(t) % 2, :]

        def token_place(t):
            name, i = kinds[turns[t]]
            if name == "ka":
                v = ka_tok[:, :, P * i:P * (i + 1)]
            elif name == "va":
                v = va_tok[:, :, 2 * i:2 * i + 2, 0:HD]
            elif name[0] == "v":
                c = P * (i + (0 if name == "vb" else 3))
                v = v_tok[:, :, c:c + P]
            else:
                v = k_st[:, k_stores.index(t) % 2]
            return v[:, 0:NT], v[0:TS, NT]

        def store_tok(pool, t):
            pool.wait_ge(sem("tok_done"), 2 * t + 2)
            prompt, sample = token_place(t)
            name, i = kinds[turns[t]]
            s = 0 if name[0] == "k" else 1
            done = k_stored[k_stores.index(t) % 2] if s == 0 else sem("v_stored")
            if name[1] == "b":
                lw = min((128, 512, 2048)[i], TP)
                dst = o_pkv[i][0, 0].rearrange("(i p) s h d -> p i s (h d)", p=P)[:, :, s, :]
                pool.dma_start(dst, prompt[:, NT - lw // P:NT, :]).then_inc(done, 16)
                n = LW[i]
                dst = o_skv[i][0, :, n - TB:n, s].rearrange("b t h d -> b t (h d)")
                pool.dma_start(dst, sample).then_inc(done, 16)
            else:
                o_p, o_s = ((o_pk, o_sk), (o_pv, o_sv))[s]
                dst = o_p[0, 0].rearrange("(i p) h d -> p i (h d)", p=P)[:, :, P * i:P * (i + 1)]
                pool.dma_start(dst, prompt).then_inc(done, 16)
                dst = o_s[0].rearrange("b t h d -> (b t) (h d)")[:, P * i:P * (i + 1)]
                pool.dma_start(dst, sample).then_inc(done, 16)

        dil = [(i, [2 * g + j for g in range(3)]) for i in range(NT) for j in range(2)]
        units = dil + [(i, [h]) for i in range(NT) for h in range(6, HEADS)]
        ND, NU = len(dil), len(units)
        segs, unit_segs, widths = [], [], []
        for u, (i, heads) in enumerate(units):
            off, mine = 0, []
            for h in heads:
                k0 = max(0, i - 1) if kind_of(h) == 1 else 0
                mine.append(len(segs))
                segs.append((u, i, h, k0, off))
                off += P * (i + 1 - k0)
            unit_segs.append(mine)
            widths.append(off)
        T_DIL, T_BLK = 18, 27
        T_ML, T_MS = 8, 12
        T_SA = 33

        def unit_time(u, part):
            return T_DIL + u + part if u < ND else T_BLK + (u - ND + part) / 4

        def scores_in(u):
            return Sb[:, u % 2, 0:widths[u]] if u < ND else Sc[:, (u - ND) % 5, 0:widths[u]]

        def bias_of(h, c0, w):
            return (TTb[:, h] if h < 6 else TTc[:, h - 6])[:, c0:c0 + w]

        NC4 = (1, 2, 2, 2, 2, 2)
        ring_order = [("k", 0), ("k", 1), ("k", 2), ("k", 3), ("v", 0), ("k", 4), ("v", 1), ("k", 5),
                      ("v", 2), ("v", 3), ("v", 4), ("v", 5)]
        ring_in = [sem(f"ring_in{i}") for i in range(4)]
        ring_count = []
        for n, (_, q) in enumerate(ring_order):
            ring_count.append((ring_count[n - 4] if n >= 4 else 0) + (16 if q < 3 else 256))

        def ring_tiles(what, q):
            n = ring_order.index((what, q))
            return ring[n % 4], ring_in[n % 4], ring_count[n]

        def turned_p(half, g, c):
            if half == 0:
                return (2, 5 * HD + HD * g) if c == 2 else (2, HD * (2 * g + c - (g > 0)))
            return (2, HD * g) if c == 2 else (6, HD * (2 * g + c))

        O4_BANK = (7, 5)

        A_OFF = (0, 512, 896, 1152)

        with nc.Block() as blk:
            @blk.sync
            def _(sp):
                def beside():
                    yield 1.6
                    sp.wait_ge(sem("sq_mm"), NT + 1)
                    for h in range(HA):
                        p = par(h)
                        sp.dma_start(C0n[p:p + HD, :, h // 2, 0:HD], I["state_mlstm_C"][0, :, h].rearrange("b k v -> k b v")).then_inc(sem("st_in"), 16)
                        sp.dma_start(C0n[p:p + HD, :, h // 2, HD], I["state_mlstm_n"][0, :, h].rearrange("b k -> k b"),
                                     allow_slow_non_contiguous=True).then_inc(sem("st_in"), 16)
                    for g in range(3):
                        yield 4 + g
                        n = LW[g]
                        sp.dma_start(o_skv[g][0, :, 0:n - TB].rearrange("b w s h d -> b (w s h d)"),
                                     caches[g][0, :, TB:n].rearrange("b w s h d -> b (w s h d)")).then_inc(sem("moved_up"), 16)
                    yield T_BLK + 1
                    pages = [sp.value_load(I["page_table"][n // 2:n // 2 + 1, n % 2:n % 2 + 1], min_val=0, max_val=19)
                             for n in range(16)]
                    when = {0: 0.4, 1: 0.41, 2: 0.42, 3: 0.43, 4: 1.55, 5: 2.05, 6: 2.55, 7: 3.05, 9: 3.55, 11: 4.05, 8: 4.2, 10: 4.4}
                    for n, time in when.items():
                        yield T_SA + time
                        what, q = ring_order[n]
                        if n < 4:
                            sp.wait_ge(sem("o_mm"), len(segs))
                            sp.wait_ge(sem("new4"), 2)
                        else:
                            was, qq = ring_order[n - 4]
                            if was == "k":
                                sp.wait_ge(sem("kt_tr"), NB * (qq + 1))
                            else:
                                sp.wait_ge(sem("o4"), qq + 1)
                        s = "kv".index(what)
                        if q < 3:
                            c = NB * LW[q] // P
                            src = caches[q].rearrange("o b (c p) s h d -> p (o b c) s (h d)", p=P)
                            sp.dma_start(ring[n % 4][:, 0:c, :], src[:, :, s, :]).then_inc(ring_in[n % 4], 16)
                        else:
                            cache = I["cache_moba_k"] if what == "k" else I["cache_moba_v"]
                            for m, page in enumerate(pages):
                                src = cache[0, bass.ds(page, 1)].rearrange("o p h d -> p (o h d)")
                                sp.dma_start(ring[n % 4][:, m, :], src[:, P * (q - 3):P * (q - 2)]).then_inc(ring_in[n % 4], 16)

                side = Side(beside())
                sp.dma_start(con[:, :], X["con"]).then_inc(sem("con_in"), 16)
                sp.dma_start(vrow[0:8, :], I["norm_mix"].rearrange("o (k p) -> (o k) p", p=P)).then_inc(sem("vec_in"), 16)
                for i in range(NT + 1):
                    if i < NT:
                        sp.dma_start(x_tok[:, i, :], I["x_prompt"][0, P * i:P * (i + 1), :]).then_inc(sem(f"x_in{i}"), 16)
                    else:
                        sp.dma_start(x_tok[0:TS, i, :], I["x_sample"].rearrange("b t d -> (b t) d")).then_inc(sem(f"x_in{i}"), 16)
                    if i == 0:
                        sp.dma_start(vrow[8:16, :], I["norm_ffn"].rearrange("o (k p) -> (o k) p", p=P)).then_inc(sem("vec_in"), 16)
                        sp.dma_start(vrow[16:24, :], I["norm_final"].rearrange("(k p) -> k p", p=P)).then_inc(sem("vec_in"), 16)
                        sp.dma_start(vrow[24:26, :], I["mlstm_gain"].rearrange("o (k p) -> (o k) p", p=P)).then_inc(sem("vec_in"), 16)
                    if i == 1:
                        load_weights(sp, 0)
                load_weights(sp, 1)
                sp.dma_start(bif[:, :], I["b_if"].rearrange("o (c h) -> (o h) c", c=2),
                             allow_slow_non_contiguous=True).then_inc(sem("row_in"), 16)
                sp.dma_start(m0_row[:, :], I["state_mlstm_m"].rearrange("o b h -> (o h) b"),
                             allow_slow_non_contiguous=True).then_inc(sem("row_in"), 16)
                sp.dma_start(scan[:, :, :], X["scan"]).then_inc(sem("row_in"), 16)
                sp.dma_start(rowc[:, :], X["rowc"]).then_inc(sem("row_in"), 16)
                sp.dma_start(oh[:, :, :], X["oh"]).then_inc(sem("oh_in"), 16)
                sp.dma_start(rb[0:32, :], I["rel_bias"]).then_inc(sem("oh_in"), 16)
                sp.dma_start(oh4[:, :, :], X["oh"][:, :, OH0:OH0 + OHN]).then_inc(sem("oh4_in"), 16)
                for n in range(2, len(loads)):
                    if n >= 3:
                        side.until(last_block[n - 3])
                    load_weights(sp, n)
                for i in range(NT + 1):
                    sp.wait_ge(sem("y_left"), i + 1)
                    sp.wait_ge(sem("y_right"), i + 1)
                    if i < NT:
                        sp.dma_start(o_yp[0, P * i:P * (i + 1), :], o_st[:, i, :]).then_inc(sem("y_stored"), 16)
                    else:
                        sp.dma_start(o_ys.rearrange("b t d -> (b t) d"), o_st[0:TS, i, :]).then_inc(sem("y_stored"), 16)
                sp.wait_ge(sem("moved_up"), 48)
                sp.wait_ge(sem("y_stored"), 16 * (NT + 1))

            @blk.gpsimd
            def _(pool):
                st = Steps(pool, sem("pool_step"))
                st.then(nc.gpsimd.memset(ones[:, :], 1.0))
                st.then(nc.gpsimd.memset(eps[:, :], EPS))
                st.then(nc.gpsimd.memset(one[:, :], 1.0))
                nc.gpsimd.memset(rb[32:33, :], 1.0).then_inc(sem("rb_one"), 1)
                pool.wait_ge(sem("rb_one"), 1)
                for i in range(NT + 1):
                    n = P if i < NT else TS
                    pool.wait_ge(sem("x_ev"), i + 1)
                    if i >= 2:
                        pool.wait_ge(sem("sq_mm"), i - 1)
                    nc.gpsimd.tensor_tensor(xsq[:, i % 2, :, 0:n], xT[:, :, P * i:P * i + n], xT[:, :, P * i:P * i + n],
                                            ALU.mult).then_inc(sem("xsq_done"), 1)
                    pool.wait_ge(sem("xsq_done"), i + 1)
                pool.wait_ge(sem("x_tr"), NT + 1)
                pool.wait_ge(sem("h_lo_done"), NT + 1)
                pool.wait_ge(sem("sq_mm"), NT + 1)
                nc.gpsimd.memset(va_tok[:, :, :, HD:HD + 1], 1.0).then_inc(sem("va_one"), 1)
                pool.wait_ge(sem("va_one"), 1)
                nc.gpsimd.memset(QpA[:, :, :, :], 0.0).then_inc(sem("qpa_zero"), 1)
                pool.wait_ge(sem("qpa_zero"), 1)
                nc.gpsimd.memset(hA[:, NT], 0.0).then_inc(sem("ha_zero"), 1)
                pool.wait_ge(sem("tab_ev"), 8)
                tab_d = X["tab"].rearrange("o (h u) -> (o h) u", u=REV)
                for g in range(3):
                    pool.dma_start(tab_d[2 * g:2 * g + 2, :], tab[0:2, g, :]).then_inc(sem("tab_out"), 16)
                pool.dma_start(tab_d[6:HEADS, :], tab[0:6, 3, :]).then_inc(sem("tab_out"), 16)
                pool.wait_ge(sem("tab_out"), 64)
                pool.dma_start(X["rev"], X["tab"].broadcast_to([P, HEADS * REV])).then_inc(sem("rev_out"), 16)
                pool.wait_ge(sem("rows_done"), 1)
                pool.dma_start(o_pm.rearrange("o b h -> h (o b)"), m_row[:, TP - 1:TP], allow_slow_non_contiguous=True).then_inc(sem("a_out"), 16)
                pool.dma_start(o_sm.rearrange("o b h -> (o h) b"), m_row[:, TP + TB - 1:T:TB],
                               allow_slow_non_contiguous=True).then_inc(sem("a_out"), 16)
                pool.wait_ge(sem("rev_out"), 16)

                def bias_tiles(dst, h0, done):
                    pool.dma_start(dst, bass.AP(X["rev"].tensor, REV * h0 + P - 1,
                                                [[HEADS * REV - 1, P], [REV, 6], [1, TP]])).then_inc(done, 16)

                def state(h):
                    pool.wait_ge(sem("stp_ev"), h + 1)
                    pool.dma_start(o_pC[0, 0, h], st_o[:, h % 2, 0:HD]).then_inc(sem(f"st_stored{h % 2}"), 16)
                    pool.dma_start(o_pn[0, 0, h].rearrange("(k o) -> k o", o=1), st_o[:, h % 2, HD:HD + 1],
                                   allow_slow_non_contiguous=True).then_inc(sem(f"st_stored{h % 2}"), 16)

                def sample_state(h):
                    p = par(h)
                    pool.wait_ge(sem("cn_done"), h + 1)
                    pool.dma_start(o_sC[0, :, h].rearrange("b k v -> k b v"), C0n[p:p + HD, :, h // 2, 0:HD]).then_inc(sem("a_out"), 16)
                    pool.dma_start(o_sn[0, :, h].rearrange("b k -> k b"), C0n[p:p + HD, :, h // 2, HD],
                                   allow_slow_non_contiguous=True).then_inc(sem("a_out"), 16)

                tb = [t for t in range(len(turns)) if kinds[turns[t]][0][1] != "a"]
                for h in range(HA):
                    state(h)
                pool.wait_ge(sem("dc_mm"), 1)
                bias_tiles(TTb[:, :, :], 0, sem("ttb_in"))
                store_tok(pool, tb[0])
                store_tok(pool, tb[1])
                sample_state(0), sample_state(1)
                store_tok(pool, tb[2])
                sample_state(2), sample_state(3)
                store_tok(pool, tb[3])
                pool.wait_ge(sem("ya_done"), 4)
                bias_tiles(TTc[:, :, :], 6, sem("ttc_in"))
                for t in tb[4:]:
                    store_tok(pool, t)
                pool.wait_ge(sem("s_used"), ND * 3)
                st.then(nc.gpsimd.memset(RBs[:, :, :, :], 0.0))
                st.then(nc.gpsimd.memset(Qs[:, :, :], 0.0))
                st.then(nc.gpsimd.memset(rb4[32:33, :], 1.0))
                nc.gpsimd.nop().then_inc(sem("zero4"), 1)
                pool.dma_start(rb4[0:32, :], I["rel_bias"]).then_inc(sem("rb4_in"), 16)
                pool.wait_ge(sem("s_used"), len(segs))
                pool.wait_ge(sem("new4"), 2)
                nc.gpsimd.memset(Qpad[:, :, :, :], 0.0).then_inc(sem("qpad_zero"), 1)
                for s in k_stored:
                    pool.wait_ge(s, 32 * 3)
                pool.wait_ge(sem("v_stored"), 32 * 6)
                pool.wait_ge(sem("a_out"), 160)
                for b in range(2):
                    pool.wait_ge(sem(f"st_stored{b}"), 16 * HA)

            @blk.tensor
            def _(pe):
                def squares(i):
                    n = P if i < NT else TS
                    pe.wait_ge(sem("xsq_done"), i + 1)
                    out = acc[:, 6, P * i:P * i + n] if i < NT else acc[:, 7, 64:64 + TS]
                    for k in range(KD):
                        ins = nc.tensor.matmul(out, ones[:, :], xsq[:, i % 2, k, 0:n], start=k == 0, stop=k == KD - 1)
                    ins.then_inc(sem("sq_mm"), 1)

                def late_squares():
                    yield 0.2
                    squares(3)
                    yield 0.3
                    squares(4)

                def bias_rows():
                    yield 1.3
                    pe.wait_ge(sem("oh_in"), 32)
                    pe.wait_ge(sem("rb_one"), 1)
                    pe.wait_ge(sem("rstd_done"), 1)
                    for n, kind in enumerate((1, 2, 3, 0)):
                        yield 1.4 + 0.2 * n
                        if n >= 2:
                            pe.wait_ge(sem("tab_ev"), 2 * (n - 1))
                        heads = rb[:, 2 * (kind - 1):2 * kind] if kind else rb[:, 6:HEADS]
                        m, b = heads.shape[1], 4 + 2 * (n % 2)
                        nc.tensor.matmul(acc[0:m, b, 0:512], heads, oh[:, kind, 0:512], start=True, stop=True)
                        nc.tensor.matmul(acc[0:m, b + 1, 0:REV - 512], heads, oh[:, kind, 512:REV],
                                         start=True, stop=True).then_inc(sem("tab_mm"), 1)

                def turn():
                    for t, w in enumerate(turns):
                        yield w + 1 + 5 / 16
                        pe.wait_ge(acc_ev, sum_at[w] + 2)
                        if t >= 1:
                            pe.wait_ge(sem("tok_done"), 2 * t)
                        src = turned_from(t)
                        for i in range(NT):
                            ins = nc.tensor.transpose(acc[:, 2, P * i:P * (i + 1)], src[:, P * i:P * (i + 1)], ident)
                        ins.then_inc(sem("tok_tr"), 1)
                        yield w + 1 + 11 / 16
                        pe.wait_ge(sem("tok_done"), 2 * t + 1)
                        nc.tensor.transpose(acc[0:TS, 2, 0:P], src[:, TP:T], ident).then_inc(sem("tok_tr"), 1)

                def mlstm():
                    yield 3.3
                    pe.wait_ge(sem("rows_done"), 2)
                    for i in range(NT):
                        nc.tensor.transpose(acc[:, 3, HA * i:HA * (i + 1)], rA[:, P * i:P * (i + 1)], ident[0:HA, 0:HA])
                        nc.tensor.transpose(acc[:, 3, 16 + HA * i:16 + HA * (i + 1)], m_row[:, P * i:P * (i + 1)], ident[0:HA, 0:HA])
                    nc.tensor.transpose(acc[0:TS, 3, 32:36], rA[:, TP:T], ident[0:HA, 0:HA])
                    nc.tensor.transpose(acc[0:TS, 3, 36:40], m_row[:, TP:T], ident[0:HA, 0:HA])
                    pe.wait_ge(sem("tails_done"), 1)
                    nc.tensor.transpose(acc[0:TS, 3, 40:44], tails[:, 0:TS], ident[0:HA, 0:HA])
                    nc.tensor.transpose(acc[0:TS, 3, 44:48], tails[:, TS:2 * TS], ident[0:HA, 0:HA]).then_inc(sem("bytok_tr"), 1)
                    yield 3.7
                    pe.wait_ge(sem("tab_ev"), 8)
                    for h in range(HA):
                        nc.tensor.matmul(acc[:, 4 + h, :], rowc[:, R_SEL + P * h:R_SEL + P * (h + 1)], g_row[:, 0:TP],
                                         start=True, stop=True).then_inc(sem("g_mm"), 1)
                    for h in range(HA):
                        p = par(h)
                        for i in range(NT):
                            u = NT * h + i
                            yield T_ML + h + (0, 2, 4, 8)[i] / 16
                            if u == 0:
                                pe.wait_ge(sem("g_ev"), HA)
                                pe.wait_ge(sem("bytok_done"), 1)
                            if u >= 3:
                                pe.wait_ge(sem("pt_done"), u - 2)
                            nc.tensor.matmul(acc[:, 3 + u % 3, 0:TP - P * i], kT[p:p + HD, h // 2, P * i:P * (i + 1)],
                                             qT[p:p + HD, h // 2, P * i:TP], start=True, stop=True).then_inc(sem("a_s"), 1)
                        yield T_ML + h + 13 / 16
                        if h >= 1:
                            pe.wait_ge(sem("stp_ev"), h)
                        pe.wait_ge(sem("pt_done"), NT * (h + 1))
                        pe.wait_ge(sem("kw_done"), h + 1)
                        for j in range(NT):
                            for s in range(j + 1):
                                o = A_OFF[s] + P * (j - s)
                                nc.tensor.matmul(acc[:, 7, (HD + 1) * j:(HD + 1) * (j + 1)], PT[:, o:o + P],
                                                 va_tok[:, s, h, :], start=s == 0, stop=s == j)
                        c = NT * (HD + 1)
                        for s in range(NT):
                            ins = nc.tensor.matmul(acc[0:HD, 7, c:c + HD + 1], kw[:, s, :], va_tok[:, s, h, :],
                                                   start=s == 0, stop=s == NT - 1)
                        ins.then_inc(sem("a_o"), 1)
                    yield T_MS + 0.1
                    pe.wait_ge(sem("pt_done"), HA * NT)
                    order = Steps(pe, sem("pe_order"))
                    for h in range(HA):
                        ins = nc.tensor.matmul(acc[0:TS, 3, TS * h:TS * (h + 1)], rowc[:, R_SEL + P * h:R_SEL + P * h + TS],
                                               g_row[:, TP:T], start=True, stop=True)
                    ins.then_inc(sem("sg_mm"), 1)
                    for h in (0, 2, 1, 3):
                        p = par(h)
                        ins = nc.tensor.matmul(acc[0:TS, 4, TS * h:TS * (h + 1)], kT[p:p + HD, h // 2, TP:T],
                                               qT[p:p + HD, h // 2, TP:T], start=True, stop=True)
                        if h >= 2:
                            order.then(ins)
                    yield T_MS + 0.8
                    pe.wait_ge(sem("spt_done"), 1)
                    pe.wait_ge(sem("qp_done"), 1)
                    pe.wait_ge(sem("st_in"), 16 * 8)
                    for h in range(HA):
                        c = h * (HD + 1)
                        nc.tensor.matmul(acc[0:TS, 5, c:c + HD + 1], W[0:TS, 0, TS * h:TS * (h + 1)], va_tok[0:TS, NT, h, :],
                                         start=True, stop=True)
                    for h in (0, 2, 1, 3):
                        p = par(h)
                        c = h * (HD + 1)
                        for b in range(NB):
                            ins = nc.tensor.matmul(acc[0:TS, 6, c:c + HD + 1], QpA[p:p + HD, h // 2, b, :],
                                                   C0n[p:p + HD, b, h // 2, :], start=b == 0, stop=b == NB - 1)
                        if h == 2:
                            order.then(ins)
                    ins.then_inc(sem("so_mm"), 1)
                    for h in range(HA):
                        p = par(h)
                        ins = nc.tensor.matmul(acc[p:p + HD, 3, NB * (h // 2):NB * (h // 2 + 1)],
                                               rowc[:, R_SEL + P * h:R_SEL + P * h + HD], tails[:, 2 * TS:], start=True, stop=True)
                    ins.then_inc(sem("dc_mm"), 1)
                    for h in range(HA):
                        p = par(h)
                        yield T_MS + 1.8 + 0.5 * h
                        pe.wait_ge(sem("vb_done"), h + 1)
                        if h >= 1:
                            pe.wait_ge(sem("cn_done"), h)
                        for half in range(2):
                            ins = nc.tensor.matmul(acc[p:p + HD, 4 + half, 0:4 * (HD + 1)], kws[:, HD * h:HD * (h + 1)],
                                                   Vb[:, 4 * half:4 * half + 4, :], start=True, stop=True)
                        ins.then_inc(sem("sst_mm"), 1)
                    yield T_MS + 4.5
                    pe.wait_ge(sem("hn_done"), 1)
                    for pr in range(2):
                        for i in range(NT + 1):
                            n = P if i < NT else TS
                            b, c = (3 + 2 * pr, P * i) if i < NT else (4 + 2 * pr, 0)
                            ins = nc.tensor.transpose(acc[:, b, c:c + n], hA[0:n, i, 2 * pr:2 * pr + 2, :].rearrange("p h d -> p (h d)"),
                                                      ident[0:n, 0:n])
                        ins.then_inc(sem("ya_tr"), 1)

                def scores(n):
                    u, i, h, k0, off = segs[n]
                    if n >= 3:
                        pe.wait_ge(sem("s_used"), n - 2)
                    else:
                        pe.wait_ge(sem("ya_done"), 4)
                    p, t = par(h), 2 + h // 2
                    nc.tensor.matmul(acc[:, 3 + n % 3, 0:P * (i + 1 - k0)], qT[p:p + HD, t, P * i:P * (i + 1)],
                                     kT[p:p + HD, t, P * k0:P * (i + 1)], start=True, stop=True).then_inc(sem("s_mm"), 1)

                def turn_p(n):
                    u, i, h, k0, off = segs[n]
                    pe.wait_ge(sem("p_done"), u + 1)
                    if n >= 1:
                        pe.wait_ge(sem("pt_ev"), n)
                    src = scores_in(u)
                    for k in range(i + 1 - k0):
                        ins = nc.tensor.transpose(acc[:, 6, P * k:P * (k + 1)], src[:, off + P * k:off + P * (k + 1)], ident)
                    ins.then_inc(sem("pt_tr"), 1)

                def outputs(n):
                    u, i, h, k0, off = segs[n]
                    pe.wait_ge(sem("pt_ev"), n + 1)
                    if n >= 1:
                        pe.wait_ge(sem("o_ev"), n)
                    p = par(h)
                    for k in range(i + 1 - k0):
                        ins = nc.tensor.matmul(acc[p:p + HD, 7, 0:P], v_tok[:, k0 + k, HD * h:HD * (h + 1)],
                                               PTs[:, n % 2, P * k:P * (k + 1)], start=k == 0, stop=k == i - k0)
                    ins.then_inc(sem("o_mm"), 1)

                def attention():
                    for u in range(ND + 1):
                        for c in range(3):
                            if u < ND:
                                yield unit_time(u, (1 + c) / 16)
                                scores(unit_segs[u][c])
                        for c in range(3):
                            if u >= 1:
                                yield T_DIL + u + (5, 8, 12)[c] / 16
                                turn_p(unit_segs[u - 1][c])
                                yield T_DIL + u + (7, 11, 15)[c] / 16
                                outputs(unit_segs[u - 1][c])
                    for c in range(NU - ND + 3):
                        u = ND + c
                        if u < NU:
                            yield unit_time(u, 0)
                            scores(unit_segs[u][0])
                        if 3 <= c:
                            yield unit_time(u, 0.25)
                            outputs(unit_segs[u - 3][0])
                        if 2 <= c < NU - ND + 2:
                            yield unit_time(u, 0.75)
                            turn_p(unit_segs[u - 2][0])

                def sample():
                    yield T_SA + 0.85
                    pe.wait_ge(sem("q4"), 1)
                    pe.wait_ge(sem("oh4_in"), 16)
                    pe.wait_ge(sem("s_used"), len(segs))
                    pe.wait_ge(sem("tok_done"), 2 * len(turns))
                    for q in range(6):
                        g, lo = q % 3, HD * (q // 3)
                        kind = 1 + q if q < 3 else 0
                        w = P * NC4[q]
                        u0 = TP - 1 - w - OH0
                        new = acc[lo:lo + HD, 2, TS * g:TS * (g + 1)]
                        for t in range(TB):
                            rbt = RBs[:, t, 2 * q:2 * q + 2, :].rearrange("p h n -> p (h n)")
                            nc.tensor.matmul(acc[lo:lo + HD, 3 + g, 0:w], rbt, oh4[:, kind, u0 - t:u0 - t + w], start=t == 0, stop=False)
                            n0 = TP - 1 - OH0 - t
                            nc.tensor.matmul(new.rearrange("p (b t) -> p b t", t=TB), rbt,
                                             oh4[:, kind, n0:n0 + TB].unsqueeze(1).broadcast_to([33, NB, TB]),
                                             start=t == 0, stop=False)
                        nc.tensor.matmul(new, Qs[:, q, :], kTn[:, q, :], start=False, stop=True).then_inc(sem("new_mm"), 1)

                    def turn_k(n):
                        q, b = divmod(n, NB)
                        if n >= 2:
                            pe.wait_ge(sem("kt_ev"), n - 1)
                        tiles, done, count = ring_tiles("k", q)
                        pe.wait_ge(done, count)
                        for c in range(NC4[q]):
                            ins = nc.tensor.transpose(acc[:, 6 + n % 2, P * c:P * (c + 1)], tiles[:, NC4[q] * b + c, :], ident)
                        ins.then_inc(sem("kt_tr"), 1)

                    yield T_SA + 1
                    pe.wait_ge(sem("o_ev"), len(segs))
                    turn_k(0)
                    for n in range(6 * NB):
                        q, b = divmod(n, NB)
                        yield T_SA + 1 + n / 16
                        if n + 1 < 6 * NB:
                            turn_k(n + 1)
                        pe.wait_ge(sem("kt_ev"), n + 1)
                        if b == 0:
                            pe.wait_ge(sem("qpad_done"), q + 1)
                        g, lo, w = q % 3, HD * (q // 3), P * NC4[q]
                        nc.tensor.matmul(acc[lo:lo + HD, 3 + g, 0:w], Qpad[:, q % 2, b, :], KTs[:, n % 2, 0:w],
                                         start=False, stop=b == NB - 1).then_inc(sem("qk4"), 1)

                def sample_outputs():
                    for half in range(2):
                        yield T_SA + (3.4, 4.7)[half]
                        pe.wait_ge(sem("p4"), half + 1)
                        if half == 0:
                            pe.wait_ge(sem("new_read"), 1)
                        else:
                            pe.wait_ge(sem("pt4_ev"), 2)
                        lo = HD * half
                        idn = con[lo:lo + HD, C_ID + lo:C_ID + lo + HD]
                        for g in range(3):
                            for c in range(NC4[3 * half + g]):
                                b, at = turned_p(half, g, c)
                                nc.tensor.transpose(acc[:, b, at:at + HD], S4[lo:lo + HD, g, P * c:P * (c + 1)], idn)
                            b, at = turned_p(half, g, 2)
                            ins = nc.tensor.transpose(acc[0:TS, b, at:at + HD], S4[lo:lo + HD, g, 256:288], idn)
                        ins.then_inc(sem("pt4"), 1)
                        for g in range(3):
                            q = 3 * half + g
                            yield T_SA + (4.05 + 0.25 * g if half == 0 else 4.95)
                            tiles, done, count = ring_tiles("v", q)
                            pe.wait_ge(done, count)
                            if g == 0:
                                pe.wait_ge(sem("pt4_ev"), 2 * half + 2)
                                pe.wait_ge(sem("kt_ev"), 6 * NB)
                            out = acc[:, O4_BANK[half], 2 * TS * g:2 * TS * (g + 1)]
                            nc.tensor.matmul(out, vn[:, P * q:P * (q + 1)], PT4[0:TS, g, 2, lo:lo + HD], start=True, stop=False)
                            for b in range(NB):
                                for c in range(NC4[q]):
                                    ins = nc.tensor.matmul(out.rearrange("p (h n) -> p h n", h=2)[:, :, TB * b:TB * (b + 1)],
                                                           tiles[:, NC4[q] * b + c, :],
                                                           PT4[:, g, c, lo:lo + HD].rearrange("p (h n) -> p h n", h=2)[:, :, TB * b:TB * (b + 1)],
                                                           start=False, stop=b == NB - 1 and c == NC4[q] - 1)
                            ins.then_inc(sem("o4"), 1)

                pe.wait_ge(sem("con_in"), 16)
                for i in range(NT + 1):
                    n = P if i < NT else TS
                    pe.wait_ge(sem(f"x_in{i}"), 16)
                    if i >= 2:
                        pe.wait_ge(sem("x_ev"), i - 1)
                    for k in range(KD):
                        ins = nc.tensor.transpose(acc[:, 2 + 2 * (i % 2) + k // 4, P * (k % 4):P * (k % 4) + n],
                                                  x_tok[0:n, i, P * k:P * (k + 1)], ident[0:n, 0:n])
                    ins.then_inc(sem("x_tr"), 1)
                    if i == 0:
                        pe.wait_ge(sem("vec_in"), 64)
                        nc.tensor.transpose(acc[:, 7, 0:26], vrow[:, :], ident[0:26, 0:26]).then_inc(sem("v_tr"), 1)
                for i in range(3):
                    squares(i)

                side = Side(late_squares(), bias_rows(), turn(), mlstm(), attention(), sample(), sample_outputs())

                def tile_split(w):
                    if w == 0:
                        return lambda half, k: pe.wait_ge(sem("h_lo_done"), 3 if half == 0 else NT + 1)
                    if info.get(w, ("",))[0] == "br":
                        return lambda half, k: pe.wait_ge(sem("y_lo_done"), k + 1)
                    if w == n_merge:
                        return lambda half, k: pe.wait_ge(sem("mg_lo_done"), k + 1)
                    if w == n_wout:
                        return lambda half, k: pe.wait_ge(sem("h2_lo_done"), k + 1)
                    if w >= n_gu:
                        return lambda half, k: pe.wait_ge(sem("s_lo_done"), k + 1)
                    return None

                for w in range(n_all):
                    pe.wait_ge(w_lo_done, w + 1)
                    if w < n_wout and info.get(w, ("",))[0] == "br":
                        products(pe, side, w, y_hi, y_lo, part=tile_split(w))
                    elif n_merge <= w < n_wout:
                        products(pe, side, w, mg_hi, mg_lo, part=tile_split(w))
                    elif w >= n_gu:
                        products(pe, side, w, s_hi, s_lo, kx=DOWN[(w - n_gu) % 6 // 2][0], part=tile_split(w))
                    else:
                        products(pe, side, w, h_hi, h_lo, part=tile_split(w))
                    if w == n_wout:
                        pe.wait_ge(sem("ssq2_done"), KD)
                        for half in range(2):
                            ins = nc.tensor.matmul(acc[:, 6 + half, 0:H2], ones[:, :], two(ssq, half), start=True, stop=True)
                        ins.then_inc(sem("ssq_mm"), 1)
                pe.wait_ge(sem("ssq3_done"), KD)
                pe.wait_ge(acc_ev, n_sum)
                for i in range(NT + 1):
                    n = P if i < NT else TS
                    ins = nc.tensor.matmul(acc[0:n, 7, i:i + 1], ssq[:, P * i:P * i + n], ones[:, 0:1], start=True, stop=True)
                ins.then_inc(sem("rt_mm"), 1)
                pe.wait_ge(sem("xg_done"), KD)
                for i in range(NT + 1):
                    n = P if i < NT else TS
                    if i >= 3:
                        pe.wait_ge(sem("y_left"), i - 2)
                        pe.wait_ge(sem("y_right"), i - 2)
                    for k in range(KD):
                        ins = nc.tensor.transpose(acc[0:n, 2 * (i % 3) + k // 4, P * (k % 4):P * (k % 4 + 1)],
                                                  xT[:, k, P * i:P * i + n], ident)
                    ins.then_inc(sem("y_tr"), 1)

            @blk.scalar
            def _(act):
                a = Steps(act, sem("act_step"))

                def rstd_rows():
                    yield 0.35
                    act.wait_ge(sem("sq_mm"), NT + 1)
                    nc.scalar.activation(rstd[:, 0:TP], acc[:, 6, :], ACT.Sqrt, bias=eps[:, :], scale=1.0 / D).then_inc(sem("std_done"), 1)
                    nc.scalar.activation(rstd[:, TP:T], acc[:, 7, 64:64 + TS], ACT.Sqrt, bias=eps[:, :], scale=1.0 / D).then_inc(sem("std_done"), 1)

                def bias_rows():
                    for n, kind in enumerate((1, 2, 3, 0)):
                        yield 1.5 + 0.2 * n
                        act.wait_ge(sem("tab_mm"), n + 1)
                        m, b = (2, 4 + 2 * (n % 2)) if kind else (6, 4 + 2 * (n % 2))
                        nc.scalar.copy(tab[0:m, n, 0:512], acc[0:m, b, 0:512]).then_inc(sem("tab_ev"), 1)
                        nc.scalar.copy(tab[0:m, n, 512:REV], acc[0:m, b + 1, 0:REV - 512]).then_inc(sem("tab_ev"), 1)

                def turn():
                    act.wait_ge(sem("va_one"), 1)
                    for t, w in enumerate(turns):
                        yield w + 1 + 8 / 16
                        act.wait_ge(sem("tok_tr"), 2 * t + 1)
                        name, i = kinds[w]
                        if t in k_stores and k_stores.index(t) >= 2:
                            n = k_stores.index(t)
                            act.wait_ge(k_stored[n % 2], 32 * (n // 2))
                        if name == "vb" and i == 0:
                            act.wait_ge(sem("oa_read"), 1)
                        pr, sa = token_place(t)
                        src, ssrc = acc[:, 2, 0:TP], acc[0:TS, 2, 0:P]
                        if name == "va":
                            src = src.rearrange("p (i h d) -> p i h d", h=2, d=HD)
                            ssrc = ssrc.rearrange("p (h d) -> p h d", d=HD)
                        else:
                            src = src.rearrange("p (i c) -> p i c", c=P)
                        nc.scalar.copy(pr, src).then_inc(sem("tok_done"), 1)
                        yield w + 1 + 13 / 16
                        act.wait_ge(sem("tok_tr"), 2 * t + 2)
                        nc.scalar.copy(sa, ssrc).then_inc(sem("tok_done"), 1)

                def mlstm():
                    yield 1.4
                    act.wait_ge(sem("f_ready"), 1)
                    a.then(nc.scalar.activation(rB[:, :], rB[:, :], ACT.Exp))
                    nc.scalar.activation(rB[:, :], rB[:, :], ACT.Ln, bias=one[0:HA, :]).then_inc(sem("ln_done"), 1)
                    yield 3.2
                    act.wait_ge(sem("rows_done"), 2)
                    nc.scalar.activation(tails[:, :], tails[:, :], ACT.Exp).then_inc(sem("tails_done"), 1)
                    yield 3.6
                    act.wait_ge(sem("bytok_tr"), 1)
                    a.then(nc.scalar.copy(by_tok[:, 0:32], acc[:, 3, 0:32]))
                    a.then(nc.scalar.copy(by_tok[0:TS, 32:48], acc[0:TS, 3, 32:48]))
                    a.then(nc.scalar.activation(e_m[:, 0:16], by_tok[:, 16:32], ACT.Exp, scale=-1.0))
                    nc.scalar.activation(e_m[0:TS, 16:20], by_tok[0:TS, 36:40], ACT.Exp, scale=-1.0).then_inc(sem("bytok_done"), 1)
                    for h in range(HA):
                        yield 4.1 + 0.2 * h
                        act.wait_ge(sem("g_mm"), h + 1)
                        nc.scalar.copy(G[:, h, :], acc[:, 4 + h, :]).then_inc(sem("g_ev"), 1)
                    yield 5.6
                    act.wait_ge(sem("ws_arg"), 1)
                    nc.scalar.activation(ws[:, :], ws[:, :], ACT.Exp).then_inc(sem("ws_done"), 1)
                    for u in range(HA * NT):
                        h, i = divmod(u, NT)
                        yield T_ML + h + (-0.1, 0.12, 0.24, 0.36)[i]
                        act.wait_ge(sem("w_arg"), u + 1)
                        bias = by_tok[:, HA * i + h:HA * i + h + 1]
                        Wb = W[:, u % 2]
                        if i < NT - 1:
                            nc.scalar.activation(Wb[:, P:TP - P * i], G[:, h, P * (i + 1):TP], ACT.Exp, bias=bias)
                        nc.scalar.activation(Wb[:, 0:P], Wb[:, 0:P], ACT.Exp, bias=bias).then_inc(sem("w_done"), 1)
                    yield T_MS + 0.4
                    act.wait_ge(sem("sw_arg"), 1)
                    for h in range(HA):
                        ins = nc.scalar.activation(W[0:TS, 1, TS * h:TS * (h + 1)], W[0:TS, 1, TS * h:TS * (h + 1)], ACT.Exp,
                                                   bias=by_tok[0:TS, 32 + h:33 + h])
                    ins.then_inc(sem("sw_done"), 1)
                    yield T_MS + 2.1
                    act.wait_ge(acc_ev, sum_at[9])
                    nc.scalar.activation(oaT[:, :, :], oaT[:, :, :], ACT.Sigmoid).then_inc(sem("oa_done"), 1)
                    yield T_MS + 4.1
                    act.wait_ge(sem("rs_arg"), 1)
                    nc.scalar.activation(rs[:, :], rs[:, :], ACT.Sqrt, bias=eps[:, :], scale=1.0 / HD).then_inc(sem("rs_std"), 1)

                def exps(u):
                    act.wait_ge(sem("m_done"), u + 1)
                    if u >= 4:
                        act.wait_ge(sem("p_done"), u - 3)
                    s = scores_in(u)
                    nc.scalar.activation(s, s, ACT.Exp, bias=mx[:, u % 4:u % 4 + 1],
                                         accum_out=dn[:, u % 4:u % 4 + 1]).then_inc(sem("e_done"), 1)

                def turned(n):
                    u, i, h, k0, off = segs[n]
                    act.wait_ge(sem("pt_tr"), n + 1)
                    if n >= 2:
                        act.wait_ge(sem("o_mm"), n - 1)
                    w = P * (i + 1 - k0)
                    nc.scalar.copy(PTs[:, n % 2, 0:w], acc[:, 6, 0:w]).then_inc(sem("pt_ev"), 1)

                def attention():
                    for u in range(ND + 1):
                        for c in range(3):
                            if u >= 1:
                                yield T_DIL + u + (6, 9, 13)[c] / 16
                                turned(unit_segs[u - 1][c])
                                if c == 0 and u < ND:
                                    exps(u)
                            elif c == 0:
                                yield unit_time(u, 7 / 16)
                                exps(u)
                    for c in range(NU - ND + 3):
                        u = ND + c
                        if 3 <= c:
                            yield unit_time(u, 0.1)
                            turned(unit_segs[u - 3][0])
                        if c < NU - ND:
                            yield unit_time(u, 0.6)
                            exps(u)

                def gates():
                    for w in range(n_proj, n_merge):
                        if info[w][0] == "gate":
                            _, j, r = info[w]
                            yield w + 1.3
                            act.wait_ge(acc_ev, sum_at[w] + 2)
                            nc.scalar.activation(gs[j % 2][:, r, :], gs[j % 2][:, r, :], ACT.Tanh, scale=0.5).then_inc(sem("g_tanh"), 1)

                def sample():
                    for n in range(6 * NB):
                        yield T_SA + 1 + (n - 0.5) / 16
                        act.wait_ge(sem("kt_tr"), n + 1)
                        if n >= 2:
                            act.wait_ge(sem("qk4"), n - 1)
                        w = P * NC4[n // NB]
                        nc.scalar.copy(KTs[:, n % 2, 0:w], acc[:, 6 + n % 2, 0:w]).then_inc(sem("kt_ev"), 1)

                def sample_softmax():
                    for half in range(2):
                        yield T_SA + (2.8, 4.4)[half]
                        act.wait_ge(sem("mx4"), half + 1)
                        lo = HD * half
                        for g in range(3):
                            s = S4[lo:lo + HD, g, :]
                            nc.scalar.activation(s, s, ACT.Exp, bias=mx4[lo:lo + HD, g:g + 1],
                                                 accum_out=dn4[lo:lo + HD, g:g + 1]).then_inc(sem("e4"), 1)
                        yield T_SA + (3.6, 4.85)[half]
                        act.wait_ge(sem("pt4"), half + 1)
                        if half == 0:
                            act.wait_ge(sem("new_mm"), 6)
                            nc.scalar.copy(PT4[:, 0, 0, 0:HD], acc[:, 2, 0:HD])
                            nc.scalar.copy(PT4[:, 1:3, 0:2, 0:HD], acc[:, 2, HD:5 * HD].rearrange("p (g c n) -> p g c n", c=2, n=HD)
                                           ).then_inc(sem("pt4_ev"), 1)
                            nc.scalar.copy(PT4[0:TS, :, 2, 0:HD], acc[0:TS, 2, 5 * HD:8 * HD].rearrange("p (g n) -> p g n", n=HD)
                                           ).then_inc(sem("pt4_ev"), 1)
                        else:
                            nc.scalar.copy(PT4[:, :, 0:2, HD:P], acc[:, 6, 0:6 * HD].rearrange("p (g c n) -> p g c n", c=2, n=HD)
                                           ).then_inc(sem("pt4_ev"), 1)
                            nc.scalar.copy(PT4[0:TS, :, 2, HD:P], acc[0:TS, 2, 0:3 * HD].rearrange("p (g n) -> p g n", n=HD)
                                           ).then_inc(sem("pt4_ev"), 1)

                def merge():
                    yield n_proj + 12 - 0.03
                    act.wait_ge(sem("y4"), 4)
                    for k in range(8):
                        nc.scalar.copy(y_hi[:, k, :], qT[:, k, :]).then_inc(sem("y_hi_done"), 1)
                    for w in range(n_proj, n_merge):
                        if info[w][0] == "br":
                            k = info[w][1]
                            yield w + 1.03
                            act.wait_ge(sem("mg_done"), k + 1)
                            nc.scalar.activation(mg_hi[:, k, :], mt[:, 0, :], ACT.Copy, scale=0.5).then_inc(sem("mg_hi_done"), 1)
                    for k in range(KD):
                        yield n_merge + k + 1.03
                        act.wait_ge(acc_ev, sum_at[n_merge + k] + 2)
                        nc.scalar.activation(h_hi[:, k, :], xT[:, k, :], ACT.Copy, scale=vecs[:, 8 + k:9 + k]).then_inc(sem("h2_hi_done"), 1)
                        if k >= 2:
                            act.wait_ge(sem("ssq2_done"), k - 1)
                        nc.scalar.activation(sq[:, k % 2, :], xT[:, k, :], ACT.Square).then_inc(sem("sq2_done"), 1)

                def feed():
                    yield n_wout + 1.1
                    act.wait_ge(sem("ssq_mm"), 1)
                    for half in range(2):
                        nc.scalar.activation(two(rstd, half), acc[:, 6 + half, 0:H2], ACT.Sqrt, bias=eps[:, :],
                                             scale=1.0 / D).then_inc(sem("std_done"), 1)
                    for w in range(n_wout, n_gu):
                        j, r = divmod(w - n_wout, 4)
                        yield w + 1.1
                        if r < 2:
                            act.wait_ge(acc_ev, sum_at[w] + 2)
                            if j >= 1:
                                act.wait_ge(sem("s_hi_done"), 2 * (j - 1) + r + 1)
                            nc.scalar.activation(sg[:, r, :], gx[:, r, :], ACT.Sigmoid).then_inc(sem("sg_done"), 1)
                        else:
                            k = 2 * j + r - 2
                            act.wait_ge(sem("s_done"), k + 1)
                            nc.scalar.copy(s_hi[:, k, :], gx[:, r - 2, :]).then_inc(sem("s_hi_done"), 1)
                    for k in range(KD):
                        w = n_gu + 6 * (k // 2) + 4 + k % 2
                        yield w + 1.1
                        act.wait_ge(acc_ev, sum_at[w - 4] + 2)
                        if k >= 2:
                            act.wait_ge(sem("ssq3_done"), k - 1)
                        nc.scalar.activation(sq[:, k % 2, :], xT[:, k, :], ACT.Square).then_inc(sem("sq3_done"), 1)
                        nc.scalar.activation(xT[:, k, :], xT[:, k, :], ACT.Copy, scale=vecs[:, 16 + k:17 + k]).then_inc(sem("xg_done"), 1)

                act.wait_ge(sem("v_tr"), 1)
                nc.scalar.copy(vecs[:, :], acc[:, 7, 0:26]).then_inc(sem("vecs_done"), 1)

                def x_hi(i):
                    n = P if i < NT else TS
                    act.wait_ge(sem("xg_made"), i + 1)
                    nc.scalar.copy(h_hi[:, :, P * i:P * i + n], xg[:, i % 2, :, 0:n]).then_inc(sem("h_hi_done"), 1)

                for i in range(NT + 1):
                    n = P if i < NT else TS
                    act.wait_ge(sem("x_tr"), i + 1)
                    b = 2 + 2 * (i % 2)
                    nc.scalar.copy(xT[:, :, P * i:P * i + n].rearrange("p (b k) n -> p b k n", b=2),
                                   acc[:, b:b + 2, :].rearrange("p b (k n) -> p b k n", n=P)[:, :, :, 0:n]).then_inc(sem("x_ev"), 1)
                    if i >= 1:
                        x_hi(i - 1)
                    if i == 2:
                        split_hi(act, 0)
                x_hi(NT)
                side = Side(rstd_rows(), bias_rows(), turn(), mlstm(), attention(), gates(), sample(), sample_softmax(), merge(), feed())
                for w in range(n_all):
                    side.until(w + 0.05)
                    if w + 1 < n_all:
                        split_hi(act, w + 1)
                side.until(n_all + 2)
                act.wait_ge(sem("rt_mm"), 1)
                act.wait_ge(sem("rt_set"), 1)
                nc.scalar.activation(rt[:, 0:NT], acc[:, 7, 0:NT], ACT.Sqrt, bias=eps[:, :], scale=1.0 / D).then_inc(sem("rt_std"), 1)
                nc.scalar.activation(rt[0:TS, NT:NT + 1], acc[0:TS, 7, NT:NT + 1], ACT.Sqrt, bias=eps[0:TS, :],
                                     scale=1.0 / D).then_inc(sem("rt_std"), 1)
                act.wait_ge(sem("rt_done"), 1)
                for i in range(NT + 1):
                    n = P if i < NT else TS
                    act.wait_ge(sem("y_tr"), i + 1)
                    nc.scalar.activation(o_st[0:n, i, 0:512], acc[0:n, 2 * (i % 3), :], ACT.Copy, scale=rt[0:n, i:i + 1]).then_inc(sem("y_left"), 1)

            @blk.vector
            def _(dve):
                v = Steps(dve, sem("dve_step"))

                def evac(w, half):
                    if w < n_proj:
                        name, i = kinds[w]
                        idx, src, ready = summed(w, half)
                        dve.wait_ge(mm_done, ready)
                        r = two(rstd, half)
                        if name == "if":
                            v.do(nc.vector.tensor_tensor(two(i_row, half), src[0:HA], r[0:HA], ALU.mult))
                            v.then(nc.vector.tensor_tensor(two(f_row, half), src[32:32 + HA], r[32:32 + HA], ALU.mult))
                            nc.vector.nop().then_inc(acc_ev, 1)
                            return
                        if name[0] == "v":
                            n = v_turns.index(turns.index(w))
                            if n >= 2:
                                dve.wait_ge(sem("tok_tr"), 2 * v_turns[n - 2] + 2)
                            dst = v_st[:, n % 2, :]
                        elif name == "oa":
                            dst = oaT[:, i, :]
                        else:
                            dst = (qT if name[0] == "q" else kT)[:, Q0[name[1]] + i, :]
                        if w == turns[0]:
                            dve.wait_ge(sem("tab_out"), 64)
                        if name == "qc" and i == 0:
                            v.sync()
                        if name in ("ka", "qb", "qc"):
                            nc.vector.scalar_tensor_tensor(two(dst, half), src, SCALE, r, ALU.mult, ALU.mult).then_inc(acc_ev, 1)
                        else:
                            nc.vector.tensor_tensor(two(dst, half), src, r, ALU.mult).then_inc(acc_ev, 1)
                    elif w < n_merge and info[w][0] == "gate":
                        _, j, r = info[w]
                        idx, src, ready = summed(w, half)
                        if half == 0:
                            v.sync()
                        if w == n_proj + 4 and half == 0:
                            for s in k_stored:
                                dve.wait_ge(s, 32 * 3)
                        if w == n_proj and half == 0:
                            dve.wait_ge(sem("tok_tr"), 2 * len(turns) - 2)
                        dve.wait_ge(mm_done, ready)
                        nc.vector.tensor_tensor(two(gs[j % 2][:, r, :], half), src, two(rstd, half), ALU.mult).then_inc(acc_ev, 1)
                    elif w < n_merge:
                        k = info[w][1]
                        g, n = gs[(k // 2) % 2], k % 2
                        for c in ((0,) if half == 0 else (1, 2)):
                            if c == 0:
                                dve.wait_ge(sem("g_tanh"), 6 * (k // 2) + 6)
                                if k >= 1:
                                    dve.wait_ge(sem("mg_hi_done"), k)
                            for hf in range(2):
                                idx, src, ready = summed(w, 2 * c + hf)
                                dve.wait_ge(mm_done, ready)
                                v.do(nc.vector.scalar_tensor_tensor(two(mt[:, min(c, 1), :], hf), two(g[:, 2 * c + n, :], hf), 1.0, src,
                                                                    ALU.add, ALU.mult))
                                v.sync()
                                nc.vector.nop().then_inc(acc_ev, 1)
                            if c:
                                v.then(nc.vector.tensor_tensor(mt[:, 0, :], mt[:, 0, :], mt[:, 1, :], ALU.add))
                        if half == 1:
                            nc.vector.nop().then_inc(sem("mg_done"), 1)
                            dve.wait_ge(sem("mg_hi_done"), k + 1)
                            v.then(nc.vector.scalar_tensor_tensor(mg_lo[:, k, :], mt[:, 0, :], 0.5, mg_hi[:, k, :].bitcast(F32),
                                                                  ALU.mult, ALU.subtract))
                            nc.vector.nop().then_inc(sem("mg_lo_done"), 1)
                    elif w < n_wout:
                        k = w - n_merge
                        idx, src, ready = summed(w, half)
                        dve.wait_ge(mm_done, ready)
                        nc.vector.tensor_tensor(two(xT[:, k, :], half), src, two(xT[:, k, :], half), ALU.add).then_inc(acc_ev, 1)
                        if half == 1:
                            dve.wait_ge(sem("h2_hi_done"), k + 1)
                            nc.vector.scalar_tensor_tensor(h_lo[:, k, :], xT[:, k, :], vecs[:, 8 + k:9 + k],
                                                           h_hi[:, k, :].bitcast(F32), ALU.mult, ALU.subtract).then_inc(sem("h2_lo_done"), 1)
                            add_squares(k, "sq2_done", "ssq2_done")
                    elif w < n_gu:
                        j, r = divmod(w - n_wout, 4)
                        if w == n_wout and half == 0:
                            dve.wait_ge(mm_done, mm_at[w + 1])
                            dve.wait_ge(sem("std_done"), 4)
                            v.then(nc.vector.reciprocal(rstd[:, :], rstd[:, :]))
                        if half == 0 and r >= 2:
                            dve.wait_ge(sem("sg_done"), 2 * j + r - 1)
                            v.then(nc.vector.tensor_tensor(gx[:, r - 2, :], gx[:, r - 2, :], sg[:, r - 2, :], ALU.mult))
                        if half == 0 and r < 2 and j >= 1:
                            dve.wait_ge(sem("s_lo_done"), 2 * (j - 1) + r + 1)
                        idx, src, ready = summed(w, half)
                        dve.wait_ge(mm_done, ready)
                        dst = gx[:, r, :] if r < 2 else sg[:, r - 2, :]
                        nc.vector.tensor_tensor(two(dst, half), src, two(rstd, half), ALU.mult).then_inc(acc_ev, 1)
                        if half == 1 and r >= 2:
                            dve.wait_ge(acc_ev, idx + 1)
                            v.then(nc.vector.tensor_tensor(gx[:, r - 2, :], gx[:, r - 2, :], sg[:, r - 2, :], ALU.mult))
                            nc.vector.nop().then_inc(sem("s_done"), 1)
                    else:
                        j, r = divmod(w - n_gu, 6)
                        if r < 4:
                            return
                        k = 2 * j + r - 4
                        idx, src, ready = summed(w, half)
                        dve.wait_ge(mm_done, ready)
                        nc.vector.tensor_tensor(two(xT[:, k, :], half), src, two(xT[:, k, :], half), ALU.add).then_inc(acc_ev, 1)
                        if half == 1:
                            add_squares(k, "sq3_done", "ssq3_done")

                def add_squares(k, squared, added):
                    dve.wait_ge(sem(squared), k + 1)
                    if k == 0:
                        nc.vector.tensor_copy(ssq[:, :], sq[:, 0, :]).then_inc(sem(added), 1)
                    else:
                        dve.wait_ge(sem(added), k)
                        nc.vector.tensor_tensor(ssq[:, :], ssq[:, :], sq[:, k % 2, :], ALU.add).then_inc(sem(added), 1)

                def feed():
                    for k in range(KF):
                        yield n_wout + 4 * (k // 2) + 3 + k % 2 + 0.26
                        dve.wait_ge(sem("s_hi_done"), k + 1)
                        nc.vector.tensor_tensor(s_lo[:, k, :], gx[:, k % 2, :], s_hi[:, k, :].bitcast(F32),
                                                ALU.subtract).then_inc(sem("s_lo_done"), 1)

                def merge():
                    yield n_proj + 12 - 0.02
                    for k in range(8):
                        dve.wait_ge(sem("y_hi_done"), k + 1)
                        nc.vector.tensor_tensor(y_lo[:, k, :], qT[:, k, :], y_hi[:, k, :].bitcast(F32), ALU.subtract).then_inc(sem("y_lo_done"), 1)

                def rstd_rows():
                    yield 0.5
                    dve.wait_ge(sem("std_done"), 2)
                    v.then(nc.vector.reciprocal(rstd[:, :], rstd[:, :]))
                    nc.vector.nop().then_inc(sem("rstd_done"), 1)

                def mlstm():
                    yield 1.1
                    dve.wait_ge(sem("row_in"), 64)
                    v.do(nc.vector.tensor_scalar(i_row[:, :], i_row[:, :], bif[:, 0:1], None, ALU.add))
                    v.do(nc.vector.tensor_scalar(rA[:, :], f_row[:, :], bif[:, 1:2], 0.0, ALU.add, ALU.min))
                    v.then(nc.vector.tensor_scalar(rB[:, :], f_row[:, :], bif[:, 1:2], None, ALU.add))
                    v.then(nc.vector.scalar_tensor_tensor(rB[:, :], rB[:, :], -1.0, rB[:, :], ALU.mult, ALU.min))
                    nc.vector.nop().then_inc(sem("f_ready"), 1)
                    yield 1.8
                    dve.wait_ge(sem("ln_done"), 1)
                    v.then(nc.vector.tensor_tensor(rA[:, :], rA[:, :], rB[:, :], ALU.subtract))
                    v.then(nc.vector.tensor_tensor_scan(b_row[:, :], scan[:, 0, :], rA[:, :], 0.0, ALU.mult, ALU.add))
                    yield 2.1
                    v.then(nc.vector.tensor_tensor(rA[:, :], i_row[:, :], b_row[:, :], ALU.subtract))
                    v.then(nc.vector.tensor_copy(rB[:, :], rA[:, :]))
                    v.do(nc.vector.tensor_scalar(rB[:, 0:1], rB[:, 0:1], 0.0, None, ALU.max))
                    v.then(nc.vector.tensor_tensor(rB[:, TP:T:TB], rB[:, TP:T:TB], m0_row[:, :], ALU.max))
                    yield 2.6
                    v.then(nc.vector.tensor_tensor_scan(g_row[:, :], scan[:, 1, :], rB[:, :], 0.0, ALU.add, ALU.max))
                    v.then(nc.vector.tensor_tensor(m_row[:, :], b_row[:, :], g_row[:, :], ALU.add))
                    nc.vector.nop().then_inc(sem("rows_done"), 1)
                    yield 3.1
                    gsm = g_row[:, TP:T].rearrange("h (b t) -> h b t", t=TB)
                    v.do(nc.vector.tensor_tensor(tails[:, 0:TS].rearrange("h (b t) -> h b t", t=TB),
                                                 m0_row[:, :].unsqueeze(2).broadcast_to([HA, NB, TB]), gsm, ALU.subtract))
                    v.do(nc.vector.tensor_tensor(tails[:, TS:2 * TS].rearrange("h (b t) -> h b t", t=TB),
                                                 rA[:, TP:T].rearrange("h (b t) -> h b t", t=TB),
                                                 gsm[:, :, TB - 1:TB].broadcast_to([HA, NB, TB]), ALU.subtract))
                    v.then(nc.vector.tensor_tensor(tails[:, 2 * TS:], m0_row[:, :], g_row[:, TP + TB - 1:T:TB], ALU.subtract))
                    nc.vector.nop().then_inc(sem("rows_done"), 1)
                    yield 5.2
                    dve.wait_ge(sem("bytok_done"), 1)
                    dve.wait_ge(sem("g_ev"), HA)
                    v.then(nc.vector.tensor_tensor(ws[:, :].rearrange("p (i h) -> p i h", h=HA),
                                                   by_tok[:, 0:16].rearrange("p (i h) -> p i h", h=HA),
                                                   G[:, :, TP - 1].unsqueeze(1).broadcast_to([P, NT, HA]), ALU.add))
                    nc.vector.nop().then_inc(sem("ws_arg"), 1)

                    def arg(u):
                        h, i = divmod(u, NT)
                        if u >= 2:
                            dve.wait_ge(sem("pt_done"), u - 1)
                        nc.vector.tensor_tensor(W[:, u % 2, 0:P], G[:, h, P * i:P * (i + 1)], con[:, C_CM:C_CM + P],
                                                ALU.add).then_inc(sem("w_arg"), 1)

                    def normal_a(h):
                        dve.wait_ge(sem("a_o"), h + 1)
                        o = acc[:, 7, 0:NT * (HD + 1)].rearrange("p (i c) -> p i c", c=HD + 1)
                        v.then(nc.vector.tensor_copy(den[:, 0:NT], o[:, :, HD]))
                        v.then(nc.vector.scalar_tensor_tensor(den[:, 0:NT], den[:, 0:NT], -1.0, den[:, 0:NT], ALU.mult, ALU.max))
                        v.then(nc.vector.tensor_tensor(den[:, 0:NT], den[:, 0:NT], e_m[:, h:16:HA], ALU.max))
                        v.then(nc.vector.reciprocal(den[:, 0:NT], den[:, 0:NT]))
                        v.then(nc.vector.tensor_tensor(hA[:, 0:NT, h, :], o[:, :, 0:HD],
                                                       den[:, 0:NT].unsqueeze(2).broadcast_to([P, NT, HD]), ALU.mult))
                        if h >= 2:
                            dve.wait_ge(sem(f"st_stored{h % 2}"), 32 * (h // 2))
                        c = NT * (HD + 1)
                        nc.vector.tensor_copy(st_o[:, h % 2, :], acc[0:HD, 7, c:c + HD + 1]).then_inc(sem("stp_ev"), 1)

                    yield T_ML - 0.2
                    dve.wait_ge(sem("ws_done"), 1)
                    arg(0)
                    for h in range(HA):
                        if h >= 1:
                            yield T_ML + h + 0.02
                            normal_a(h - 1)
                        for i in range(NT):
                            u = NT * h + i
                            yield T_ML + h + (0.1, 0.2, 0.4, 0.55)[i]
                            if u + 1 < HA * NT:
                                arg(u + 1)
                            if i == 0:
                                if h >= 1:
                                    dve.wait_ge(sem("a_o"), h)
                                nc.vector.tensor_tensor(kw[:, :, :], ka_tok[:, 0:NT, HD * h:HD * (h + 1)],
                                                        ws[:, h:16:HA].unsqueeze(2).broadcast_to([P, NT, HD]), ALU.mult).then_inc(sem("kw_done"), 1)
                            dve.wait_ge(sem("w_done"), u + 1)
                            dve.wait_ge(sem("a_s"), u + 1)
                            n = TP - P * i
                            nc.vector.tensor_tensor(PT[:, A_OFF[i]:A_OFF[i] + n], acc[:, 3 + u % 3, 0:n],
                                                    W[:, u % 2, 0:n], ALU.mult).then_inc(sem("pt_done"), 1)
                    yield T_MS + 0.02
                    normal_a(HA - 1)
                    dve.wait_ge(sem("qpa_zero"), 1)
                    for h in range(HA):
                        p = par(h)
                        at = QpA[p:p + HD, h // 2, 0, 0:1]
                        v.do(nc.vector.tensor_copy(
                            bass.AP(at.tensor, at.offset, [at.ap[0], [TS + TB, NB], [1, TB]]),
                            qT[p:p + HD, h // 2, TP:T].rearrange("p (b t) -> p b t", t=TB)))
                    v.sync()
                    nc.vector.nop().then_inc(sem("qp_done"), 1)
                    yield T_MS + 0.3
                    SPT, Swt = W[0:TS, 0, 0:HA * TS], W[0:TS, 1, 0:HA * TS]
                    dve.wait_ge(sem("sg_mm"), 1)
                    dve.wait_ge(sem("pt_done"), HA * NT)
                    nc.vector.tensor_tensor(Swt.rearrange("p (h t) -> p h t", t=TS),
                                            acc[0:TS, 3, 0:HA * TS].rearrange("p (h t) -> p h t", t=TS),
                                            con[0:TS, C_SM:C_SM + TS].unsqueeze(1).broadcast_to([TS, HA, TS]),
                                            ALU.add).then_inc(sem("sw_arg"), 1)
                    v.do(nc.vector.tensor_tensor(kws[:, :].rearrange("p (h d) -> p h d", d=HD),
                                                 ka_tok[0:TS, NT, :].rearrange("p (h d) -> p h d", d=HD),
                                                 by_tok[0:TS, 44:48].unsqueeze(2).broadcast_to([TS, HA, HD]), ALU.mult))
                    yield T_MS + 0.6
                    dve.wait_ge(sem("sw_done"), 1)
                    dve.wait_ge(sem("pe_order"), 2)
                    nc.vector.tensor_tensor(SPT, acc[0:TS, 4, 0:HA * TS], Swt, ALU.mult).then_inc(sem("spt_done"), 1)
                    yield T_MS + 1.2
                    dve.wait_ge(sem("so_mm"), 1)
                    v.then(nc.vector.tensor_copy(oA[:, :], acc[0:TS, 5, 0:HA * (HD + 1)]))
                    for h in range(HA):
                        c = h * (HD + 1)
                        v.do(nc.vector.scalar_tensor_tensor(oA[:, c:c + HD + 1], acc[0:TS, 6, c:c + HD + 1],
                                                            by_tok[0:TS, 40 + h:41 + h], oA[:, c:c + HD + 1], ALU.mult, ALU.add))
                    v.sync()
                    o = oA[:, :].rearrange("p (h c) -> p h c", c=HD + 1)
                    v.then(nc.vector.scalar_tensor_tensor(den[0:TS, 0:HA], o[:, :, HD], -1.0, o[:, :, HD], ALU.mult, ALU.max))
                    v.then(nc.vector.tensor_tensor(den[0:TS, 0:HA], den[0:TS, 0:HA], e_m[0:TS, 16:20], ALU.max))
                    v.then(nc.vector.reciprocal(den[0:TS, 0:HA], den[0:TS, 0:HA]))
                    dve.wait_ge(sem("ha_zero"), 1)
                    v.then(nc.vector.tensor_tensor(hA[0:TS, NT], o[:, :, 0:HD], den[0:TS, 0:HA].unsqueeze(2).broadcast_to([TS, HA, HD]), ALU.mult))
                    nc.vector.nop().then_inc(sem("oa_read"), 1)
                    yield T_MS + 1.6
                    dve.wait_ge(sem("dc_mm"), 1)
                    v.then(nc.vector.tensor_scalar(dcy[:, :, :], acc[:, 3, 0:2 * NB].rearrange("p (a b) -> p a b", b=NB), -1.0, None, ALU.mult))
                    for h in range(HA):
                        p = par(h)
                        yield T_MS + 1.65 + 0.5 * h
                        if h >= 1:
                            dve.wait_ge(sem("sst_mm"), h)
                        v.then(nc.vector.tensor_tensor(Vb[:, :, :], va_tok[0:TS, NT, h, :].unsqueeze(1).broadcast_to([TS, NB, HD + 1]),
                                                       con[0:TS, C_BM:C_BM + NB].unsqueeze(2).broadcast_to([TS, NB, HD + 1]), ALU.mult))
                        nc.vector.nop().then_inc(sem("vb_done"), 1)
                        cn = C0n[p:p + HD, :, h // 2, :]
                        v.then(nc.vector.tensor_tensor(cn, cn, dcy[p:p + HD, h // 2, :].unsqueeze(2).broadcast_to([HD, NB, HD + 1]), ALU.mult))
                        yield T_MS + 2.1 + 0.5 * h
                        dve.wait_ge(sem("sst_mm"), h + 1)
                        for half in range(2):
                            v.do(nc.vector.tensor_tensor(
                                cn[:, 4 * half:4 * half + 4], cn[:, 4 * half:4 * half + 4],
                                acc[p:p + HD, 4 + half, 0:4 * (HD + 1)].rearrange("p (b c) -> p b c", c=HD + 1), ALU.add))
                        v.sync()
                        nc.vector.nop().then_inc(sem("cn_done"), 1)
                    yield T_MS + 3.65
                    hh = hA[:, :, :, :].rearrange("p i h d -> p (i h) d")
                    v.then(nc.vector.tensor_tensor(hsq[:, :, :], hh, hh, ALU.mult))
                    v.then(nc.vector.tensor_reduce(rs[:, :], hsq[:, :, :], AXX, ALU.add))
                    nc.vector.nop().then_inc(sem("rs_arg"), 1)
                    yield T_MS + 4.2
                    dve.wait_ge(sem("rs_std"), 1)
                    v.then(nc.vector.reciprocal(rs[:, :], rs[:, :]))
                    v.then(nc.vector.tensor_tensor(hh, hh, rs[:, :].unsqueeze(2).broadcast_to([P, (NT + 1) * HA, HD]), ALU.mult))
                    nc.vector.nop().then_inc(sem("hn_done"), 1)
                    yield T_MS + 4.7
                    dve.wait_ge(sem("oa_done"), 1)
                    for pr in range(2):
                        dve.wait_ge(sem("ya_tr"), pr + 1)
                        for b, c0, c1 in ((3 + 2 * pr, 0, TP), (4 + 2 * pr, TP, T)):
                            nc.vector.scalar_tensor_tensor(qT[:, pr, c0:c1], acc[:, b, 0:c1 - c0], vecs[:, 24 + pr:25 + pr],
                                                           oaT[:, pr, c0:c1], ALU.mult, ALU.mult).then_inc(sem("ya_done"), 1)

                def biased(u):
                    for n in unit_segs[u]:
                        _, i, h, k0, off = segs[n]
                        w = P * (i + 1 - k0)
                        if n == 0:
                            dve.wait_ge(sem("ttb_in"), 16)
                            dve.wait_ge(sem("a_out"), 160)
                            for b in range(2):
                                dve.wait_ge(sem(f"st_stored{b}"), 16 * HA)
                        if u == ND:
                            dve.wait_ge(sem("ttc_in"), 16)
                        dve.wait_ge(sem("s_mm"), n + 1)
                        if n == unit_segs[u][0]:
                            if u >= ND:
                                dve.wait_ge(sem("pt_tr"), unit_segs[max(u - 5, ND - 1)][-1] + 1)
                            elif u >= 2:
                                dve.wait_ge(sem("pt_tr"), unit_segs[u - 2][-1] + 1)
                        c0 = P * (NT - 1 - i + k0)
                        nc.vector.tensor_tensor(scores_in(u)[:, off:off + w], acc[:, 3 + n % 3, 0:w],
                                                bias_of(h, c0, w), ALU.add).then_inc(sem("s_used"), 1)
                    dve.wait_ge(sem("s_used"), unit_segs[u][-1] + 1)
                    if u >= 4:
                        dve.wait_ge(sem("e_done"), u - 3)
                    nc.vector.tensor_reduce(mx[:, u % 4:u % 4 + 1], scores_in(u), AXX, ALU.max,
                                            negate=True).then_inc(sem("m_done"), 1)

                def normal(u):
                    dve.wait_ge(sem("e_done"), u + 1)
                    v.then(nc.vector.reciprocal(dn[:, u % 4:u % 4 + 1], dn[:, u % 4:u % 4 + 1]))
                    nc.vector.tensor_scalar(scores_in(u), scores_in(u), dn[:, u % 4:u % 4 + 1], None,
                                            ALU.mult).then_inc(sem("p_done"), 1)

                def collect(n):
                    _, i, h, k0, off = segs[n]
                    p = par(h)
                    dve.wait_ge(sem("o_mm"), n + 1)
                    nc.vector.tensor_copy(qT[p:p + HD, 2 + h // 2, P * i:P * (i + 1)], acc[p:p + HD, 7, 0:P]).then_inc(sem("o_ev"), 1)

                def attention():
                    for u in range(ND + 1):
                        if u < ND:
                            yield unit_time(u, 4 / 16)
                            biased(u)
                        if u >= 1:
                            yield T_DIL + u + 8 / 16
                            collect(unit_segs[u - 1][0])
                            yield T_DIL + u + 12 / 16
                            collect(unit_segs[u - 1][1])
                        if u < ND:
                            yield unit_time(u, 14 / 16)
                            normal(u)
                        if u >= 1:
                            yield T_DIL + u + 1
                            collect(unit_segs[u - 1][2])
                    for c in range(NU - ND + 3):
                        u = ND + c
                        if c < NU - ND:
                            yield unit_time(u, 0.3)
                            biased(u)
                        if 3 <= c:
                            yield unit_time(u, 0.5)
                            collect(unit_segs[u - 3][0])
                        if 1 <= c < NU - ND + 1:
                            yield unit_time(u, 0.6)
                            normal(u - 1)

                def sample():
                    yield T_SA + 0.1
                    dve.wait_ge(sem("tok_done"), 2 * len(turns))
                    nc.vector.tensor_copy(kTn[:, :, :], kT[:, 2:8, TP:T]).then_inc(sem("new4"), 1)
                    nc.vector.tensor_copy(vn[:, :], v_tok[0:TS, NT, :]).then_inc(sem("new4"), 1)
                    dve.wait_ge(sem("zero4"), 1)
                    dve.wait_ge(sem("rb4_in"), 16)
                    for h in range(2):
                        p = HD * h
                        v.do(nc.vector.tensor_copy(Qs[p:p + HD, :, TS * h:TS * (h + 1)], qT[p:p + HD, 2:8, TP:T]))
                    for t in range(TB):
                        v.do(nc.vector.tensor_copy(RBs[:, t, :, :].rearrange("p h (b t) -> p h b t", t=TB)[:, :, :, t],
                                                   rb4[:, :].unsqueeze(2).broadcast_to([33, HEADS, NB])))
                    v.sync()
                    nc.vector.nop().then_inc(sem("q4"), 1)
                    yield T_SA + 1.1
                    dve.wait_ge(sem("new_mm"), 6)
                    dve.wait_ge(sem("o_mm"), len(segs))
                    v.then(nc.vector.tensor_tensor(S4[:, :, 256:288], acc[:, 2, 0:96].rearrange("p (g n) -> p g n", n=TS),
                                                   con[:, C_NEW:C_NEW + TS].unsqueeze(1).broadcast_to([P, 3, TS]), ALU.add))
                    nc.vector.nop().then_inc(sem("new_read"), 1)

                def queries():
                    for q in range(6):
                        yield T_SA + 0.25 + q / 2
                        if q == 0:
                            dve.wait_ge(sem("qpad_zero"), 1)
                        if q >= 2:
                            dve.wait_ge(sem("qk4"), NB * (q - 1))
                        for h in range(2):
                            p = HD * h
                            at = Qpad[p:p + HD, q % 2, 0, TS * h:TS * h + 1]
                            v.do(nc.vector.tensor_copy(
                                bass.AP(at.tensor, at.offset, [at.ap[0], [2 * TS + TB, NB], [1, TB]]),
                                qT[p:p + HD, 2 + q, TP:T].rearrange("p (b t) -> p b t", t=TB)))
                        v.sync()
                        nc.vector.nop().then_inc(sem("qpad_done"), 1)

                def sample_softmax():
                    for half in range(2):
                        yield T_SA + (2.6, 4.1)[half]
                        lo = HD * half
                        dve.wait_ge(sem("qk4"), 3 * NB * (half + 1))
                        r = slice(lo, lo + HD)
                        if half == 0:
                            v.do(nc.vector.memset(S4[r, 0, P:256], NEG))
                            v.do(nc.vector.tensor_copy(S4[r, 0, 0:P], acc[r, 3, 0:P]))
                            v.then(nc.vector.tensor_copy(S4[r, 1:3, 0:256], acc[r, 4:6, 0:256]))
                        else:
                            v.then(nc.vector.tensor_copy(S4[r, :, 0:256], acc[r, 3:6, 0:256]))
                        v.then(nc.vector.tensor_reduce(mx4[r, 0:3], S4[r, :, :], AXX, ALU.max))
                        if half == 0:
                            v.then(nc.vector.tensor_reduce(mx4[r, 3:4], mx4[r, 0:3], AXX, ALU.max))
                            v.then(nc.vector.tensor_copy(mx4[r, 0:3], mx4[r, 3:4].broadcast_to([HD, 3])))
                        v.then(nc.vector.tensor_scalar(mx4[r, 0:3], mx4[r, 0:3], -1.0, None, ALU.mult))
                        nc.vector.nop().then_inc(sem("mx4"), 1)
                        yield T_SA + (3.1, 4.55)[half]
                        dve.wait_ge(sem("e4"), 3 * (half + 1))
                        if half == 0:
                            v.then(nc.vector.tensor_reduce(dn4[r, 3:4], dn4[r, 0:3], AXX, ALU.add))
                            v.then(nc.vector.tensor_copy(dn4[r, 0:3], dn4[r, 3:4].broadcast_to([HD, 3])))
                        v.then(nc.vector.reciprocal(dn4[r, 0:3], dn4[r, 0:3]))
                        nc.vector.tensor_tensor(S4[r, :, :], S4[r, :, :], dn4[r, 0:3].unsqueeze(2).broadcast_to([HD, 3, 288]),
                                                ALU.mult).then_inc(sem("p4"), 1)

                def sample_collect():
                    for half in range(2):
                        yield T_SA + (5.1, 5.95)[half]
                        dve.wait_ge(sem("o4"), 3 * (half + 1))
                        if half == 0:
                            dve.wait_ge(sem("qk4"), 6 * NB)
                        for h in range(2):
                            p = HD * h
                            nc.vector.tensor_copy(qT[p:p + HD, 2 + 3 * half:5 + 3 * half, TP:T],
                                                  acc[p:p + HD, O4_BANK[half], 0:192].rearrange("p (q n) -> p q n", n=2 * TS)[:, :, TS * h:TS * (h + 1)]
                                                  ).then_inc(sem("y4"), 1)

                dve.wait_ge(sem("vecs_done"), 1)
                for i in range(NT + 2):
                    if i < NT + 1:
                        n = P if i < NT else TS
                        dve.wait_ge(sem("x_ev"), i + 1)
                        if i >= 2:
                            dve.wait_ge(sem("h_lo_done"), i - 1)
                        nc.vector.tensor_tensor(xg[:, i % 2, :, 0:n], xT[:, :, P * i:P * i + n],
                                                vecs[:, 0:KD].unsqueeze(2).broadcast_to([P, KD, n]), ALU.mult).then_inc(sem("xg_made"), 1)
                    if i >= 1:
                        n = P if i - 1 < NT else TS
                        dve.wait_ge(sem("h_hi_done"), i)
                        c = P * (i - 1)
                        nc.vector.tensor_tensor(h_lo[:, :, c:c + n], xg[:, (i - 1) % 2, :, 0:n], h_hi[:, :, c:c + n].bitcast(F32),
                                                ALU.subtract).then_inc(sem("h_lo_done"), 1)
                    if i == 3:
                        split_lo(dve, 0)

                side = Side(rstd_rows(), mlstm(), attention(), sample(), queries(), sample_softmax(), sample_collect(), merge(), feed())
                for w in range(n_all):
                    side.until(w + 0.25)
                    if w + 1 < n_all:
                        split_lo(dve, w + 1)
                    side.until(w + 0.5)
                    evac(w, 0)
                    side.until(w + 1)
                    evac(w, 1)
                dve.wait_ge(mm_done, mm_at[n_all])
                nc.vector.memset(rt[:, :], 1.0).then_inc(sem("rt_set"), 1)
                dve.wait_ge(sem("rt_std"), 2)
                nc.vector.reciprocal(rt[:, :], rt[:, :]).then_inc(sem("rt_done"), 1)
                dve.wait_ge(sem("rt_done"), 1)
                for i in range(NT + 1):
                    n = P if i < NT else TS
                    dve.wait_ge(sem("y_tr"), i + 1)
                    nc.vector.tensor_scalar(o_st[0:n, i, 512:D], acc[0:n, 2 * (i % 3) + 1, :], rt[0:n, i:i + 1], None,
                                            ALU.mult).then_inc(sem("y_right"), 1)

    return nc


OUT_SHAPES = [
    (1, TP, D), (NB, TB, D), (1, 1, HA, HD, HD), (1, 1, HA, HD), (1, 1, HA),
    (1, NB, HA, HD, HD), (1, NB, HA, HD), (1, NB, HA),
    (1, 1, 128, 2, 2, HD), (1, 1, 512, 2, 2, HD), (1, 1, 512, 2, 2, HD),
    (1, NB, 128, 2, 2, HD), (1, NB, 256, 2, 2, HD), (1, NB, 256, 2, 2, HD),
    (1, 1, TP, 6, HD), (1, 1, TP, 6, HD), (1, NB, TB, 6, HD), (1, NB, TB, 6, HD)]


def kernel(**inputs):
    import concourse.bacc as bacc
    from concourse.bass_utils import run_bass_kernel_spmd

    nc = bacc.Bacc("TRN2", target_bir_lowering=False, num_devices=1)
    arrays = {name: np.ascontiguousarray(a) for name, a in inputs.items()}
    arrays.update(con=wide_constants(), rowc=row_constants(), scan=scan_constants(), oh=bias_selectors())
    aps = {name: nc.dram_tensor("in_" + name, a.shape, mybir.dt.from_np(a.dtype), kind="ExternalInput").ap()
           for name, a in arrays.items()}
    outs = [nc.dram_tensor(f"out_{i}", shape, F32, kind="ExternalOutput").ap()
            for i, shape in enumerate(OUT_SHAPES)]
    aps["tab"] = nc.dram_tensor("tab", (1, HEADS * REV), F32, kind="Internal").ap()
    aps["rev"] = nc.dram_tensor("rev", (P, HEADS * REV), F32, kind="Internal").ap()
    build(nc, aps, outs, aps)
    got = run_bass_kernel_spmd(nc, [{"in_" + n: a for n, a in arrays.items()}], core_ids=[0]).results[0]
    return tuple(got[f"out_{i}"] for i in range(len(OUT_SHAPES)))
```

```python
from contextlib import ExitStack

import numpy as np

import concourse.bass as bass
from concourse import mybir

ALU = mybir.AluOpType
ACT = mybir.ActivationFunctionType
AXX = mybir.AxisListType.X
F32 = mybir.dt.float32
F32R = mybir.dt.float32r

P = 128
D = 1024
KD = D // P
TP, NB, TB = 512, 8, 4
TS = NB * TB
T = TP + TS
HALF = (256, T - 256)
NT = TP // P
HD = 64
HA = 4
D_FF = 2816
KF = D_FF // P
N_QKV = 1032
N_GATE = 3336
REV = 640
NEG = -1e30
EPS = 1e-6
SCALE = HD ** -0.5
HEADS = 12


def kind_of(head):
    return 1 + head // 2 if head < 6 else 0


def rel_bucket(dist):
    dist = np.maximum(dist, 0)
    ratio = np.log(np.maximum(dist, 1).astype(np.float64) / 16) / np.log(2048 / 16)
    large = np.minimum(16 + (ratio * 16).astype(np.int64), 31)
    return np.where(dist < 16, dist, large)


def bias_selectors():
    dist = TP - 1 - np.arange(REV)
    out = np.zeros((33, 4, REV), np.float32)
    for kind in range(4):
        ok = dist >= 0
        if kind:
            win, dil = ((128, 1), (512, 4), (2048, 16))[kind - 1]
            ok = ok & (dist <= win) & (dist % dil == 0)
        out[rel_bucket(dist), kind, np.arange(REV)] = ok
        out[32, kind] = np.where(ok, 0.0, NEG)
    return out


def sample_selectors():
    sel = bias_selectors()
    out = np.zeros((TB, 32, 4, 2 * P + TB), np.float32)
    for t in range(TB):
        u0 = TP - 1 - 2 * P - t
        out[t] = sel[:32, :, u0:u0 + 2 * P + TB]
    return out.reshape(TB * 32, 4, 2 * P + TB)


def sample_masks():
    sel = bias_selectors()[32]
    out = np.full((2, 2, NB, TB, 3, 2 * P + TS), NEG, np.float32)
    for half in range(2):
        for g in range(3):
            w = P if half == 0 and g == 0 else 2 * P
            row = sel[0 if half else 1 + g]
            for t in range(TB):
                out[half, :, :, t, g, 0:w] = row[TP - 1 - w - t:TP - 1 - t]
                for b in range(NB):
                    out[half, :, b, t, g, 2 * P + TB * b:2 * P + TB * (b + 1)] = row[TP - 1 - t:TP - 1 - t + TB]
    return out.reshape(P, 3, 2 * P + TS)


C_ID, C_CM, C_SM, C_BM = 0, 128, 256, 288
C_W = 296
R_SEL, R_W = 0, HA * P


def wide_constants():
    out = np.zeros((P, C_W), np.float32)
    r = np.arange(P)
    out[:, C_ID:C_ID + P] = np.eye(P)
    out[:, C_CM:C_CM + P] = np.where(r[None, :] >= r[:, None], 0.0, NEG)
    s = np.arange(TS)
    same = (s[:, None] // TB == s[None, :] // TB) & (s[None, :] >= s[:, None])
    out[:TS, C_SM:C_SM + TS] = np.where(same, 0.0, NEG)
    out[:TS, C_BM:C_BM + NB] = s[:, None] // TB == np.arange(NB)[None, :]
    return out


def row_constants():
    out = np.zeros((HA, R_W), np.float32)
    for h in range(HA):
        out[h, R_SEL + P * h:R_SEL + P * (h + 1)] = -1.0
    return out


def scan_constants():
    out = np.zeros((HA, 2, T), np.float32)
    starts = np.concatenate([[0], TP + TB * np.arange(NB)])
    out[:, 0] = 1.0
    out[:, 0, starts] = 0.0
    out[:, 1, starts] = NEG
    return out


class Steps:

    def __init__(self, eng, sem):
        self.eng, self.sem, self.n = eng, sem, 0

    def do(self, ins):
        ins.then_inc(self.sem, 1)
        self.n += 1
        return self.n

    def sync(self):
        self.eng.wait_ge(self.sem, self.n)

    def then(self, ins):
        self.do(ins)
        self.sync()


class Side:

    END = 1e9

    def __init__(self, *programs):
        self.programs = [[next(p, self.END), p] for p in programs]

    def until(self, time):
        while True:
            first = min(self.programs, key=lambda p: p[0])
            if first[0] > time:
                return
            first[0] = next(first[1], self.END)


def build(nc, I, O, X):
    with ExitStack() as ctx:
        low = nc.sbuf_base
        low += -low % 64
        top = nc.sbuf_top
        ctx.enter_context(nc.sbuf_tensor("whole", [P, (top - low) // 4 - 16], F32))
        sems = {}

        def sem(name):
            if name not in sems:
                sems[name] = ctx.enter_context(nc.semaphore(name))
            return sems[name]

        class Map:

            def __init__(self, at, size=None):
                self.at = at
                self.end = top - 64 if size is None else at + size

            def __call__(self, name, shape, dt=F32):
                n = 4 * int(np.prod(shape[1:]))
                assert self.at + n <= self.end, (name, self.at, n, self.end)
                t = nc.alloc_sbuf_tensor_at(name, shape, dt, offset=self.at)
                self.at += n + (-n % 64)
                return t

        keep = Map(low)
        con = keep("con", [P, C_W])
        ident = con[:, C_ID:C_ID + P]
        rowc = keep("rowc", [HA, R_W])
        vecs = keep("vecs", [P, 26])
        ones = keep("ones", [P, P])
        eps = keep("eps", [P, 1])
        one = keep("one", [P, 1])
        spare = keep("spare", [P, 1])
        rstd = keep("rstd", [P, T])
        ssq = keep("ssq", [P, T])
        xT = keep("xT", [P, KD, T])
        h_hi = keep("h_hi", [P, KD, T], F32R)
        h_lo = keep("h_lo", [P, KD, T], F32R)
        raw = keep("raw", [P, 3, 2048])
        w_hi = keep("w_hi", [P, 2, 1024], F32R)
        w_lo = keep("w_lo", [P, 2, 1024], F32R)
        sq_at = keep.at
        sq = keep("sq", [P, 2, T])
        region = keep.at

        TB4 = 4 * T
        a_q = region
        a_g0 = a_q + 8 * TB4
        a_k = a_g0 + 13824
        a_v = a_k + 8 * TB4
        a_a = a_v + 15360
        a_b = a_a + 14720
        a_s = a_b + 12288
        qT = Map(a_q)("qT", [P, 8, T])
        m = Map(a_g0, 13824)
        i_row, f_row = m("i_row", [HA, T]), m("f_row", [HA, T])
        v_st = m("v_st", [P, 2, T])
        k_st = m("k_st", [P, 2, NT + 1, P])
        gs = [Map(a_g0)("gs0", [P, 6, T]), Map(a_k)("gs1", [P, 6, T])]
        kT = Map(a_k)("kT", [P, 8, T])
        v_tok = Map(a_v)("v_tok", [P, NT + 1, HEADS * HD])
        m = Map(a_a, 14720)
        oaT = m("oaT", [P, 2, T])
        va_tok = m("va_tok", [P, NT + 1, HA, HD + 1])
        ka_tok = m("ka_tok", [P, NT + 1, HA * HD])
        TTb = Map(a_b)("TTb", [P, 6, TP])
        TTc = Map(a_a)("TTc", [P, 6, TP])
        m = Map(a_s)
        Sb = m("Sb", [P, 2, 1280])
        Sc = Map(a_s)("Sc", [P, 5, TP])
        PTs = m("PTs", [P, 2, TP])
        mx = m("mx", [P, 4])
        dn = m("dn", [P, 4])
        m = Map(a_a)
        x_tok = m("x_tok", [P, NT + 1, D])
        xg = m("xg", [P, 2, KD, P])
        xsq = m("xsq", [P, D])
        diag = m("diag", [P, NT + 1, P])
        ssx = m("ssx", [P, NT + 1])
        vrow = m("vrow", [26, P])
        m = Map(a_v, 15360)
        oh = m("oh", [33, 4, REV])
        rb = m("rb", [33, HEADS])
        tab = Map(a_k + 2 * TB4, 6 * TB4)("tab", [6, 4, REV])
        m = Map(a_v, 15360)
        G = m("G", [P, HA, TP])
        W = m("W", [P, 2, TP])
        kw = m("kw", [P, NT, HD])
        oA = m("oA", [TS, HA * (HD + 1)])
        m = Map(a_b, 12288)
        rA, b_row, g_row = (m(n, [HA, T]) for n in ("rA", "b_row", "g_row"))
        PT = m("PT", [P, 1280])
        rB = f_row
        m = Map(a_s)
        m_row = m("m_row", [HA, T])
        hA = m("hA", [P, NT + 1, HA, HD])
        C0n = m("C0n", [P, NB, 2, HD + 1])
        QpA = m("QpA", [P, 2, NB, TS])
        tails = m("tails", [HA, 2 * TS + NB])
        m0_row = m("m0_row", [HA, NB])
        by_tok = m("by_tok", [P, 48])
        e_m = m("e_m", [P, 20])
        ws = m("ws", [P, 4 * NT])
        den = m("den", [P, 8])
        rs = m("rs", [P, (NT + 1) * HA])
        dcy = m("dcy", [P, 2, NB])
        st_o = m("st_o", [HD, 2, HD + 1])
        bif = m("bif", [HA, 2])
        m = Map(a_q + 5 * TB4, 3 * TB4)
        scan = m("scan", [HA, 2, T])
        Vb = m("Vb", [TS, NB, HD + 1])
        m = Map(a_k + 5 * TB4, 3 * TB4)
        kws = m("kws", [TS, HA * HD])
        hsq = m("hsq", [P, (NT + 1) * HA, HD])
        sel4 = Map(sq_at)("sel4", [P, 4, 2 * P + TB])
        m = Map(a_b, 12288)
        RBs = m("RBs", [P, HEADS, TS])
        kTn = m("kTn", [P, 6, TS])
        Qs = m("Qs", [P, 6, 2 * TS])
        rb4 = m("rb4", [P, HEADS])
        vn = Map(a_b + 8192)("vn", [TS, HEADS * HD])
        PTp = Map(a_b, 8192)("PTp", [P, 2, NB, 2, HD])
        PTn = Map(a_s + 13696, 768)("PTn", [TS, 3, HD])
        Osb = Map(a_k + 6 * TB4, 2 * TB4)("Osb", [HD, 2, 3, P])
        ring = [Map(a_v)("ring0", [P, 16, P]), Map(a_v + 8192)("ring1", [P, 16, P]),
                Map(a_v + 16384)("ring2", [P, 16, P]), Map(a_s)("ring3", [P, 16, P])]
        Qpad = Map(a_k + 6 * TB4, 2 * TB4)("Qpad", [P, 2, NB, 2 * TS])
        KTs = Map(a_s + 8192, 2048)("KTs", [P, 2, 256])
        S4 = Map(a_s + 10240, 4096)("S4", [P, 3, 288])
        mx4 = Map(a_s + 14464)("mx4", [P, 4])
        dn4 = Map(a_s + 14528)("dn4", [P, 4])
        m = Map(a_v)
        y_hi, y_lo = (m(n, [P, 8, T], F32R) for n in ("y_hi", "y_lo"))
        mg_hi = m("mg_hi", [P, KD, T], F32R)
        mt = m("mt", [P, 2, T])
        mg_lo = Map(a_q)("mg_lo", [P, KD, T], F32R)
        m = Map(region)
        s_hi, s_lo = (m(n, [P, KF, T], F32R) for n in ("s_hi", "s_lo"))
        sg = m("sg", [P, 2, T])
        gx = sq
        o_st = Map(region)("o_st", [P, NT + 1, D])
        rt = Map(region + 4 * (NT + 1) * D)("rt", [P, 8])

        acc = ctx.enter_context(nc.psum_tensor("acc", [P, 8, 512], F32))

        def two(ap, half):
            return ap[:, HALF[0] * half:HALF[0] + HALF[1] * half]

        w_in, w_gu, w_dn, w_out = I["w_in"][0], I["w_gate_up"][0], I["w_down"][0], I["w_out"][0]

        def rows(w, k0, k1, c0, n):
            return w[k0 * P:k1 * P, c0:c0 + n].rearrange("(k p) n -> p k n", p=P)

        loads = []
        blocks = []

        def add_load(parts, kts):
            loads.append((parts, 2 * P))
            blocks.extend((len(loads) - 1, kts, 2 * P, j * P) for j in range(2))

        loads.append(([(0, 0, rows(w_in, 0, KD, 1024, 32)), (0, 32, rows(w_in, 0, KD, 1028, 96))], P))
        blocks.append((0, KD, P, 0))
        for c in list(range(0, 1024, 256)) + list(range(N_QKV, N_GATE, 256)):
            add_load([(0, 0, rows(w_in, 0, KD, c, 256))], KD)
        n_proj = len(blocks)

        info = {}

        def gates(j):
            for g in range(3):
                for n in range(2):
                    info[len(blocks) + n] = ("gate", j, 2 * g + n)
                add_load([(0, 0, rows(w_in, 0, KD, N_GATE + g * D + 2 * j * P, 256))], KD)

        def branches(j):
            for n in range(2):
                info[len(blocks) + n] = ("br", 2 * j + n, 0)
            c = 2 * j * P
            add_load([(0, 0, rows(I["w_br_a"][0], 0, 2, c, 256)), (2, 0, rows(I["w_br_b"][0], 0, 3, c, 256)),
                      (5, 0, rows(I["w_br_c"][0], 0, 3, c, 256))], KD)

        gates(0), gates(1), branches(0), gates(2), branches(1), gates(3), branches(2), branches(3)
        n_merge = len(blocks)
        for j in range(0, KD, 2):
            add_load([(0, 0, rows(w_out, 0, KD, j * P, 256))], KD)
        n_wout = len(blocks)
        for j in range(0, KF, 2):
            add_load([(0, 0, rows(w_gu, 0, KD, j * P, 256))], KD)
            add_load([(0, 0, rows(w_gu, 0, KD, D_FF + j * P, 256))], KD)
        n_gu = len(blocks)
        DOWN = ((0, 8), (8, 16), (16, 22))
        for j in range(0, KD, 2):
            for k0, k1 in DOWN:
                add_load([(0, 0, rows(w_dn, k0, k1, j * P, 256))], k1 - k0)
        n_all = len(blocks)
        w_loaded = [sem(f"w_loaded{i}") for i in range(3)]
        loaded_count, seen = [], [0, 0, 0]
        for n, (parts, _) in enumerate(loads):
            seen[n % 3] += 16 * len(parts)
            loaded_count.append(seen[n % 3])
        last_block = {b[0]: w for w, b in enumerate(blocks)}

        groups = []
        mm_at = [0]
        holder, before = {}, {}
        n_sum = 0
        sum_at = {}

        down = {}

        def allot(w):
            nonlocal n_sum
            bank = n_sum % 6 if w >= n_proj + 12 else n_sum % 4 if w < 3 else n_sum % 2
            before[n_sum] = holder.get(bank)
            holder[bank] = n_sum
            n_sum += 1
            return n_sum - 1, bank

        for w in range(n_all):
            sum_at[w] = n_sum
            g = []
            if info.get(w, ("",))[0] == "br":
                for k0, k1 in ((0, 2), (2, 5), (5, 8)):
                    for half in range(2):
                        g.append(allot(w) + (True, True, half, k0, k1))
            elif w < n_gu:
                for half in range(2):
                    g.append(allot(w) + (True, True, half, 0, KD))
            else:
                c, n = divmod((w - n_gu) % 6, 2)
                for half in range(2):
                    if c == 0:
                        down[n, half] = allot(w)
                    g.append(down[n, half] + (c == 0, c == 2, half, 0, DOWN[c][1] - DOWN[c][0]))
            groups.append(g)
            mm_at.append(mm_at[-1] + len(g))
        mm_done, acc_ev, w_hi_done, w_lo_done = sem("mm_done"), sem("acc_ev"), sem("w_hi_done"), sem("w_lo_done")

        def raw_block(w):
            load, kts, ncol, off = blocks[w]
            v = raw[:, load % 3, 0:kts * ncol].rearrange("p (k n) -> p k n", n=ncol)
            return v[:, :, off:off + P]

        def split_block(t, w):
            return t[:, w % 2, 0:blocks[w][1] * P].rearrange("p (k n) -> p k n", n=P)

        def load_weights(sp, n):
            parts, ncol = loads[n]
            if n >= 3:
                sp.wait_ge(w_lo_done, last_block[n - 3] + 1)
            for k0, c0, src in parts:
                k, mcol = src.shape[1], src.shape[2]
                dst = raw[:, n % 3, k0 * ncol:(k0 + k) * ncol].rearrange("p (k n) -> p k n", n=ncol)
                sp.dma_start(dst[:, :, c0:c0 + mcol], src).then_inc(w_loaded[n % 3], 16)

        def split_hi(act, w):
            load = blocks[w][0]
            act.wait_ge(w_loaded[load % 3], loaded_count[load])
            if w >= 2:
                act.wait_ge(mm_done, mm_at[w - 1])
            nc.scalar.activation(split_block(w_hi, w), raw_block(w), ACT.Copy).then_inc(w_hi_done, 1)

        def split_lo(dve, w):
            dve.wait_ge(w_hi_done, w + 1)
            nc.vector.tensor_tensor(split_block(w_lo, w), raw_block(w), split_block(w_hi, w).bitcast(F32),
                                    ALU.subtract).then_inc(w_lo_done, 1)

        def products(pe, side, w, x_hi, x_lo, kx=0, part=None, late=False):
            hi, lo = split_block(w_hi, w), split_block(w_lo, w)
            order = [(g, k) for g in groups[w] for k in range(g[5], g[6])]
            if late:
                order = [o for o in order if o[1] < KD - 1] + [o for o in order if o[1] == KD - 1]
            for place, ((idx, bank, first, last, half, k0, k1), k) in enumerate(order):
                if k == k0 and first and before[idx] is not None:
                    pe.wait_ge(acc_ev, before[idx] + 1)
                side.until(w + place / len(order))
                if part is not None:
                    part(half, kx + k)
                for c, (a, b) in enumerate(((hi, x_hi), (hi, x_lo), (lo, x_hi))):
                    ins = nc.tensor.matmul(acc[:, bank, 0:HALF[half]], a[:, k, :], two(b[:, kx + k, :], half),
                                           start=first and k == k0 and c == 0,
                                           stop=last and k == k1 - 1 and c == 2)
                if k == k1 - 1:
                    ins.then_inc(mm_done, 1)

        def summed(w, n):
            idx, bank = groups[w][n][0:2]
            return idx, acc[:, bank, 0:HALF[groups[w][n][4]]], mm_at[w] + n + 1

        def par(h):
            return HD * (h % 2)


        kinds = [("if", 0)] + [(n, i) for n, c in
                               (("qa", 2), ("ka", 2), ("va", 2), ("oa", 2), ("qb", 3), ("kb", 3), ("vb", 3),
                                ("qc", 3), ("kc", 3), ("vc", 3)) for i in range(c)]
        assert len(kinds) == n_proj
        Q0 = {"a": 0, "b": 2, "c": 5}
        turns = [w for w, (n, _) in enumerate(kinds) if n[0] in "kv"]
        k_stores = [t for t, w in enumerate(turns) if kinds[w][0] in ("kb", "kc")]
        v_turns = [t for t, w in enumerate(turns) if kinds[w][0][0] == "v"]
        (o_yp, o_ys, o_pC, o_pn, o_pm, o_sC, o_sn, o_sm, o_pkv1, o_pkv2, o_pkv3, o_skv1, o_skv2, o_skv3,
         o_pk, o_pv, o_sk, o_sv) = O
        o_pkv, o_skv = (o_pkv1, o_pkv2, o_pkv3), (o_skv1, o_skv2, o_skv3)
        LW = (128, 256, 256)
        caches = (I["cache_dsa_kv1"], I["cache_dsa_kv2"], I["cache_dsa_kv3"])
        k_stored = [sem("k_stored0"), sem("k_stored1")]

        def turned_from(t):
            name, i = kinds[turns[t]]
            return kT[:, Q0[name[1]] + i, :] if name[0] == "k" else v_st[:, v_turns.index(t) % 2, :]

        def token_place(t):
            name, i = kinds[turns[t]]
            if name == "ka":
                v = ka_tok[:, :, P * i:P * (i + 1)]
            elif name == "va":
                v = va_tok[:, :, 2 * i:2 * i + 2, 0:HD]
            elif name[0] == "v":
                c = P * (i + (0 if name == "vb" else 3))
                v = v_tok[:, :, c:c + P]
            else:
                v = k_st[:, k_stores.index(t) % 2]
            return v[:, 0:NT], v[0:TS, NT]

        def store_tok(pool, t):
            pool.wait_ge(sem("tok_done"), 2 * t + 2)
            prompt, sample = token_place(t)
            name, i = kinds[turns[t]]
            s = 0 if name[0] == "k" else 1
            done = k_stored[k_stores.index(t) % 2] if s == 0 else sem("v_stored")
            if name[1] == "b":
                lw = min((128, 512, 2048)[i], TP)
                dst = o_pkv[i][0, 0].rearrange("(i p) s h d -> p i s (h d)", p=P)[:, :, s, :]
                pool.dma_start(dst, prompt[:, NT - lw // P:NT, :]).then_inc(done, 16)
                n = LW[i]
                dst = o_skv[i][0, :, n - TB:n, s].rearrange("b t h d -> b t (h d)")
                pool.dma_start(dst, sample).then_inc(done, 16)
            else:
                o_p, o_s = ((o_pk, o_sk), (o_pv, o_sv))[s]
                dst = o_p[0, 0].rearrange("(i p) h d -> p i (h d)", p=P)[:, :, P * i:P * (i + 1)]
                pool.dma_start(dst, prompt).then_inc(done, 16)
                dst = o_s[0].rearrange("b t h d -> (b t) (h d)")[:, P * i:P * (i + 1)]
                pool.dma_start(dst, sample).then_inc(done, 16)

        dil = [(i, [2 * g + j for g in range(3)]) for i in range(NT) for j in range(2)]
        units = dil + [(i, [h]) for i in range(NT) for h in range(6, HEADS)]
        ND, NU = len(dil), len(units)
        segs, unit_segs, widths = [], [], []
        for u, (i, heads) in enumerate(units):
            off, mine = 0, []
            for h in heads:
                k0 = max(0, i - 1) if kind_of(h) == 1 else 0
                mine.append(len(segs))
                segs.append((u, i, h, k0, off))
                off += P * (i + 1 - k0)
            unit_segs.append(mine)
            widths.append(off)
        T_DIL, T_BLK = 18, 27
        T_ML, T_MS = 8, 12
        T_SA = 33

        def unit_time(u, part):
            return T_DIL + u + part if u < ND else T_BLK + (u - ND + part) / 4

        def scores_in(u):
            return Sb[:, u % 2, 0:widths[u]] if u < ND else Sc[:, (u - ND) % 5, 0:widths[u]]

        def bias_of(h, c0, w):
            return (TTb[:, h] if h < 6 else TTc[:, h - 6])[:, c0:c0 + w]

        NC4 = (1, 2, 2, 2, 2, 2)
        ring_order = [(what, q) for what in "kv" for q in range(6)]
        ring_in = [sem(f"ring_in{i}") for i in range(4)]
        ring_count = []
        for n, (_, q) in enumerate(ring_order):
            ring_count.append((ring_count[n - 4] if n >= 4 else 0) + (16 if q < 3 else 256))

        def ring_tiles(what, q):
            n = ring_order.index((what, q))
            return ring[n % 4], ring_in[n % 4], ring_count[n]

        def turned_p(half, g, c):
            if half == 0:
                return (2, 5 * HD + HD * g) if c == 2 else (2, HD * (2 * g + c - (g > 0)))
            return (2, HD * g) if c == 2 else (6, HD * (2 * g + c))

        O4_BANK = (7, 5)

        def gated_part(k, c):
            return mt[:, c, :] if c < 2 else sq[:, k % 2, :]

        x_order = (0, 1, NT, 2, 3)
        A_OFF = (0, 512, 896, 1152)

        with nc.Block() as blk:
            @blk.sync
            def _(sp):
                def beside():
                    yield 2.6
                    sp.wait_ge(sem("rstd_done"), 2)
                    for h in range(HA):
                        p = par(h)
                        sp.dma_start(C0n[p:p + HD, :, h // 2, 0:HD], I["state_mlstm_C"][0, :, h].rearrange("b k v -> k b v")).then_inc(sem("st_in"), 16)
                        sp.dma_start(C0n[p:p + HD, :, h // 2, HD], I["state_mlstm_n"][0, :, h].rearrange("b k -> k b"),
                                     allow_slow_non_contiguous=True).then_inc(sem("st_in"), 16)
                    for g in range(3):
                        yield 4 + g
                        n = LW[g]
                        sp.dma_start(o_skv[g][0, :, 0:n - TB].rearrange("b w s h d -> b (w s h d)"),
                                     caches[g][0, :, TB:n].rearrange("b w s h d -> b (w s h d)")).then_inc(sem("moved_up"), 16)
                    yield T_BLK + 1
                    pages = [sp.value_load(I["page_table"][n // 2:n // 2 + 1, n % 2:n % 2 + 1], min_val=0, max_val=19)
                             for n in range(16)]
                    when = (0.4, 0.41, 0.42, 0.43, 1.55, 2.05, 2.55, 3.05, 3.55, 4.05, 4.3, 4.5)
                    for n, time in enumerate(when):
                        yield T_SA + time
                        what, q = ring_order[n]
                        if n < 4:
                            sp.wait_ge(sem("o_mm"), len(segs))
                            sp.wait_ge(sem("new4"), 2)
                            if n == 0:
                                sp.dma_start(S4[:, :, :], X["mask4"]).then_inc(sem("mask_in"), 16)
                        else:
                            was, qq = ring_order[n - 4]
                            if was == "k":
                                sp.wait_ge(sem("kt_tr"), NB * (qq + 1))
                            else:
                                sp.wait_ge(sem("o4"), qq + 1)
                        s = "kv".index(what)
                        if q < 3:
                            c = NB * LW[q] // P
                            src = caches[q].rearrange("o b (c p) s h d -> p (o b c) s (h d)", p=P)
                            sp.dma_start(ring[n % 4][:, 0:c, :], src[:, :, s, :]).then_inc(ring_in[n % 4], 16)
                        else:
                            cache = I["cache_moba_k"] if what == "k" else I["cache_moba_v"]
                            for m, page in enumerate(pages):
                                src = cache[0, bass.ds(page, 1)].rearrange("o p h d -> p (o h d)")
                                sp.dma_start(ring[n % 4][:, m, :], src[:, P * (q - 3):P * (q - 2)]).then_inc(ring_in[n % 4], 16)

                side = Side(beside())
                sp.dma_start(con[:, C_ID:C_ID + P], X["con"][:, C_ID:C_ID + P]).then_inc(sem("con_in"), 16)
                sp.dma_start(vrow[0:8, :], I["norm_mix"].rearrange("o (k p) -> (o k) p", p=P)).then_inc(sem("vec_in"), 16)
                for i in (0, 1, NT, 2, 3):
                    if i < NT:
                        sp.dma_start(x_tok[:, i, :], I["x_prompt"][0, P * i:P * (i + 1), :]).then_inc(sem(f"x_in{i}"), 16)
                    else:
                        sp.dma_start(x_tok[0:TS, i, :], I["x_sample"].rearrange("b t d -> (b t) d")).then_inc(sem(f"x_in{i}"), 16)
                    if i == 0:
                        sp.dma_start(vrow[8:16, :], I["norm_ffn"].rearrange("o (k p) -> (o k) p", p=P)).then_inc(sem("vec_in"), 16)
                        sp.dma_start(vrow[16:24, :], I["norm_final"].rearrange("(k p) -> k p", p=P)).then_inc(sem("vec_in"), 16)
                        sp.dma_start(vrow[24:26, :], I["mlstm_gain"].rearrange("o (k p) -> (o k) p", p=P)).then_inc(sem("vec_in"), 16)
                    if i == 1:
                        load_weights(sp, 0)
                sp.dma_start(con[:, P:C_W], X["con"][:, P:C_W]).then_inc(sem("masks_in"), 16)
                load_weights(sp, 1)
                sp.dma_start(bif[:, :], I["b_if"].rearrange("o (c h) -> (o h) c", c=2),
                             allow_slow_non_contiguous=True).then_inc(sem("row_in"), 16)
                sp.dma_start(m0_row[:, :], I["state_mlstm_m"].rearrange("o b h -> (o h) b"),
                             allow_slow_non_contiguous=True).then_inc(sem("row_in"), 16)
                sp.dma_start(scan[:, :, :], X["scan"]).then_inc(sem("row_in"), 16)
                sp.dma_start(rowc[:, :], X["rowc"]).then_inc(sem("row_in"), 16)
                sp.dma_start(oh[:, :, :], X["oh"]).then_inc(sem("oh_in"), 16)
                sp.dma_start(rb[0:32, :], I["rel_bias"]).then_inc(sem("oh_in"), 16)
                sp.dma_start(sel4[:, :, :], X["sel4"]).then_inc(sem("sel4_in"), 16)
                for n in range(2, len(loads)):
                    if n >= 3:
                        side.until(last_block[n - 3])
                    load_weights(sp, n)
                for i in range(NT + 1):
                    sp.wait_ge(sem("y_left"), i + 1)
                    sp.wait_ge(sem("y_right"), i + 1)
                    if i < NT:
                        sp.dma_start(o_yp[0, P * i:P * (i + 1), :], o_st[:, i, :]).then_inc(sem("y_stored"), 16)
                    else:
                        sp.dma_start(o_ys.rearrange("b t d -> (b t) d"), o_st[0:TS, i, :]).then_inc(sem("y_stored"), 16)
                sp.wait_ge(sem("moved_up"), 48)
                sp.wait_ge(sem("y_stored"), 16 * (NT + 1))

            @blk.gpsimd
            def _(pool):
                st = Steps(pool, sem("pool_step"))
                st.then(nc.gpsimd.memset(ones[:, :], 1.0))
                st.then(nc.gpsimd.memset(eps[:, :], EPS))
                st.then(nc.gpsimd.memset(one[:, :], 1.0))
                nc.gpsimd.memset(rb[32:33, :], 1.0).then_inc(sem("rb_one"), 1)
                pool.wait_ge(sem("rb_one"), 1)
                nc.gpsimd.memset(ssx[:, :], 1.0).then_inc(sem("ssx_set"), 1)
                pool.wait_ge(sem("ssx_set"), 1)
                pool.wait_ge(sem("vecs_done"), 1)
                for m, i in enumerate(x_order):
                    n = P if i < NT else TS
                    pool.wait_ge(sem("x_ev"), m + 1)
                    if m >= 2:
                        pool.wait_ge(sem("h_lo_done"), m - 1)
                    nc.gpsimd.tensor_tensor(xg[:, m % 2, :, 0:n], xT[:, :, P * i:P * i + n],
                                            vecs[:, 0:KD].unsqueeze(2).broadcast_to([P, KD, n]), ALU.mult).then_inc(sem("xg_made"), 1)
                    pool.wait_ge(sem("xg_made"), m + 1)
                pool.wait_ge(sem("x_tr"), NT + 1)
                pool.wait_ge(sem("h_lo_done"), NT + 1)
                pool.wait_ge(sem("rstd_done"), 2)
                nc.gpsimd.memset(va_tok[:, :, :, HD:HD + 1], 1.0).then_inc(sem("va_one"), 1)
                pool.wait_ge(sem("va_one"), 1)
                nc.gpsimd.memset(QpA[:, :, :, :], 0.0).then_inc(sem("qpa_zero"), 1)
                pool.wait_ge(sem("qpa_zero"), 1)
                nc.gpsimd.memset(hA[:, NT], 0.0).then_inc(sem("ha_zero"), 1)
                pool.wait_ge(sem("tab_ev"), 8)
                tab_d = X["tab"].rearrange("o (h u) -> (o h) u", u=REV)
                for g in range(3):
                    pool.dma_start(tab_d[2 * g:2 * g + 2, :], tab[0:2, g, :]).then_inc(sem("tab_out"), 16)
                pool.dma_start(tab_d[6:HEADS, :], tab[0:6, 3, :]).then_inc(sem("tab_out"), 16)
                pool.wait_ge(sem("tab_out"), 64)
                pool.dma_start(X["rev"], X["tab"].broadcast_to([P, HEADS * REV])).then_inc(sem("rev_out"), 16)
                pool.wait_ge(sem("rows_done"), 1)
                pool.dma_start(o_pm.rearrange("o b h -> h (o b)"), m_row[:, TP - 1:TP], allow_slow_non_contiguous=True).then_inc(sem("a_out"), 16)
                pool.dma_start(o_sm.rearrange("o b h -> (o h) b"), m_row[:, TP + TB - 1:T:TB],
                               allow_slow_non_contiguous=True).then_inc(sem("a_out"), 16)
                pool.wait_ge(sem("rev_out"), 16)

                def bias_tiles(dst, h0, done):
                    pool.dma_start(dst, bass.AP(X["rev"].tensor, REV * h0 + P - 1,
                                                [[HEADS * REV - 1, P], [REV, 6], [1, TP]])).then_inc(done, 16)

                def state(h):
                    pool.wait_ge(sem("stp_ev"), h + 1)
                    pool.dma_start(o_pC[0, 0, h], st_o[:, h % 2, 0:HD]).then_inc(sem(f"st_stored{h % 2}"), 16)
                    pool.dma_start(o_pn[0, 0, h].rearrange("(k o) -> k o", o=1), st_o[:, h % 2, HD:HD + 1],
                                   allow_slow_non_contiguous=True).then_inc(sem(f"st_stored{h % 2}"), 16)

                def sample_state(h):
                    p = par(h)
                    pool.wait_ge(sem("cn_done"), h + 1)
                    pool.dma_start(o_sC[0, :, h].rearrange("b k v -> k b v"), C0n[p:p + HD, :, h // 2, 0:HD]).then_inc(sem("a_out"), 16)
                    pool.dma_start(o_sn[0, :, h].rearrange("b k -> k b"), C0n[p:p + HD, :, h // 2, HD],
                                   allow_slow_non_contiguous=True).then_inc(sem("a_out"), 16)

                tb = [t for t in range(len(turns)) if kinds[turns[t]][0][1] != "a"]
                for h in range(HA):
                    state(h)
                pool.wait_ge(sem("dc_mm"), 1)
                bias_tiles(TTb[:, :, :], 0, sem("ttb_in"))
                store_tok(pool, tb[0])
                store_tok(pool, tb[1])
                sample_state(0), sample_state(1)
                store_tok(pool, tb[2])
                sample_state(2), sample_state(3)
                store_tok(pool, tb[3])
                pool.wait_ge(sem("ya_done"), 4)
                bias_tiles(TTc[:, :, :], 6, sem("ttc_in"))
                for t in tb[4:]:
                    store_tok(pool, t)
                pool.wait_ge(sem("s_used"), ND * 3)
                st.then(nc.gpsimd.memset(RBs[:, :, :], 0.0))
                st.then(nc.gpsimd.memset(Qs[:, :, :], 0.0))
                nc.gpsimd.nop().then_inc(sem("zero4"), 1)
                for t in range(TB):
                    pool.dma_start(rb4[32 * t:32 * (t + 1), :], I["rel_bias"]).then_inc(sem("rb4_in"), 16)
                pool.wait_ge(sem("s_used"), len(segs))
                pool.wait_ge(sem("new4"), 2)
                nc.gpsimd.memset(Qpad[:, :, :, :], 0.0).then_inc(sem("qpad_zero"), 1)
                pool.wait_ge(sem("new_mm"), 6)
                nc.gpsimd.memset(PTp[:, :, :, :, :], 0.0).then_inc(sem("pad_zero"), 1)
                pool.wait_ge(sem("pad_zero"), 1)
                for k in range(KD):
                    for c in (1, 2):
                        pool.wait_ge(sem("gated"), 3 * k + c + 1)
                        st.then(nc.gpsimd.tensor_tensor(mt[:, 0, :], mt[:, 0, :], gated_part(k, c), ALU.add))
                    nc.gpsimd.nop().then_inc(sem("mg_done"), 1)
                for s in k_stored:
                    pool.wait_ge(s, 32 * 3)
                pool.wait_ge(sem("v_stored"), 32 * 6)
                pool.wait_ge(sem("a_out"), 160)
                for b in range(2):
                    pool.wait_ge(sem(f"st_stored{b}"), 16 * HA)

            @blk.tensor
            def _(pe):
                def rstd_rows():
                    yield 1.5
                    pe.wait_ge(sem("ssx_set"), 1)
                    for i in range(NT + 1):
                        n = P if i < NT else TS
                        pe.wait_ge(sem("diag_done"), i + 1)
                        out = acc[:, 6, P * i:P * i + n] if i < NT else acc[:, 7, 64:64 + TS]
                        nc.tensor.matmul(out, ones[0:n, :], diag[0:n, i, 0:n], start=True, stop=True).then_inc(sem("rstd_mm"), 1)

                def bias_rows():
                    yield 2.1
                    pe.wait_ge(sem("oh_in"), 32)
                    pe.wait_ge(sem("rb_one"), 1)
                    pe.wait_ge(sem("rstd_done"), 2)
                    for n, kind in enumerate((1, 2, 3, 0)):
                        yield 2.15 + 0.25 * n
                        if n >= 2:
                            pe.wait_ge(sem("tab_ev"), 2 * (n - 1))
                        heads = rb[:, 2 * (kind - 1):2 * kind] if kind else rb[:, 6:HEADS]
                        m, b = heads.shape[1], 4 + 2 * (n % 2)
                        nc.tensor.matmul(acc[0:m, b, 0:512], heads, oh[:, kind, 0:512], start=True, stop=True)
                        nc.tensor.matmul(acc[0:m, b + 1, 0:REV - 512], heads, oh[:, kind, 512:REV],
                                         start=True, stop=True).then_inc(sem("tab_mm"), 1)

                def turn():
                    for t, w in enumerate(turns):
                        yield w + 1 + 5 / 16
                        pe.wait_ge(acc_ev, sum_at[w] + 2)
                        if t >= 1:
                            pe.wait_ge(sem("tok_done"), 2 * t)
                        src = turned_from(t)
                        for i in range(NT):
                            ins = nc.tensor.transpose(acc[:, 2, P * i:P * (i + 1)], src[:, P * i:P * (i + 1)], ident)
                        ins.then_inc(sem("tok_tr"), 1)
                        yield w + 1 + 11 / 16
                        pe.wait_ge(sem("tok_done"), 2 * t + 1)
                        nc.tensor.transpose(acc[0:TS, 2, 0:P], src[:, TP:T], ident).then_inc(sem("tok_tr"), 1)

                def mlstm():
                    yield 3.45
                    pe.wait_ge(sem("rows_done"), 2)
                    for i in range(NT):
                        nc.tensor.transpose(acc[:, 3, HA * i:HA * (i + 1)], rA[:, P * i:P * (i + 1)], ident[0:HA, 0:HA])
                        nc.tensor.transpose(acc[:, 3, 16 + HA * i:16 + HA * (i + 1)], m_row[:, P * i:P * (i + 1)], ident[0:HA, 0:HA])
                    nc.tensor.transpose(acc[0:TS, 3, 32:36], rA[:, TP:T], ident[0:HA, 0:HA])
                    nc.tensor.transpose(acc[0:TS, 3, 36:40], m_row[:, TP:T], ident[0:HA, 0:HA])
                    pe.wait_ge(sem("tails_done"), 1)
                    nc.tensor.transpose(acc[0:TS, 3, 40:44], tails[:, 0:TS], ident[0:HA, 0:HA])
                    nc.tensor.transpose(acc[0:TS, 3, 44:48], tails[:, TS:2 * TS], ident[0:HA, 0:HA]).then_inc(sem("bytok_tr"), 1)
                    yield 3.7
                    pe.wait_ge(sem("tab_ev"), 8)
                    for h in range(HA):
                        nc.tensor.matmul(acc[:, 4 + h, :], rowc[:, R_SEL + P * h:R_SEL + P * (h + 1)], g_row[:, 0:TP],
                                         start=True, stop=True).then_inc(sem("g_mm"), 1)
                    for h in range(HA):
                        p = par(h)
                        for i in range(NT):
                            u = NT * h + i
                            yield T_ML + h + (0, 2, 4, 8)[i] / 16
                            if u == 0:
                                pe.wait_ge(sem("g_ev"), HA)
                                pe.wait_ge(sem("bytok_done"), 1)
                            if u >= 3:
                                pe.wait_ge(sem("pt_done"), u - 2)
                            nc.tensor.matmul(acc[:, 3 + u % 3, 0:TP - P * i], kT[p:p + HD, h // 2, P * i:P * (i + 1)],
                                             qT[p:p + HD, h // 2, P * i:TP], start=True, stop=True).then_inc(sem("a_s"), 1)
                        yield T_ML + h + 13 / 16
                        if h >= 1:
                            pe.wait_ge(sem("stp_ev"), h)
                        pe.wait_ge(sem("pt_done"), NT * (h + 1))
                        pe.wait_ge(sem("kw_done"), h + 1)
                        for j in range(NT):
                            for s in range(j + 1):
                                o = A_OFF[s] + P * (j - s)
                                nc.tensor.matmul(acc[:, 7, (HD + 1) * j:(HD + 1) * (j + 1)], PT[:, o:o + P],
                                                 va_tok[:, s, h, :], start=s == 0, stop=s == j)
                        c = NT * (HD + 1)
                        for s in range(NT):
                            ins = nc.tensor.matmul(acc[0:HD, 7, c:c + HD + 1], kw[:, s, :], va_tok[:, s, h, :],
                                                   start=s == 0, stop=s == NT - 1)
                        ins.then_inc(sem("a_o"), 1)
                    yield T_MS + 0.1
                    pe.wait_ge(sem("pt_done"), HA * NT)
                    order = Steps(pe, sem("pe_order"))
                    for h in range(HA):
                        ins = nc.tensor.matmul(acc[0:TS, 3, TS * h:TS * (h + 1)], rowc[:, R_SEL + P * h:R_SEL + P * h + TS],
                                               g_row[:, TP:T], start=True, stop=True)
                    ins.then_inc(sem("sg_mm"), 1)
                    for h in (0, 2, 1, 3):
                        p = par(h)
                        ins = nc.tensor.matmul(acc[0:TS, 4, TS * h:TS * (h + 1)], kT[p:p + HD, h // 2, TP:T],
                                               qT[p:p + HD, h // 2, TP:T], start=True, stop=True)
                        if h >= 2:
                            order.then(ins)
                    yield T_MS + 0.8
                    pe.wait_ge(sem("spt_done"), 1)
                    pe.wait_ge(sem("qp_done"), 1)
                    pe.wait_ge(sem("st_in"), 16 * 8)
                    for h in range(HA):
                        c = h * (HD + 1)
                        nc.tensor.matmul(acc[0:TS, 5, c:c + HD + 1], W[0:TS, 0, TS * h:TS * (h + 1)], va_tok[0:TS, NT, h, :],
                                         start=True, stop=True)
                    for h in (0, 2, 1, 3):
                        p = par(h)
                        c = h * (HD + 1)
                        for b in range(NB):
                            ins = nc.tensor.matmul(acc[0:TS, 6, c:c + HD + 1], QpA[p:p + HD, h // 2, b, :],
                                                   C0n[p:p + HD, b, h // 2, :], start=b == 0, stop=b == NB - 1)
                        if h == 2:
                            order.then(ins)
                    ins.then_inc(sem("so_mm"), 1)
                    for h in range(HA):
                        p = par(h)
                        ins = nc.tensor.matmul(acc[p:p + HD, 3, NB * (h // 2):NB * (h // 2 + 1)],
                                               rowc[:, R_SEL + P * h:R_SEL + P * h + HD], tails[:, 2 * TS:], start=True, stop=True)
                    ins.then_inc(sem("dc_mm"), 1)
                    for h in range(HA):
                        p = par(h)
                        yield T_MS + 1.95 + 0.5 * h
                        pe.wait_ge(sem("vb_done"), h + 1)
                        if h >= 1:
                            pe.wait_ge(sem("cn_done"), h)
                        for half in range(2):
                            ins = nc.tensor.matmul(acc[p:p + HD, 4 + half, 0:4 * (HD + 1)], kws[:, HD * h:HD * (h + 1)],
                                                   Vb[:, 4 * half:4 * half + 4, :], start=True, stop=True)
                        ins.then_inc(sem("sst_mm"), 1)
                    yield T_MS + 4.85
                    pe.wait_ge(sem("hn_done"), 1)
                    for pr in range(2):
                        for i in range(NT + 1):
                            n = P if i < NT else TS
                            b, c = (3 + 2 * pr, P * i) if i < NT else (4 + 2 * pr, 0)
                            ins = nc.tensor.transpose(acc[:, b, c:c + n], hA[0:n, i, 2 * pr:2 * pr + 2, :].rearrange("p h d -> p (h d)"),
                                                      ident[0:n, 0:n])
                        ins.then_inc(sem("ya_tr"), 1)

                def scores(n):
                    u, i, h, k0, off = segs[n]
                    if n >= 3:
                        pe.wait_ge(sem("s_used"), n - 2)
                    else:
                        pe.wait_ge(sem("ya_done"), 4)
                    p, t = par(h), 2 + h // 2
                    nc.tensor.matmul(acc[:, 3 + n % 3, 0:P * (i + 1 - k0)], qT[p:p + HD, t, P * i:P * (i + 1)],
                                     kT[p:p + HD, t, P * k0:P * (i + 1)], start=True, stop=True).then_inc(sem("s_mm"), 1)

                def turn_p(n):
                    u, i, h, k0, off = segs[n]
                    pe.wait_ge(sem("p_done"), u + 1)
                    if n >= 1:
                        pe.wait_ge(sem("pt_ev"), n)
                    src = scores_in(u)
                    for k in range(i + 1 - k0):
                        ins = nc.tensor.transpose(acc[:, 6, P * k:P * (k + 1)], src[:, off + P * k:off + P * (k + 1)], ident)
                    ins.then_inc(sem("pt_tr"), 1)

                def outputs(n):
                    u, i, h, k0, off = segs[n]
                    pe.wait_ge(sem("pt_ev"), n + 1)
                    if n >= 1:
                        pe.wait_ge(sem("o_ev"), n)
                    p = par(h)
                    for k in range(i + 1 - k0):
                        ins = nc.tensor.matmul(acc[p:p + HD, 7, 0:P], v_tok[:, k0 + k, HD * h:HD * (h + 1)],
                                               PTs[:, n % 2, P * k:P * (k + 1)], start=k == 0, stop=k == i - k0)
                    ins.then_inc(sem("o_mm"), 1)

                def attention():
                    for u in range(ND + 1):
                        for c in range(3):
                            if u < ND:
                                yield unit_time(u, (1 + c) / 16)
                                scores(unit_segs[u][c])
                        for c in range(3):
                            if u >= 1:
                                yield T_DIL + u + (5, 8, 12)[c] / 16
                                turn_p(unit_segs[u - 1][c])
                                yield T_DIL + u + (7, 11, 15)[c] / 16
                                outputs(unit_segs[u - 1][c])
                    for c in range(NU - ND + 3):
                        u = ND + c
                        if u < NU:
                            yield unit_time(u, 0)
                            scores(unit_segs[u][0])
                        if 3 <= c:
                            yield unit_time(u, 0.25)
                            outputs(unit_segs[u - 3][0])
                        if 2 <= c < NU - ND + 2:
                            yield unit_time(u, 0.75)
                            turn_p(unit_segs[u - 2][0])

                def sample():
                    yield T_SA + 0.7
                    pe.wait_ge(sem("q4"), 1)
                    pe.wait_ge(sem("sel4_in"), 16)
                    pe.wait_ge(sem("s_used"), len(segs))
                    pe.wait_ge(sem("tok_done"), 2 * len(turns))
                    for q in range(6):
                        yield T_SA + 0.7 + q / 24
                        g, lo = q % 3, HD * (q // 3)
                        kind = 1 + q if q < 3 else 0
                        w = P * NC4[q]
                        new = acc[lo:lo + HD, 2, TS * g:TS * (g + 1)]
                        rbq = RBs[:, 2 * q:2 * q + 2, :].rearrange("p h n -> p (h n)")
                        nc.tensor.matmul(acc[lo:lo + HD, 3 + g, 0:w], rbq, sel4[:, kind, 2 * P - w:2 * P], start=True, stop=False)
                        nc.tensor.matmul(new.rearrange("p (b t) -> p b t", t=TB), rbq,
                                         sel4[:, kind, 2 * P:2 * P + TB].unsqueeze(1).broadcast_to([P, NB, TB]),
                                         start=True, stop=False)
                        nc.tensor.matmul(new, Qs[:, q, :], kTn[:, q, :], start=False, stop=True).then_inc(sem("new_mm"), 1)

                    def turn_k(n):
                        q, b = divmod(n, NB)
                        if n >= 2:
                            pe.wait_ge(sem("kt_ev"), n - 1)
                        tiles, done, count = ring_tiles("k", q)
                        pe.wait_ge(done, count)
                        for c in range(NC4[q]):
                            ins = nc.tensor.transpose(acc[:, 6 + n % 2, P * c:P * (c + 1)], tiles[:, NC4[q] * b + c, :], ident)
                        ins.then_inc(sem("kt_tr"), 1)

                    yield T_SA + 1
                    pe.wait_ge(sem("o_ev"), len(segs))
                    turn_k(0)
                    for n in range(6 * NB):
                        q, b = divmod(n, NB)
                        yield T_SA + 1 + n / 16
                        if n + 1 < 6 * NB:
                            turn_k(n + 1)
                        pe.wait_ge(sem("kt_ev"), n + 1)
                        if b == 0:
                            pe.wait_ge(sem("qpad_done"), q + 1)
                        g, lo, w = q % 3, HD * (q // 3), P * NC4[q]
                        nc.tensor.matmul(acc[lo:lo + HD, 3 + g, 0:w], Qpad[:, q % 2, b, :], KTs[:, n % 2, 0:w],
                                         start=False, stop=b == NB - 1).then_inc(sem("qk4"), 1)

                def second_norm():
                    yield n_wout + 0.6
                    pe.wait_ge(sem("ssq2_done"), KD)
                    for half in range(2):
                        ins = nc.tensor.matmul(acc[:, 6 + half, 0:HALF[half]], ones[:, :], two(ssq, half), start=True, stop=True)
                    ins.then_inc(sem("ssq_mm"), 1)

                def sample_outputs():
                    for half in range(2):
                        yield T_SA + (3.65, 4.62)[half]
                        pe.wait_ge(sem("p4"), half + 1)
                        if half == 0:
                            pe.wait_ge(sem("new_read"), 1)
                        else:
                            pe.wait_ge(sem("ptn_ev"), 1)
                            pe.wait_ge(sem("pad_ev"), 3)
                        lo = HD * half
                        idn = con[lo:lo + HD, C_ID + lo:C_ID + lo + HD]
                        for g in range(3):
                            for c in range(NC4[3 * half + g]):
                                b, at = turned_p(half, g, c)
                                nc.tensor.transpose(acc[:, b, at:at + HD], S4[lo:lo + HD, g, P * c:P * (c + 1)], idn)
                            b, at = turned_p(half, g, 2)
                            ins = nc.tensor.transpose(acc[0:TS, b, at:at + HD], S4[lo:lo + HD, g, 256:288], idn)
                        ins.then_inc(sem("pt4"), 1)
                        for g in range(3):
                            q = 3 * half + g
                            out = acc[0:HD, O4_BANK[half], P * g:P * (g + 1)]
                            for b in range(NB):
                                yield T_SA + 4.0 + (q + b / NB) / 4
                                if b == 0:
                                    tiles, done, count = ring_tiles("v", q)
                                    pe.wait_ge(done, count)
                                    pe.wait_ge(sem("pad_ev"), q + 1)
                                    pe.wait_ge(sem("ptn_ev"), half + 1)
                                    pe.wait_ge(sem("kt_ev"), 6 * NB)
                                    nc.tensor.matmul(out, PTn[:, g, :], vn[:, P * q:P * (q + 1)], start=True, stop=False)
                                for c in range(NC4[q]):
                                    ins = nc.tensor.matmul(out, PTp[:, q % 2, b, c, :], tiles[:, NC4[q] * b + c, :],
                                                           start=False, stop=b == NB - 1 and c == NC4[q] - 1)
                            ins.then_inc(sem("o4"), 1)

                def sample_turns():
                    for half in range(2):
                        yield T_SA + (5.1, 5.62)[half]
                        pe.wait_ge(sem("osb_ev"), half + 1)
                        for g in range(3):
                            ins = nc.tensor.transpose(acc[:, 3 + half, HD * g:HD * (g + 1)], Osb[:, half, g, :], ident[0:HD, 0:HD])
                        ins.then_inc(sem("ot_tr"), 1)

                def x_turned(n):
                    i = x_order[n]
                    rows = P if i < NT else TS
                    pe.wait_ge(sem(f"x_in{i}"), 16)
                    if n >= 2:
                        pe.wait_ge(sem("x_ev"), n - 1)
                    for k in range(KD):
                        ins = nc.tensor.transpose(acc[:, 2 + 2 * (n % 2) + k // 4, P * (k % 4):P * (k % 4) + rows],
                                                  x_tok[0:rows, i, P * k:P * (k + 1)], ident[0:rows, 0:rows])
                    ins.then_inc(sem("x_tr"), 1)

                pe.wait_ge(sem("con_in"), 16)
                x_turned(0)
                pe.wait_ge(sem("vec_in"), 64)
                nc.tensor.transpose(acc[:, 7, 0:26], vrow[:, :], ident[0:26, 0:26]).then_inc(sem("v_tr"), 1)
                for n in range(1, NT + 1):
                    x_turned(n)
                side = Side(rstd_rows(), bias_rows(), turn(), mlstm(), attention(), sample(), sample_outputs(), sample_turns(), second_norm())

                def tile_split(w):
                    if w == 0:
                        return lambda half, k: pe.wait_ge(sem("h_lo_done"), HALF[0] // P if half == 0 else NT + 1)
                    if info.get(w, ("",))[0] == "br":
                        return lambda half, k: pe.wait_ge(sem("y_lo_done"), k + 1)
                    if w == n_merge:
                        return lambda half, k: pe.wait_ge(sem("mg_lo_done"), k + 1)
                    if w == n_wout:
                        return lambda half, k: pe.wait_ge(sem("h2_lo_done"), k + 1)
                    if w >= n_gu:
                        return lambda half, k: pe.wait_ge(sem("s_lo_done"), k + 1)
                    return None

                for w in range(n_all):
                    pe.wait_ge(w_lo_done, w + 1)
                    if w < n_wout and info.get(w, ("",))[0] == "br":
                        products(pe, side, w, y_hi, y_lo, part=tile_split(w))
                    elif n_merge <= w < n_wout:
                        products(pe, side, w, mg_hi, mg_lo, part=tile_split(w), late=w == n_merge)
                    elif w >= n_gu:
                        products(pe, side, w, s_hi, s_lo, kx=DOWN[(w - n_gu) % 6 // 2][0], part=tile_split(w))
                    else:
                        products(pe, side, w, h_hi, h_lo, part=tile_split(w), late=w == n_wout)
                pe.wait_ge(sem("ssq3_done"), KD - 1)
                pe.wait_ge(acc_ev, n_sum)
                for i in range(NT + 1):
                    n = P if i < NT else TS
                    nc.tensor.matmul(acc[0:n, 7, i:i + 1], ssq[:, P * i:P * i + n], ones[:, 0:1], start=True, stop=False)
                    if i == 0:
                        pe.wait_ge(sem("sq3_done"), KD)
                    ins = nc.tensor.matmul(acc[0:n, 7, i:i + 1], sq[:, (KD - 1) % 2, P * i:P * i + n], ones[:, 0:1],
                                           start=False, stop=True)
                ins.then_inc(sem("rt_mm"), 1)
                pe.wait_ge(sem("xg_done"), KD)
                for i in range(NT + 1):
                    n = P if i < NT else TS
                    if i >= 3:
                        pe.wait_ge(sem("y_left"), i - 2)
                        pe.wait_ge(sem("y_right"), i - 2)
                    for k in range(KD):
                        ins = nc.tensor.transpose(acc[0:n, 2 * (i % 3) + k // 4, P * (k % 4):P * (k % 4 + 1)],
                                                  xT[:, k, P * i:P * i + n], ident)
                    ins.then_inc(sem("y_tr"), 1)

            @blk.scalar
            def _(act):
                a = Steps(act, sem("act_step"))

                def rstd_rows():
                    yield 0.1
                    act.wait_ge(sem("ssx_set"), 1)
                    for i in range(NT + 1):
                        n = P if i < NT else TS
                        a.then(nc.scalar.activation(xsq[0:n, :], x_tok[0:n, i, :], ACT.Square, accum_out=ssx[0:n, i:i + 1]))
                    nc.scalar.activation(ssx[:, :], ssx[:, :], ACT.Sqrt, bias=eps[:, :], scale=1.0 / D).then_inc(sem("std_done"), 1)
                    yield 1.3
                    act.wait_ge(sem("rstd_mm"), NT + 1)
                    nc.scalar.copy(rstd[:, 0:TP], acc[:, 6, :]).then_inc(sem("rstd_done"), 1)
                    nc.scalar.copy(rstd[:, TP:T], acc[:, 7, 64:64 + TS]).then_inc(sem("rstd_done"), 1)

                def bias_rows():
                    for n, kind in enumerate((1, 2, 3, 0)):
                        yield 2.25 + 0.25 * n
                        act.wait_ge(sem("tab_mm"), n + 1)
                        m, b = (2, 4 + 2 * (n % 2)) if kind else (6, 4 + 2 * (n % 2))
                        nc.scalar.copy(tab[0:m, n, 0:512], acc[0:m, b, 0:512]).then_inc(sem("tab_ev"), 1)
                        nc.scalar.copy(tab[0:m, n, 512:REV], acc[0:m, b + 1, 0:REV - 512]).then_inc(sem("tab_ev"), 1)

                def turn():
                    yield 4
                    act.wait_ge(sem("va_one"), 1)
                    for t, w in enumerate(turns):
                        yield w + 1 + 8 / 16
                        act.wait_ge(sem("tok_tr"), 2 * t + 1)
                        name, i = kinds[w]
                        if t in k_stores and k_stores.index(t) >= 2:
                            n = k_stores.index(t)
                            act.wait_ge(k_stored[n % 2], 32 * (n // 2))
                        if name == "vb" and i == 0:
                            act.wait_ge(sem("oa_read"), 1)
                        pr, sa = token_place(t)
                        src, ssrc = acc[:, 2, 0:TP], acc[0:TS, 2, 0:P]
                        if name == "va":
                            src = src.rearrange("p (i h d) -> p i h d", h=2, d=HD)
                            ssrc = ssrc.rearrange("p (h d) -> p h d", d=HD)
                        else:
                            src = src.rearrange("p (i c) -> p i c", c=P)
                        nc.scalar.copy(pr, src).then_inc(sem("tok_done"), 1)
                        yield w + 1 + 13 / 16
                        act.wait_ge(sem("tok_tr"), 2 * t + 2)
                        nc.scalar.copy(sa, ssrc).then_inc(sem("tok_done"), 1)

                def mlstm():
                    yield 1.4
                    act.wait_ge(sem("f_ready"), 1)
                    a.then(nc.scalar.activation(rB[:, :], rB[:, :], ACT.Exp))
                    nc.scalar.activation(rB[:, :], rB[:, :], ACT.Ln, bias=one[0:HA, :]).then_inc(sem("ln_done"), 1)
                    yield 3.2
                    act.wait_ge(sem("rows_done"), 2)
                    nc.scalar.activation(tails[:, :], tails[:, :], ACT.Exp).then_inc(sem("tails_done"), 1)
                    yield 3.6
                    act.wait_ge(sem("bytok_tr"), 1)
                    a.then(nc.scalar.copy(by_tok[:, 0:32], acc[:, 3, 0:32]))
                    a.then(nc.scalar.copy(by_tok[0:TS, 32:48], acc[0:TS, 3, 32:48]))
                    a.then(nc.scalar.activation(e_m[:, 0:16], by_tok[:, 16:32], ACT.Exp, scale=-1.0))
                    nc.scalar.activation(e_m[0:TS, 16:20], by_tok[0:TS, 36:40], ACT.Exp, scale=-1.0).then_inc(sem("bytok_done"), 1)
                    for h in range(HA):
                        yield 4.1 + 0.2 * h
                        act.wait_ge(sem("g_mm"), h + 1)
                        nc.scalar.copy(G[:, h, :], acc[:, 4 + h, :]).then_inc(sem("g_ev"), 1)
                    yield 5.6
                    act.wait_ge(sem("ws_arg"), 1)
                    nc.scalar.activation(ws[:, :], ws[:, :], ACT.Exp).then_inc(sem("ws_done"), 1)
                    for u in range(HA * NT):
                        h, i = divmod(u, NT)
                        yield T_ML + h + (-0.1, 0.12, 0.24, 0.36)[i]
                        act.wait_ge(sem("w_arg"), u + 1)
                        bias = by_tok[:, HA * i + h:HA * i + h + 1]
                        Wb = W[:, u % 2]
                        if i < NT - 1:
                            nc.scalar.activation(Wb[:, P:TP - P * i], G[:, h, P * (i + 1):TP], ACT.Exp, bias=bias)
                        nc.scalar.activation(Wb[:, 0:P], Wb[:, 0:P], ACT.Exp, bias=bias).then_inc(sem("w_done"), 1)
                    yield T_MS + 0.4
                    act.wait_ge(sem("sw_arg"), 1)
                    for h in range(HA):
                        ins = nc.scalar.activation(W[0:TS, 1, TS * h:TS * (h + 1)], W[0:TS, 1, TS * h:TS * (h + 1)], ACT.Exp,
                                                   bias=by_tok[0:TS, 32 + h:33 + h])
                    ins.then_inc(sem("sw_done"), 1)
                    yield T_MS + 2.1
                    act.wait_ge(acc_ev, sum_at[9])
                    nc.scalar.activation(oaT[:, :, :], oaT[:, :, :], ACT.Sigmoid).then_inc(sem("oa_done"), 1)
                    yield T_MS + 4.1
                    act.wait_ge(sem("rs_arg"), 1)
                    nc.scalar.activation(rs[:, :], rs[:, :], ACT.Sqrt, bias=eps[:, :], scale=1.0 / HD).then_inc(sem("rs_std"), 1)

                def exps(u):
                    act.wait_ge(sem("m_done"), u + 1)
                    if u >= 4:
                        act.wait_ge(sem("p_done"), u - 3)
                    s = scores_in(u)
                    nc.scalar.activation(s, s, ACT.Exp, bias=mx[:, u % 4:u % 4 + 1],
                                         accum_out=dn[:, u % 4:u % 4 + 1]).then_inc(sem("e_done"), 1)

                def turned(n):
                    u, i, h, k0, off = segs[n]
                    act.wait_ge(sem("pt_tr"), n + 1)
                    if n >= 2:
                        act.wait_ge(sem("o_mm"), n - 1)
                    w = P * (i + 1 - k0)
                    nc.scalar.copy(PTs[:, n % 2, 0:w], acc[:, 6, 0:w]).then_inc(sem("pt_ev"), 1)

                def attention():
                    for u in range(ND + 1):
                        for c in range(3):
                            if u >= 1:
                                yield T_DIL + u + (6, 9, 13)[c] / 16
                                turned(unit_segs[u - 1][c])
                                if c == 0 and u < ND:
                                    exps(u)
                            elif c == 0:
                                yield unit_time(u, 7 / 16)
                                exps(u)
                    for c in range(NU - ND + 3):
                        u = ND + c
                        if 3 <= c:
                            yield unit_time(u, 0.1)
                            turned(unit_segs[u - 3][0])
                        if c < NU - ND:
                            yield unit_time(u, 0.6)
                            exps(u)

                def gates():
                    for w in range(n_proj, n_merge):
                        if info[w][0] == "gate":
                            _, j, r = info[w]
                            yield w + 1.3
                            act.wait_ge(acc_ev, sum_at[w] + 2)
                            nc.scalar.activation(gs[j % 2][:, r, :], gs[j % 2][:, r, :], ACT.Tanh, scale=0.5).then_inc(sem("g_tanh"), 1)

                def sample():
                    for n in range(6 * NB):
                        yield T_SA + 1 + (n - 0.5) / 16
                        act.wait_ge(sem("kt_tr"), n + 1)
                        if n >= 2:
                            act.wait_ge(sem("qk4"), n - 1)
                        w = P * NC4[n // NB]
                        nc.scalar.copy(KTs[:, n % 2, 0:w], acc[:, 6 + n % 2, 0:w]).then_inc(sem("kt_ev"), 1)

                def sample_softmax():
                    for half in range(2):
                        lo = HD * half
                        for g in range(3):
                            yield T_SA + (3.12, 4.2)[half] + 0.065 * g
                            act.wait_ge(sem("mx4"), half + 1)
                            s = S4[lo:lo + HD, g, :]
                            nc.scalar.activation(s, s, ACT.Exp, bias=mx4[lo:lo + HD, g:g + 1],
                                                 accum_out=dn4[lo:lo + HD, g:g + 1]).then_inc(sem("e4"), 1)
                        yield T_SA + (3.75, 4.65)[half]
                        act.wait_ge(sem("pt4"), half + 1)
                        if half == 1:
                            act.wait_ge(sem("o4"), 3)
                        bk, at = turned_p(half, 0, 2)
                        nc.scalar.copy(PTn[:, :, :], acc[0:TS, bk, at:at + 3 * HD].rearrange("p (g n) -> p g n", n=HD)
                                       ).then_inc(sem("ptn_ev"), 1)
                        act.wait_ge(sem("pad_zero"), 1)
                        for g in range(3):
                            q = 3 * half + g
                            yield T_SA + (3.76, 3.77, 4.27, 4.66, 4.8, 5.05)[q]
                            if q >= 2:
                                act.wait_ge(sem("o4"), q - 1)
                            n = 2 * NC4[q]
                            bk, at = turned_p(half, g, 0)
                            to = PTp[:, q % 2, 0, 0, 0:1]
                            nc.scalar.copy(bass.AP(to.tensor, to.offset, [to.ap[0], [TS, n], [2 * HD + TB, NB], [1, TB]]),
                                           acc[:, bk, at:at + n * TS].rearrange("p (x b t) -> p x b t", x=n, t=TB)
                                           ).then_inc(sem("pad_ev"), 1)

                def merge():
                    yield n_proj + 11.6
                    act.wait_ge(sem("o4"), 6)
                    act.wait_ge(sem("pad_ev"), 6)
                    for k in range(8):
                        if k >= 2:
                            yield n_proj + 11.7
                            act.wait_ge(sem("y4"), 2 if k < 5 else 4)
                        nc.scalar.copy(y_hi[:, k, :], qT[:, k, :]).then_inc(sem("y_hi_done"), 1)
                    for w in range(n_proj, n_merge):
                        if info[w][0] == "br":
                            k = info[w][1]
                            yield w + 1.2
                            act.wait_ge(sem("mg_done"), k + 1)
                            nc.scalar.activation(mg_hi[:, k, :], mt[:, 0, :], ACT.Copy, scale=0.5).then_inc(sem("mg_hi_done"), 1)
                    for k in range(KD):
                        yield n_merge + k + 1.03
                        act.wait_ge(acc_ev, sum_at[n_merge + k] + 2)
                        nc.scalar.activation(h_hi[:, k, :], xT[:, k, :], ACT.Copy, scale=vecs[:, 8 + k:9 + k]).then_inc(sem("h2_hi_done"), 1)
                        if k >= 2:
                            act.wait_ge(sem("ssq2_done"), k - 1)
                        nc.scalar.activation(sq[:, k % 2, :], xT[:, k, :], ACT.Square).then_inc(sem("sq2_done"), 1)

                def feed():
                    yield n_wout + 0.7
                    act.wait_ge(sem("ssq_mm"), 1)
                    for half in range(2):
                        nc.scalar.activation(two(rstd, half), acc[:, 6 + half, 0:HALF[half]], ACT.Sqrt, bias=eps[:, :],
                                             scale=1.0 / D).then_inc(sem("std_done"), 1)
                    for w in range(n_wout, n_gu):
                        j, r = divmod(w - n_wout, 4)
                        yield w + 1.1
                        if r < 2:
                            act.wait_ge(acc_ev, sum_at[w] + 2)
                            if j >= 1:
                                act.wait_ge(sem("s_hi_done"), 2 * (j - 1) + r + 1)
                            nc.scalar.activation(sg[:, r, :], gx[:, r, :], ACT.Sigmoid).then_inc(sem("sg_done"), 1)
                        else:
                            k = 2 * j + r - 2
                            act.wait_ge(sem("s_done"), k + 1)
                            nc.scalar.copy(s_hi[:, k, :], gx[:, r - 2, :]).then_inc(sem("s_hi_done"), 1)
                    nc.scalar.activation(spare[:, :], one[:, :], ACT.Sqrt)
                    for k in range(KD):
                        w = n_gu + 6 * (k // 2) + 4 + k % 2
                        yield w + 1.1
                        act.wait_ge(acc_ev, sum_at[w - 4] + 2)
                        if k >= 2:
                            act.wait_ge(sem("ssq3_done"), k - 1)
                        nc.scalar.activation(sq[:, k % 2, :], xT[:, k, :], ACT.Square).then_inc(sem("sq3_done"), 1)
                        nc.scalar.activation(xT[:, k, :], xT[:, k, :], ACT.Copy, scale=vecs[:, 16 + k:17 + k]).then_inc(sem("xg_done"), 1)

                act.wait_ge(sem("v_tr"), 1)
                nc.scalar.copy(vecs[:, :], acc[:, 7, 0:26]).then_inc(sem("vecs_done"), 1)

                def x_copied(m):
                    i = x_order[m]
                    n = P if i < NT else TS
                    act.wait_ge(sem("x_tr"), m + 1)
                    b = 2 + 2 * (m % 2)
                    nc.scalar.copy(xT[:, :, P * i:P * i + n].rearrange("p (b k) n -> p b k n", b=2),
                                   acc[:, b:b + 2, :].rearrange("p b (k n) -> p b k n", n=P)[:, :, :, 0:n]).then_inc(sem("x_ev"), 1)

                x_copied(0)
                x_copied(1)
                split_hi(act, 0)
                for m in range(2, NT + 1):
                    x_copied(m)
                side = Side(rstd_rows(), bias_rows(), turn(), mlstm(), attention(), gates(), sample(), sample_softmax(), merge(), feed())
                for w in range(n_all):
                    side.until(w + 0.05)
                    if w + 1 < n_all:
                        split_hi(act, w + 1)
                side.until(n_all + 2)
                act.wait_ge(sem("rt_mm"), 1)
                act.wait_ge(sem("rt_set"), 1)
                nc.scalar.activation(rt[:, 0:NT], acc[:, 7, 0:NT], ACT.Sqrt, bias=eps[:, :], scale=1.0 / D).then_inc(sem("rt_std"), 1)
                nc.scalar.activation(rt[0:TS, NT:NT + 1], acc[0:TS, 7, NT:NT + 1], ACT.Sqrt, bias=eps[0:TS, :],
                                     scale=1.0 / D).then_inc(sem("rt_std"), 1)
                act.wait_ge(sem("rt_done"), 1)
                for i in range(NT + 1):
                    n = P if i < NT else TS
                    act.wait_ge(sem("y_tr"), i + 1)
                    nc.scalar.activation(o_st[0:n, i, 0:512], acc[0:n, 2 * (i % 3), :], ACT.Copy, scale=rt[0:n, i:i + 1]).then_inc(sem("y_left"), 1)

            @blk.vector
            def _(dve):
                v = Steps(dve, sem("dve_step"))

                def evac(w, half):
                    if w < n_proj:
                        name, i = kinds[w]
                        idx, src, ready = summed(w, half)
                        dve.wait_ge(mm_done, ready)
                        r = two(rstd, half)
                        if name == "if":
                            v.do(nc.vector.tensor_tensor(two(i_row, half), src[0:HA], r[0:HA], ALU.mult))
                            v.then(nc.vector.tensor_tensor(two(f_row, half), src[32:32 + HA], r[32:32 + HA], ALU.mult))
                            nc.vector.nop().then_inc(acc_ev, 1)
                            return
                        if name[0] == "v":
                            n = v_turns.index(turns.index(w))
                            if n >= 2:
                                dve.wait_ge(sem("tok_tr"), 2 * v_turns[n - 2] + 2)
                            dst = v_st[:, n % 2, :]
                        elif name == "oa":
                            dst = oaT[:, i, :]
                        else:
                            dst = (qT if name[0] == "q" else kT)[:, Q0[name[1]] + i, :]
                        if name == "kb" and i == 0:
                            dve.wait_ge(sem("tab_out"), 64)
                        if name == "qc" and i == 0:
                            v.sync()
                        if name in ("ka", "qb", "qc"):
                            nc.vector.scalar_tensor_tensor(two(dst, half), src, SCALE, r, ALU.mult, ALU.mult).then_inc(acc_ev, 1)
                        else:
                            nc.vector.tensor_tensor(two(dst, half), src, r, ALU.mult).then_inc(acc_ev, 1)
                    elif w < n_merge and info[w][0] == "gate":
                        _, j, r = info[w]
                        idx, src, ready = summed(w, half)
                        if half == 0:
                            v.sync()
                        if w == n_proj + 4 and half == 0:
                            for s in k_stored:
                                dve.wait_ge(s, 32 * 3)
                        if w == n_proj and half == 0:
                            dve.wait_ge(sem("tok_tr"), 2 * len(turns) - 2)
                        dve.wait_ge(mm_done, ready)
                        nc.vector.tensor_tensor(two(gs[j % 2][:, r, :], half), src, two(rstd, half), ALU.mult).then_inc(acc_ev, 1)
                    elif w < n_merge:
                        k = info[w][1]
                        g, n = gs[(k // 2) % 2], k % 2
                        for c in ((0,) if half == 0 else (1, 2)):
                            if c == 0:
                                dve.wait_ge(sem("g_tanh"), 6 * (k // 2) + 6)
                            if k >= 1:
                                dve.wait_ge(sem("mg_done" if c else "mg_hi_done"), k)
                                dve.wait_ge(sem("mg_lo_done"), k)
                            for hf in range(2):
                                idx, src, ready = summed(w, 2 * c + hf)
                                dve.wait_ge(mm_done, ready)
                                nc.vector.scalar_tensor_tensor(two(gated_part(k, c), hf), two(g[:, 2 * c + n, :], hf), 1.0, src,
                                                               ALU.add, ALU.mult).then_inc(acc_ev, 1)
                            dve.wait_ge(acc_ev, summed(w, 2 * c + 1)[0] + 1)
                            nc.vector.nop().then_inc(sem("gated"), 1)
                    elif w < n_wout:
                        k = w - n_merge
                        idx, src, ready = summed(w, half)
                        dve.wait_ge(mm_done, ready)
                        nc.vector.tensor_tensor(two(xT[:, k, :], half), src, two(xT[:, k, :], half), ALU.add).then_inc(acc_ev, 1)
                        if half == 1:
                            dve.wait_ge(sem("h2_hi_done"), k + 1)
                            nc.vector.scalar_tensor_tensor(h_lo[:, k, :], xT[:, k, :], vecs[:, 8 + k:9 + k],
                                                           h_hi[:, k, :].bitcast(F32), ALU.mult, ALU.subtract).then_inc(sem("h2_lo_done"), 1)
                            add_squares(k, "sq2_done", "ssq2_done")
                    elif w < n_gu:
                        j, r = divmod(w - n_wout, 4)
                        if w == n_wout and half == 0:
                            dve.wait_ge(sem("std_done"), 3)
                            v.then(nc.vector.reciprocal(rstd[:, :], rstd[:, :]))
                        if half == 0 and r >= 2:
                            dve.wait_ge(sem("sg_done"), 2 * j + r - 1)
                            v.then(nc.vector.tensor_tensor(gx[:, r - 2, :], gx[:, r - 2, :], sg[:, r - 2, :], ALU.mult))
                        if half == 0 and r < 2 and j >= 1:
                            dve.wait_ge(sem("s_lo_done"), 2 * (j - 1) + r + 1)
                        idx, src, ready = summed(w, half)
                        dve.wait_ge(mm_done, ready)
                        dst = gx[:, r, :] if r < 2 else sg[:, r - 2, :]
                        nc.vector.tensor_tensor(two(dst, half), src, two(rstd, half), ALU.mult).then_inc(acc_ev, 1)
                        if half == 1 and r >= 2:
                            dve.wait_ge(acc_ev, idx + 1)
                            v.then(nc.vector.tensor_tensor(gx[:, r - 2, :], gx[:, r - 2, :], sg[:, r - 2, :], ALU.mult))
                            nc.vector.nop().then_inc(sem("s_done"), 1)
                    else:
                        j, r = divmod(w - n_gu, 6)
                        if r < 4:
                            return
                        k = 2 * j + r - 4
                        idx, src, ready = summed(w, half)
                        dve.wait_ge(mm_done, ready)
                        nc.vector.tensor_tensor(two(xT[:, k, :], half), src, two(xT[:, k, :], half), ALU.add).then_inc(acc_ev, 1)
                        if half == 1 and k < KD - 1:
                            add_squares(k, "sq3_done", "ssq3_done")

                def add_squares(k, squared, added):
                    dve.wait_ge(sem(squared), k + 1)
                    if k == 0:
                        nc.vector.tensor_copy(ssq[:, :], sq[:, 0, :]).then_inc(sem(added), 1)
                    else:
                        dve.wait_ge(sem(added), k)
                        nc.vector.tensor_tensor(ssq[:, :], ssq[:, :], sq[:, k % 2, :], ALU.add).then_inc(sem(added), 1)

                def feed():
                    for k in range(KF):
                        yield n_wout + 4 * (k // 2) + 3 + k % 2 + 0.26
                        dve.wait_ge(sem("s_hi_done"), k + 1)
                        nc.vector.tensor_tensor(s_lo[:, k, :], gx[:, k % 2, :], s_hi[:, k, :].bitcast(F32),
                                                ALU.subtract).then_inc(sem("s_lo_done"), 1)

                def merge():
                    for k in range(8):
                        yield n_proj + (11.75 if k < 4 else 12.02)
                        dve.wait_ge(sem("y_hi_done"), k + 1)
                        nc.vector.tensor_tensor(y_lo[:, k, :], qT[:, k, :], y_hi[:, k, :].bitcast(F32), ALU.subtract).then_inc(sem("y_lo_done"), 1)
                    for w in range(n_proj, n_merge):
                        if info[w][0] == "br":
                            k = info[w][1]
                            yield w + 1 + (0.35 if w + 1 < n_merge else 0.1)
                            dve.wait_ge(sem("mg_hi_done"), k + 1)
                            nc.vector.scalar_tensor_tensor(mg_lo[:, k, :], mt[:, 0, :], 0.5, mg_hi[:, k, :].bitcast(F32),
                                                           ALU.mult, ALU.subtract).then_inc(sem("mg_lo_done"), 1)

                def rstd_rows():
                    yield 0.5
                    dve.wait_ge(sem("std_done"), 1)
                    v.then(nc.vector.reciprocal(ssx[:, :], ssx[:, :]))
                    for i in range(NT + 1):
                        nc.vector.tensor_scalar(diag[:, i, :], ident, ssx[:, i:i + 1], None, ALU.mult).then_inc(sem("diag_done"), 1)
                    dve.wait_ge(sem("rstd_done"), 2)

                def mlstm():
                    yield 1.4
                    dve.wait_ge(sem("row_in"), 64)
                    v.do(nc.vector.tensor_scalar(i_row[:, :], i_row[:, :], bif[:, 0:1], None, ALU.add))
                    v.do(nc.vector.tensor_scalar(rA[:, :], f_row[:, :], bif[:, 1:2], 0.0, ALU.add, ALU.min))
                    v.then(nc.vector.tensor_scalar(rB[:, :], f_row[:, :], bif[:, 1:2], None, ALU.add))
                    v.then(nc.vector.scalar_tensor_tensor(rB[:, :], rB[:, :], -1.0, rB[:, :], ALU.mult, ALU.min))
                    nc.vector.nop().then_inc(sem("f_ready"), 1)
                    yield 2.1
                    dve.wait_ge(sem("ln_done"), 1)
                    v.then(nc.vector.tensor_tensor(rA[:, :], rA[:, :], rB[:, :], ALU.subtract))
                    v.then(nc.vector.tensor_tensor_scan(b_row[:, :], scan[:, 0, :], rA[:, :], 0.0, ALU.mult, ALU.add))
                    yield 2.4
                    v.then(nc.vector.tensor_tensor(rA[:, :], i_row[:, :], b_row[:, :], ALU.subtract))
                    v.then(nc.vector.tensor_copy(rB[:, :], rA[:, :]))
                    v.do(nc.vector.tensor_scalar(rB[:, 0:1], rB[:, 0:1], 0.0, None, ALU.max))
                    v.then(nc.vector.tensor_tensor(rB[:, TP:T:TB], rB[:, TP:T:TB], m0_row[:, :], ALU.max))
                    yield 2.8
                    v.then(nc.vector.tensor_tensor_scan(g_row[:, :], scan[:, 1, :], rB[:, :], 0.0, ALU.add, ALU.max))
                    v.then(nc.vector.tensor_tensor(m_row[:, :], b_row[:, :], g_row[:, :], ALU.add))
                    nc.vector.nop().then_inc(sem("rows_done"), 1)
                    yield 3.1
                    gsm = g_row[:, TP:T].rearrange("h (b t) -> h b t", t=TB)
                    v.do(nc.vector.tensor_tensor(tails[:, 0:TS].rearrange("h (b t) -> h b t", t=TB),
                                                 m0_row[:, :].unsqueeze(2).broadcast_to([HA, NB, TB]), gsm, ALU.subtract))
                    v.do(nc.vector.tensor_tensor(tails[:, TS:2 * TS].rearrange("h (b t) -> h b t", t=TB),
                                                 rA[:, TP:T].rearrange("h (b t) -> h b t", t=TB),
                                                 gsm[:, :, TB - 1:TB].broadcast_to([HA, NB, TB]), ALU.subtract))
                    v.then(nc.vector.tensor_tensor(tails[:, 2 * TS:], m0_row[:, :], g_row[:, TP + TB - 1:T:TB], ALU.subtract))
                    nc.vector.nop().then_inc(sem("rows_done"), 1)
                    yield 5.2
                    dve.wait_ge(sem("bytok_done"), 1)
                    dve.wait_ge(sem("g_ev"), HA)
                    v.then(nc.vector.tensor_tensor(ws[:, :].rearrange("p (i h) -> p i h", h=HA),
                                                   by_tok[:, 0:16].rearrange("p (i h) -> p i h", h=HA),
                                                   G[:, :, TP - 1].unsqueeze(1).broadcast_to([P, NT, HA]), ALU.add))
                    nc.vector.nop().then_inc(sem("ws_arg"), 1)

                    def arg(u):
                        h, i = divmod(u, NT)
                        if u == 0:
                            dve.wait_ge(sem("masks_in"), 16)
                        if u >= 2:
                            dve.wait_ge(sem("pt_done"), u - 1)
                        nc.vector.tensor_tensor(W[:, u % 2, 0:P], G[:, h, P * i:P * (i + 1)], con[:, C_CM:C_CM + P],
                                                ALU.add).then_inc(sem("w_arg"), 1)

                    def normal_a(h):
                        dve.wait_ge(sem("a_o"), h + 1)
                        o = acc[:, 7, 0:NT * (HD + 1)].rearrange("p (i c) -> p i c", c=HD + 1)
                        v.then(nc.vector.tensor_copy(den[:, 0:NT], o[:, :, HD]))
                        v.then(nc.vector.scalar_tensor_tensor(den[:, 0:NT], den[:, 0:NT], -1.0, den[:, 0:NT], ALU.mult, ALU.max))
                        v.then(nc.vector.tensor_tensor(den[:, 0:NT], den[:, 0:NT], e_m[:, h:16:HA], ALU.max))
                        v.then(nc.vector.reciprocal(den[:, 0:NT], den[:, 0:NT]))
                        v.then(nc.vector.tensor_tensor(hA[:, 0:NT, h, :], o[:, :, 0:HD],
                                                       den[:, 0:NT].unsqueeze(2).broadcast_to([P, NT, HD]), ALU.mult))
                        if h >= 2:
                            dve.wait_ge(sem(f"st_stored{h % 2}"), 32 * (h // 2))
                        c = NT * (HD + 1)
                        nc.vector.tensor_copy(st_o[:, h % 2, :], acc[0:HD, 7, c:c + HD + 1]).then_inc(sem("stp_ev"), 1)

                    yield T_ML - 0.2
                    dve.wait_ge(sem("ws_done"), 1)
                    arg(0)
                    for h in range(HA):
                        if h >= 1:
                            yield T_ML + h + 0.02
                            normal_a(h - 1)
                        for i in range(NT):
                            u = NT * h + i
                            yield T_ML + h + (0.1, 0.2, 0.4, 0.55)[i]
                            if u + 1 < HA * NT:
                                arg(u + 1)
                            if i == 0:
                                if h >= 1:
                                    dve.wait_ge(sem("a_o"), h)
                                nc.vector.tensor_tensor(kw[:, :, :], ka_tok[:, 0:NT, HD * h:HD * (h + 1)],
                                                        ws[:, h:16:HA].unsqueeze(2).broadcast_to([P, NT, HD]), ALU.mult).then_inc(sem("kw_done"), 1)
                            dve.wait_ge(sem("w_done"), u + 1)
                            dve.wait_ge(sem("a_s"), u + 1)
                            n = TP - P * i
                            nc.vector.tensor_tensor(PT[:, A_OFF[i]:A_OFF[i] + n], acc[:, 3 + u % 3, 0:n],
                                                    W[:, u % 2, 0:n], ALU.mult).then_inc(sem("pt_done"), 1)
                    yield T_MS + 0.02
                    normal_a(HA - 1)
                    dve.wait_ge(sem("qpa_zero"), 1)
                    for h in range(HA):
                        p = par(h)
                        at = QpA[p:p + HD, h // 2, 0, 0:1]
                        v.do(nc.vector.tensor_copy(
                            bass.AP(at.tensor, at.offset, [at.ap[0], [TS + TB, NB], [1, TB]]),
                            qT[p:p + HD, h // 2, TP:T].rearrange("p (b t) -> p b t", t=TB)))
                    v.sync()
                    nc.vector.nop().then_inc(sem("qp_done"), 1)
                    yield T_MS + 0.3
                    SPT, Swt = W[0:TS, 0, 0:HA * TS], W[0:TS, 1, 0:HA * TS]
                    dve.wait_ge(sem("sg_mm"), 1)
                    dve.wait_ge(sem("pt_done"), HA * NT)
                    nc.vector.tensor_tensor(Swt.rearrange("p (h t) -> p h t", t=TS),
                                            acc[0:TS, 3, 0:HA * TS].rearrange("p (h t) -> p h t", t=TS),
                                            con[0:TS, C_SM:C_SM + TS].unsqueeze(1).broadcast_to([TS, HA, TS]),
                                            ALU.add).then_inc(sem("sw_arg"), 1)
                    v.do(nc.vector.tensor_tensor(kws[:, :].rearrange("p (h d) -> p h d", d=HD),
                                                 ka_tok[0:TS, NT, :].rearrange("p (h d) -> p h d", d=HD),
                                                 by_tok[0:TS, 44:48].unsqueeze(2).broadcast_to([TS, HA, HD]), ALU.mult))
                    yield T_MS + 0.6
                    dve.wait_ge(sem("sw_done"), 1)
                    dve.wait_ge(sem("pe_order"), 2)
                    nc.vector.tensor_tensor(SPT, acc[0:TS, 4, 0:HA * TS], Swt, ALU.mult).then_inc(sem("spt_done"), 1)
                    yield T_MS + 1.2
                    dve.wait_ge(sem("so_mm"), 1)
                    v.then(nc.vector.tensor_copy(oA[:, :], acc[0:TS, 5, 0:HA * (HD + 1)]))
                    for h in range(HA):
                        c = h * (HD + 1)
                        v.do(nc.vector.scalar_tensor_tensor(oA[:, c:c + HD + 1], acc[0:TS, 6, c:c + HD + 1],
                                                            by_tok[0:TS, 40 + h:41 + h], oA[:, c:c + HD + 1], ALU.mult, ALU.add))
                    v.sync()
                    o = oA[:, :].rearrange("p (h c) -> p h c", c=HD + 1)
                    v.then(nc.vector.scalar_tensor_tensor(den[0:TS, 0:HA], o[:, :, HD], -1.0, o[:, :, HD], ALU.mult, ALU.max))
                    v.then(nc.vector.tensor_tensor(den[0:TS, 0:HA], den[0:TS, 0:HA], e_m[0:TS, 16:20], ALU.max))
                    v.then(nc.vector.reciprocal(den[0:TS, 0:HA], den[0:TS, 0:HA]))
                    dve.wait_ge(sem("ha_zero"), 1)
                    v.then(nc.vector.tensor_tensor(hA[0:TS, NT], o[:, :, 0:HD], den[0:TS, 0:HA].unsqueeze(2).broadcast_to([TS, HA, HD]), ALU.mult))
                    nc.vector.nop().then_inc(sem("oa_read"), 1)
                    yield T_MS + 1.6
                    dve.wait_ge(sem("dc_mm"), 1)
                    v.then(nc.vector.tensor_scalar(dcy[:, :, :], acc[:, 3, 0:2 * NB].rearrange("p (a b) -> p a b", b=NB), -1.0, None, ALU.mult))
                    for h in range(HA):
                        p = par(h)
                        yield T_MS + 1.65 + 0.5 * h
                        if h >= 1:
                            dve.wait_ge(sem("sst_mm"), h)
                        v.then(nc.vector.tensor_tensor(Vb[:, :, :], va_tok[0:TS, NT, h, :].unsqueeze(1).broadcast_to([TS, NB, HD + 1]),
                                                       con[0:TS, C_BM:C_BM + NB].unsqueeze(2).broadcast_to([TS, NB, HD + 1]), ALU.mult))
                        nc.vector.nop().then_inc(sem("vb_done"), 1)
                        cn = C0n[p:p + HD, :, h // 2, :]
                        v.then(nc.vector.tensor_tensor(cn, cn, dcy[p:p + HD, h // 2, :].unsqueeze(2).broadcast_to([HD, NB, HD + 1]), ALU.mult))
                        yield T_MS + 2.12 + 0.5 * h
                        dve.wait_ge(sem("sst_mm"), h + 1)
                        for half in range(2):
                            v.do(nc.vector.tensor_tensor(
                                cn[:, 4 * half:4 * half + 4], cn[:, 4 * half:4 * half + 4],
                                acc[p:p + HD, 4 + half, 0:4 * (HD + 1)].rearrange("p (b c) -> p b c", c=HD + 1), ALU.add))
                        v.sync()
                        nc.vector.nop().then_inc(sem("cn_done"), 1)
                    yield T_MS + 3.65
                    hh = hA[:, :, :, :].rearrange("p i h d -> p (i h) d")
                    v.then(nc.vector.tensor_tensor(hsq[:, :, :], hh, hh, ALU.mult))
                    yield T_MS + 4.05
                    v.then(nc.vector.tensor_reduce(rs[:, :], hsq[:, :, :], AXX, ALU.add))
                    nc.vector.nop().then_inc(sem("rs_arg"), 1)
                    yield T_MS + 4.52
                    dve.wait_ge(sem("rs_std"), 1)
                    v.then(nc.vector.reciprocal(rs[:, :], rs[:, :]))
                    v.then(nc.vector.tensor_tensor(hh, hh, rs[:, :].unsqueeze(2).broadcast_to([P, (NT + 1) * HA, HD]), ALU.mult))
                    nc.vector.nop().then_inc(sem("hn_done"), 1)
                    yield T_MS + 5.02
                    dve.wait_ge(sem("oa_done"), 1)
                    for pr in range(2):
                        dve.wait_ge(sem("ya_tr"), pr + 1)
                        for b, c0, c1 in ((3 + 2 * pr, 0, TP), (4 + 2 * pr, TP, T)):
                            nc.vector.scalar_tensor_tensor(qT[:, pr, c0:c1], acc[:, b, 0:c1 - c0], vecs[:, 24 + pr:25 + pr],
                                                           oaT[:, pr, c0:c1], ALU.mult, ALU.mult).then_inc(sem("ya_done"), 1)

                def biased(u):
                    for n in unit_segs[u]:
                        _, i, h, k0, off = segs[n]
                        w = P * (i + 1 - k0)
                        if n == 0:
                            dve.wait_ge(sem("ttb_in"), 16)
                            dve.wait_ge(sem("a_out"), 160)
                            for b in range(2):
                                dve.wait_ge(sem(f"st_stored{b}"), 16 * HA)
                        if u == ND:
                            dve.wait_ge(sem("ttc_in"), 16)
                        dve.wait_ge(sem("s_mm"), n + 1)
                        if n == unit_segs[u][0]:
                            if u >= ND:
                                dve.wait_ge(sem("pt_tr"), unit_segs[max(u - 5, ND - 1)][-1] + 1)
                            elif u >= 2:
                                dve.wait_ge(sem("pt_tr"), unit_segs[u - 2][-1] + 1)
                        c0 = P * (NT - 1 - i + k0)
                        nc.vector.tensor_tensor(scores_in(u)[:, off:off + w], acc[:, 3 + n % 3, 0:w],
                                                bias_of(h, c0, w), ALU.add).then_inc(sem("s_used"), 1)
                    dve.wait_ge(sem("s_used"), unit_segs[u][-1] + 1)
                    if u >= 4:
                        dve.wait_ge(sem("e_done"), u - 3)
                    nc.vector.tensor_reduce(mx[:, u % 4:u % 4 + 1], scores_in(u), AXX, ALU.max,
                                            negate=True).then_inc(sem("m_done"), 1)

                def normal(u):
                    dve.wait_ge(sem("e_done"), u + 1)
                    v.then(nc.vector.reciprocal(dn[:, u % 4:u % 4 + 1], dn[:, u % 4:u % 4 + 1]))
                    nc.vector.tensor_scalar(scores_in(u), scores_in(u), dn[:, u % 4:u % 4 + 1], None,
                                            ALU.mult).then_inc(sem("p_done"), 1)

                def collect(n):
                    _, i, h, k0, off = segs[n]
                    p = par(h)
                    dve.wait_ge(sem("o_mm"), n + 1)
                    nc.vector.tensor_copy(qT[p:p + HD, 2 + h // 2, P * i:P * (i + 1)], acc[p:p + HD, 7, 0:P]).then_inc(sem("o_ev"), 1)

                def attention():
                    for u in range(ND + 1):
                        if u < ND:
                            yield unit_time(u, 4 / 16)
                            biased(u)
                        if u >= 1:
                            yield T_DIL + u + 8 / 16
                            collect(unit_segs[u - 1][0])
                            yield T_DIL + u + 12 / 16
                            collect(unit_segs[u - 1][1])
                        if u < ND:
                            yield unit_time(u, 14 / 16)
                            normal(u)
                        if u >= 1:
                            yield T_DIL + u + 1
                            collect(unit_segs[u - 1][2])
                    for c in range(NU - ND + 3):
                        u = ND + c
                        if c < NU - ND:
                            yield unit_time(u, 0.3)
                            biased(u)
                        if 3 <= c:
                            yield unit_time(u, 0.5)
                            collect(unit_segs[u - 3][0])
                        if 1 <= c < NU - ND + 1:
                            yield unit_time(u, 0.6)
                            normal(u - 1)

                def sample():
                    yield T_SA + 0.1
                    dve.wait_ge(sem("tok_done"), 2 * len(turns))
                    nc.vector.tensor_copy(kTn[:, :, :], kT[:, 2:8, TP:T]).then_inc(sem("new4"), 1)
                    nc.vector.tensor_copy(vn[:, :], v_tok[0:TS, NT, :]).then_inc(sem("new4"), 1)
                    dve.wait_ge(sem("zero4"), 1)
                    dve.wait_ge(sem("rb4_in"), 64)
                    for h in range(2):
                        p = HD * h
                        v.do(nc.vector.tensor_copy(Qs[p:p + HD, :, TS * h:TS * (h + 1)], qT[p:p + HD, 2:8, TP:T]))
                    for t in range(TB):
                        r = slice(32 * t, 32 * (t + 1))
                        v.do(nc.vector.tensor_copy(RBs[r, :, :].rearrange("p h (b t) -> p h b t", t=TB)[:, :, :, t],
                                                   rb4[r, :].unsqueeze(2).broadcast_to([32, HEADS, NB])))
                    v.sync()
                    nc.vector.nop().then_inc(sem("q4"), 1)
                    yield T_SA + 1.1
                    dve.wait_ge(sem("new_mm"), 6)
                    dve.wait_ge(sem("mask_in"), 16)
                    new = S4[:, :, 256:288]
                    v.then(nc.vector.tensor_tensor(new, acc[:, 2, 0:96].rearrange("p (g n) -> p g n", n=TS), new, ALU.add))
                    nc.vector.nop().then_inc(sem("new_read"), 1)

                def queries():
                    for q in range(6):
                        yield T_SA + 0.25 + q / 2
                        if q == 0:
                            dve.wait_ge(sem("qpad_zero"), 1)
                        if q >= 2:
                            dve.wait_ge(sem("qk4"), NB * (q - 1))
                        for h in range(2):
                            p = HD * h
                            at = Qpad[p:p + HD, q % 2, 0, TS * h:TS * h + 1]
                            v.do(nc.vector.tensor_copy(
                                bass.AP(at.tensor, at.offset, [at.ap[0], [2 * TS + TB, NB], [1, TB]]),
                                qT[p:p + HD, 2 + q, TP:T].rearrange("p (b t) -> p b t", t=TB)))
                        v.sync()
                        nc.vector.nop().then_inc(sem("qpad_done"), 1)

                def sample_softmax():
                    for half in range(2):
                        yield T_SA + (2.6, 4.02)[half]
                        lo = HD * half
                        dve.wait_ge(sem("qk4"), 3 * NB * (half + 1))
                        r = slice(lo, lo + HD)
                        if half == 0:
                            v.do(nc.vector.tensor_tensor(S4[r, 0, 0:P], acc[r, 3, 0:P], S4[r, 0, 0:P], ALU.add))
                            v.then(nc.vector.tensor_tensor(S4[r, 1:3, 0:256], acc[r, 4:6, 0:256], S4[r, 1:3, 0:256], ALU.add))
                        else:
                            v.then(nc.vector.tensor_tensor(S4[r, :, 0:256], acc[r, 3:6, 0:256], S4[r, :, 0:256], ALU.add))
                        v.then(nc.vector.tensor_reduce(mx4[r, 0:3], S4[r, :, :], AXX, ALU.max))
                        if half == 0:
                            v.then(nc.vector.tensor_reduce(mx4[r, 3:4], mx4[r, 0:3], AXX, ALU.max))
                            v.then(nc.vector.tensor_copy(mx4[r, 0:3], mx4[r, 3:4].broadcast_to([HD, 3])))
                        v.then(nc.vector.tensor_scalar(mx4[r, 0:3], mx4[r, 0:3], -1.0, None, ALU.mult))
                        nc.vector.nop().then_inc(sem("mx4"), 1)
                        yield T_SA + (3.3, 4.4)[half]
                        dve.wait_ge(sem("e4"), 3 * (half + 1))
                        if half == 0:
                            v.then(nc.vector.tensor_reduce(dn4[r, 3:4], dn4[r, 0:3], AXX, ALU.add))
                            v.then(nc.vector.tensor_copy(dn4[r, 0:3], dn4[r, 3:4].broadcast_to([HD, 3])))
                        v.then(nc.vector.reciprocal(dn4[r, 0:3], dn4[r, 0:3]))
                        nc.vector.tensor_tensor(S4[r, :, :], S4[r, :, :], dn4[r, 0:3].unsqueeze(2).broadcast_to([HD, 3, 288]),
                                                ALU.mult).then_inc(sem("p4"), 1)

                def sample_collect():
                    for half in range(2):
                        yield T_SA + (4.8, 5.55)[half]
                        dve.wait_ge(sem("o4"), 3 * (half + 1))
                        nc.vector.tensor_copy(Osb[:, half, :, :], acc[0:HD, O4_BANK[half], 0:3 * P].rearrange("p (g n) -> p g n", n=P)
                                              ).then_inc(sem("osb_ev"), 1)
                        yield T_SA + (5.2, 5.65)[half]
                        dve.wait_ge(sem("ot_tr"), half + 1)
                        for h in range(2):
                            p = HD * h
                            nc.vector.tensor_copy(qT[p:p + HD, 2 + 3 * half:5 + 3 * half, TP:T],
                                                  acc[p:p + HD, 3 + half, 0:3 * HD].rearrange("p (q n) -> p q n", n=HD)[:, :, TS * h:TS * (h + 1)]
                                                  ).then_inc(sem("y4"), 1)

                dve.wait_ge(sem("vecs_done"), 1)
                def x_hi(m):
                    i = x_order[m]
                    n = P if i < NT else TS
                    dve.wait_ge(sem("x_ev"), m + 1)
                    nc.vector.tensor_tensor(h_hi[:, :, P * i:P * i + n], xT[:, :, P * i:P * i + n],
                                            vecs[:, 0:KD].unsqueeze(2).broadcast_to([P, KD, n]), ALU.mult).then_inc(sem("h_hi_done"), 1)

                def x_lo(m):
                    i = x_order[m]
                    n = P if i < NT else TS
                    dve.wait_ge(sem("h_hi_done"), m + 1)
                    dve.wait_ge(sem("xg_made"), m + 1)
                    nc.vector.tensor_tensor(h_lo[:, :, P * i:P * i + n], xg[:, m % 2, :, 0:n], h_hi[:, :, P * i:P * i + n].bitcast(F32),
                                            ALU.subtract).then_inc(sem("h_lo_done"), 1)

                x_hi(0)
                x_hi(1)
                x_lo(0)
                x_lo(1)
                split_lo(dve, 0)
                x_hi(2)
                x_hi(3)
                x_lo(2)
                x_hi(4)
                x_lo(3)
                x_lo(4)

                side = Side(rstd_rows(), mlstm(), attention(), sample(), queries(), sample_softmax(), sample_collect(), merge(), feed())
                for w in range(n_all):
                    side.until(w + 0.25)
                    if w + 1 < n_all:
                        split_lo(dve, w + 1)
                    side.until(w + 0.5)
                    evac(w, 0)
                    side.until(w + 1)
                    evac(w, 1)
                dve.wait_ge(mm_done, mm_at[n_all])
                nc.vector.memset(rt[:, :], 1.0).then_inc(sem("rt_set"), 1)
                dve.wait_ge(sem("rt_std"), 2)
                nc.vector.reciprocal(rt[:, :], rt[:, :]).then_inc(sem("rt_done"), 1)
                dve.wait_ge(sem("rt_done"), 1)
                for i in range(NT + 1):
                    n = P if i < NT else TS
                    dve.wait_ge(sem("y_tr"), i + 1)
                    nc.vector.tensor_scalar(o_st[0:n, i, 512:D], acc[0:n, 2 * (i % 3) + 1, :], rt[0:n, i:i + 1], None,
                                            ALU.mult).then_inc(sem("y_right"), 1)

    return nc


OUT_SHAPES = [
    (1, TP, D), (NB, TB, D), (1, 1, HA, HD, HD), (1, 1, HA, HD), (1, 1, HA),
    (1, NB, HA, HD, HD), (1, NB, HA, HD), (1, NB, HA),
    (1, 1, 128, 2, 2, HD), (1, 1, 512, 2, 2, HD), (1, 1, 512, 2, 2, HD),
    (1, NB, 128, 2, 2, HD), (1, NB, 256, 2, 2, HD), (1, NB, 256, 2, 2, HD),
    (1, 1, TP, 6, HD), (1, 1, TP, 6, HD), (1, NB, TB, 6, HD), (1, NB, TB, 6, HD)]


def kernel(**inputs):
    import concourse.bacc as bacc
    from concourse.bass_utils import run_bass_kernel_spmd

    nc = bacc.Bacc("TRN2", target_bir_lowering=False, num_devices=1)
    arrays = {name: np.ascontiguousarray(a) for name, a in inputs.items()}
    arrays.update(con=wide_constants(), rowc=row_constants(), scan=scan_constants(), oh=bias_selectors(),
                  sel4=sample_selectors(), mask4=sample_masks())
    aps = {name: nc.dram_tensor("in_" + name, a.shape, mybir.dt.from_np(a.dtype), kind="ExternalInput").ap()
           for name, a in arrays.items()}
    outs = [nc.dram_tensor(f"out_{i}", shape, F32, kind="ExternalOutput").ap()
            for i, shape in enumerate(OUT_SHAPES)]
    aps["tab"] = nc.dram_tensor("tab", (1, HEADS * REV), F32, kind="Internal").ap()
    aps["rev"] = nc.dram_tensor("rev", (P, HEADS * REV), F32, kind="Internal").ap()
    build(nc, aps, outs, aps)
    got = run_bass_kernel_spmd(nc, [{"in_" + n: a for n, a in arrays.items()}], core_ids=[0]).results[0]
    return tuple(got[f"out_{i}"] for i in range(len(OUT_SHAPES)))
```
